# Optimizing a Trainium2 kernel written in Bass

```python
import jax, jax.numpy as jnp
from jax import lax
import numpy as np

D_MODEL = 1024
BATCH = 1
SEQ = 256
DEPTH = 2

GRID_W = 64
CTX_LEN = 256

FOURIER_GROUPS = 4
FOURIER_GROUP_DIM = 128
FOURIER_DIM = FOURIER_GROUPS * FOURIER_GROUP_DIM

MLA_HEADS = 8
MLA_NOPE = 64
MLA_ROPE = 32
MLA_QK = MLA_NOPE + MLA_ROPE
MLA_V = 64
MLA_Q_LORA = 384
MLA_KV_LORA = 256
MLA_SCALE = MLA_QK ** -0.5
ROPE_PAIRS = MLA_ROPE // 4
ROPE_BASE = 10000.0
Q_BLOCK = 128

RWKV_HEADS = 8
RWKV_HEAD = 64
RWKV_DIM = RWKV_HEADS * RWKV_HEAD
DECAY_LORA = 64
AAA_LORA = 64
GATE_LORA = 128
RWKV_IN = 3 * RWKV_DIM + DECAY_LORA + AAA_LORA + GATE_LORA
GN_EPS = 64e-5

N_BRANCHES = 3
IN_SIZES = (FOURIER_DIM, MLA_Q_LORA, MLA_KV_LORA, MLA_ROPE, RWKV_IN, D_MODEL, D_MODEL, D_MODEL)
IN_DIM = FOURIER_DIM + MLA_Q_LORA + MLA_KV_LORA + MLA_ROPE + RWKV_IN + N_BRANCHES * D_MODEL

N_EXPERTS = 16
N_GROUPS = 4
EXPERTS_PER_GROUP = N_EXPERTS // N_GROUPS
GROUP_SCORE_TOPK = 2
TOP_K = 2
EXPERT_FF = 512
SHARED_FF = 512

NORM_EPS = 1e-6

kernel_name = "hybrid_fourier_mla_rwkv7_moe_dit"

F32 = jnp.float32

def rmsnorm(x, g):
    xf = x.astype(F32)
    return (xf * lax.rsqrt(jnp.mean(xf * xf, axis=-1, keepdims=True) + NORM_EPS)).astype(x.dtype) * g

def split_cols(p, sizes):
    return jnp.split(p, np.cumsum(sizes)[:-1].tolist(), axis=-1)

def axial_rope_tables(row, col):
    inv = ROPE_BASE ** (-jnp.arange(ROPE_PAIRS, dtype=F32) / ROPE_PAIRS)
    ang = jnp.stack([row, col], axis=-1).astype(F32)[..., None] * inv
    return jnp.cos(ang), jnp.sin(ang)

def rope_2d(x, cos, sin):
    xr = x.reshape(x.shape[:-1] + (2, 2, ROPE_PAIRS))
    x1, x2 = xr[..., 0, :], xr[..., 1, :]
    c, s = cos[None, :, None], sin[None, :, None]
    out = jnp.stack([x1 * c - x2 * s, x2 * c + x1 * s], axis=-2)
    return out.reshape(x.shape).astype(x.dtype)

def fourier_mix(p):
    B, T, _ = p.shape
    z = p.astype(F32).reshape(B, T, FOURIER_GROUPS, FOURIER_GROUP_DIM)
    f = jnp.fft.fft2(z, axes=(1, 3), norm="ortho").real
    return f.reshape(B, T, FOURIER_DIM).astype(p.dtype)

def mla_project(c_q, c_kv, k_r, q_norm_g, kv_norm_g, w_uq, w_ukv, cos=None, sin=None):
    B, T, _ = c_q.shape
    q = (rmsnorm(c_q, q_norm_g) @ w_uq).reshape(B, T, MLA_HEADS, MLA_QK)
    kv = (rmsnorm(c_kv, kv_norm_g) @ w_ukv).reshape(B, T, MLA_HEADS, MLA_NOPE + MLA_V)
    q_nope, q_rope = q[..., :MLA_NOPE], q[..., MLA_NOPE:]
    k_nope, v = kv[..., :MLA_NOPE], kv[..., MLA_NOPE:]
    k_rope = k_r[:, :, None, :]
    if cos is not None:
        q_rope = rope_2d(q_rope, cos, sin)
        k_rope = rope_2d(k_rope, cos, sin)
    q = jnp.concatenate([q_nope, q_rope], axis=-1)
    k = jnp.concatenate([k_nope, jnp.broadcast_to(k_rope, (B, T, MLA_HEADS, MLA_ROPE))], axis=-1)
    return q, k, v

def attend(q, k, v):
    s = jnp.einsum('bqhd,bkhd->bhqk', q, k).astype(F32) * MLA_SCALE
    p = jax.nn.softmax(s, axis=-1).astype(v.dtype)
    return jnp.einsum('bhqk,bkhd->bqhd', p, v)

def latent_attention(q, k_lat, v_lat, k_ctx, v_ctx):
    B, T, H, _ = q.shape
    k = jnp.concatenate([k_lat, k_ctx], axis=1)
    v = jnp.concatenate([v_lat, v_ctx], axis=1)
    qb = q.reshape(B, T // Q_BLOCK, Q_BLOCK, H, MLA_QK).transpose(1, 0, 2, 3, 4)
    o = lax.map(lambda qi: attend(qi, k, v), qb)
    return o.transpose(1, 0, 2, 3, 4).reshape(B, T, H * MLA_V)

def centred_shift(p):
    pad = jnp.pad(p, ((0, 0), (1, 1), (0, 0)))
    return 0.5 * (pad[:, :-2] + pad[:, 2:])

def wkv_scan(r, w, k, v, a, b, S0, reverse):
    xs = tuple(jnp.moveaxis(t, 1, 0) for t in (r, w, k, v, a, b))

    def step(S, inp):
        rt, wt, kt, vt, at, bt = inp
        sa = jnp.einsum('bhvk,bhk->bhv', S, at)
        S = S * wt[:, :, None, :] + sa[..., None] * bt[:, :, None, :] + vt[..., None] * kt[:, :, None, :]
        return S, jnp.einsum('bhvk,bhk->bhv', S, rt)

    S_fin, ys = lax.scan(step, S0, xs, reverse=reverse)
    return S_fin, jnp.moveaxis(ys, 0, 1)

def rwkv_mix(p, S0, mu, w0, w_up, a0, a_up, g_up, k_k, k_a, r_k, gn_g, gn_b):
    B, T, _ = p.shape
    H, N = RWKV_HEADS, RWKV_HEAD
    xs = (p + (centred_shift(p) - p) * mu).astype(F32)
    r, k, v, xw, xa, xg = split_cols(xs, (RWKV_DIM, RWKV_DIM, RWKV_DIM, DECAY_LORA, AAA_LORA, GATE_LORA))
    g = jax.nn.sigmoid(xg) @ g_up
    rh, vh = r.reshape(B, T, H, N), v.reshape(B, T, H, N)
    kk = (k * k_k).reshape(B, T, H, N)
    kk = kk * lax.rsqrt(jnp.sum(kk * kk, axis=-1, keepdims=True) + 1e-12)
    ys, bonuses, finals = [], [], []
    for d in range(2):
        w = -jax.nn.softplus(-(w0[d] + jnp.tanh(xw) @ w_up[d])) - 0.5
        decay = jnp.exp(-jnp.exp(w)).reshape(B, T, H, N)
        a = jax.nn.sigmoid(a0[d] + xa @ a_up[d]).reshape(B, T, H, N)
        kd = k.reshape(B, T, H, N) * (1.0 + (a - 1.0) * k_a.reshape(H, N))
        s_fin, yd = wkv_scan(rh, decay, kd, vh, -kk, kk * a, S0[d], reverse=(d == 1))
        ys.append(yd)
        bonuses.append(jnp.sum(rh * kd * r_k, axis=-1, keepdims=True) * vh)
        finals.append(s_fin)
    y = ys[0] + ys[1]
    mean = jnp.mean(y, axis=-1, keepdims=True)
    var = jnp.mean(jnp.square(y - mean), axis=-1, keepdims=True)
    y = ((y - mean) * lax.rsqrt(var + GN_EPS)).reshape(B, T, RWKV_DIM) * gn_g + gn_b
    y = (y + (bonuses[0] + bonuses[1]).reshape(B, T, RWKV_DIM)) * g
    return y.astype(p.dtype), jnp.stack(finals)

def merge_branches(fa, attn, rw, ga, gb, gc, w_a, w_b, w_c, w_out):
    merged = (jax.nn.sigmoid(ga) * (fa @ w_a) + jax.nn.sigmoid(gb) * (attn @ w_b)
              + jax.nn.sigmoid(gc) * (rw @ w_c))
    return merged @ w_out

def moe(h, router_w, router_b, w_gate, w_up, w_down, sw_gate, sw_up, sw_down):
    T = h.shape[0]
    scores = jax.nn.sigmoid((h @ router_w).astype(F32))
    sel = (scores + router_b.astype(F32)).reshape(T, N_GROUPS, EXPERTS_PER_GROUP)
    group_score = lax.top_k(sel, GROUP_SCORE_TOPK)[0].sum(-1)
    best = jnp.argmax(group_score, axis=-1)
    in_group = jax.nn.one_hot(best, N_GROUPS, dtype=F32)[..., None] > 0
    masked = jnp.where(in_group, sel, -jnp.inf).reshape(T, N_EXPERTS)
    _, idx = lax.top_k(masked, TOP_K)
    wts = jnp.take_along_axis(scores, idx, axis=-1)
    wts = wts / jnp.sum(wts, axis=-1, keepdims=True)
    combine = jnp.einsum('tk,tke->te', wts, jax.nn.one_hot(idx, N_EXPERTS, dtype=F32)).astype(h.dtype)
    y = (jax.nn.silu(h @ sw_gate) * (h @ sw_up)) @ sw_down
    for gi in range(N_GROUPS):
        e = slice(gi * EXPERTS_PER_GROUP, (gi + 1) * EXPERTS_PER_GROUP)
        hg = jnp.einsum('td,edf->tef', h, w_gate[e])
        hu = jnp.einsum('td,edf->tef', h, w_up[e])
        y = y + jnp.einsum('tef,efd->td', jax.nn.silu(hg) * hu * combine[:, e, None], w_down[e])
    return y

def setup_inputs(seed: int = 0) -> dict:
    key = jax.random.key(seed)
    ks = iter(jax.random.split(key, 40))

    def nrm(shape, scale):
        return jax.random.normal(next(ks), shape, F32) * scale

    def gain(shape):
        return 1.0 + nrm(shape, 0.01)

    D, L = D_MODEL, DEPTH
    return {
        "x": nrm((BATCH, SEQ, D), 1.0),
        "c": nrm((BATCH, D), 1.0),
        "ctx": nrm((BATCH, CTX_LEN, D), 1.0),
        "c_ctx": nrm((D,), 1.0),
        "w_ada": nrm((L, D, 6 * D), 0.5 * D ** -0.5),
        "b_ada": nrm((L, 6 * D), 0.01),
        "norm1_g": gain((L, D)),
        "norm2_g": gain((L, D)),
        "w_in": nrm((L, D, IN_DIM), D ** -0.5),
        "q_norm_g": gain((L, MLA_Q_LORA)),
        "kv_norm_g": gain((L, MLA_KV_LORA)),
        "w_uq": nrm((L, MLA_Q_LORA, MLA_HEADS * MLA_QK), MLA_Q_LORA ** -0.5),
        "w_ukv": nrm((L, MLA_KV_LORA, MLA_HEADS * (MLA_NOPE + MLA_V)), MLA_KV_LORA ** -0.5),
        "rwkv_mu": jax.random.uniform(next(ks), (L, RWKV_IN), F32),
        "rwkv_w0": nrm((L, 2, RWKV_DIM), 1.0),
        "rwkv_w_up": nrm((L, 2, DECAY_LORA, RWKV_DIM), 0.1 * DECAY_LORA ** -0.5),
        "rwkv_a0": nrm((L, 2, RWKV_DIM), 0.5),
        "rwkv_a_up": nrm((L, 2, AAA_LORA, RWKV_DIM), AAA_LORA ** -0.5),
        "rwkv_g_up": nrm((L, GATE_LORA, RWKV_DIM), GATE_LORA ** -0.5),
        "rwkv_k_k": 0.85 + nrm((L, RWKV_DIM), 0.05),
        "rwkv_k_a": 1.0 + nrm((L, RWKV_DIM), 0.05),
        "rwkv_r_k": nrm((L, RWKV_HEADS, RWKV_HEAD), 0.1),
        "rwkv_gn_g": gain((L, RWKV_DIM)),
        "rwkv_gn_b": nrm((L, RWKV_DIM), 0.01),
        "w_proj_a": nrm((L, FOURIER_DIM, D), FOURIER_DIM ** -0.5),
        "w_proj_b": nrm((L, MLA_HEADS * MLA_V, D), (MLA_HEADS * MLA_V) ** -0.5),
        "w_proj_c": nrm((L, RWKV_DIM, D), RWKV_DIM ** -0.5),
        "w_out": nrm((L, D, D), D ** -0.5),
        "router_w": nrm((D, N_EXPERTS), D ** -0.5),
        "router_b": nrm((N_EXPERTS,), 0.01),
        "exp_w_gate": nrm((L, N_EXPERTS, D, EXPERT_FF), D ** -0.5),
        "exp_w_up": nrm((L, N_EXPERTS, D, EXPERT_FF), D ** -0.5),
        "exp_w_down": nrm((L, N_EXPERTS, EXPERT_FF, D), EXPERT_FF ** -0.5),
        "sh_w_gate": nrm((L, D, SHARED_FF), D ** -0.5),
        "sh_w_up": nrm((L, D, SHARED_FF), D ** -0.5),
        "sh_w_down": nrm((L, SHARED_FF, D), SHARED_FF ** -0.5),
        "final_norm_g": gain((D,)),
    }

def reference(x, c, ctx, c_ctx, w_ada, b_ada, norm1_g, norm2_g, w_in, q_norm_g, kv_norm_g, w_uq, w_ukv,
              rwkv_mu, rwkv_w0, rwkv_w_up, rwkv_a0, rwkv_a_up, rwkv_g_up, rwkv_k_k, rwkv_k_a, rwkv_r_k,
              rwkv_gn_g, rwkv_gn_b, w_proj_a, w_proj_b, w_proj_c, w_out, router_w, router_b,
              exp_w_gate, exp_w_up, exp_w_down, sh_w_gate, sh_w_up, sh_w_down, final_norm_g):
    B, T, D = x.shape
    rows = T // GRID_W
    row = jnp.repeat(jnp.arange(rows), GRID_W)
    col = jnp.tile(jnp.arange(GRID_W), rows)
    cos, sin = axial_rope_tables(row, col)
    zero_state = jnp.zeros((2, B, RWKV_HEADS, RWKV_HEAD, RWKV_HEAD), F32)

    for l in range(DEPTH):
        last = l == DEPTH - 1
        mod_lat = (jax.nn.silu(c) @ w_ada[l] + b_ada[l])[:, None, :]
        mod_ctx = (jax.nn.silu(c_ctx) @ w_ada[l] + b_ada[l])[None, None, :]
        sh1, sc1, g1, sh2, sc2, g2 = jnp.split(mod_lat, 6, axis=-1)
        csh1, csc1, cg1, csh2, csc2, cg2 = jnp.split(mod_ctx, 6, axis=-1)

        h_lat = rmsnorm(x, norm1_g[l]) * (1.0 + sc1) + sh1
        h_ctx = rmsnorm(ctx, norm1_g[l]) * (1.0 + csc1) + csh1
        pf_l, pq_l, pkv_l, pkr_l, pr_l, ga_l, gb_l, gc_l = split_cols(h_lat @ w_in[l], IN_SIZES)
        pf_c, pq_c, pkv_c, pkr_c, pr_c, ga_c, gb_c, gc_c = split_cols(h_ctx @ w_in[l], IN_SIZES)

        q_l, k_l, v_l = mla_project(pq_l, pkv_l, pkr_l, q_norm_g[l], kv_norm_g[l], w_uq[l], w_ukv[l], cos, sin)
        q_c, k_c, v_c = mla_project(pq_c, pkv_c, pkr_c, q_norm_g[l], kv_norm_g[l], w_uq[l], w_ukv[l])
        attn_lat = latent_attention(q_l, k_l, v_l, k_c, v_c)

        rw = (rwkv_mu[l], rwkv_w0[l], rwkv_w_up[l], rwkv_a0[l], rwkv_a_up[l], rwkv_g_up[l],
              rwkv_k_k[l], rwkv_k_a[l], rwkv_r_k[l], rwkv_gn_g[l], rwkv_gn_b[l])
        y_ctx, s_ctx = rwkv_mix(pr_c, zero_state, *rw)
        y_lat, _ = rwkv_mix(pr_l, s_ctx, *rw)

        out_lat = merge_branches(fourier_mix(pf_l), attn_lat, y_lat, ga_l, gb_l, gc_l,
                                 w_proj_a[l], w_proj_b[l], w_proj_c[l], w_out[l])
        x = x + g1 * out_lat

        moe_w = (router_w, router_b, exp_w_gate[l], exp_w_up[l], exp_w_down[l],
                 sh_w_gate[l], sh_w_up[l], sh_w_down[l])
        m_lat = rmsnorm(x, norm2_g[l]) * (1.0 + sc2) + sh2
        x = x + g2 * moe(m_lat.reshape(B * T, D), *moe_w).reshape(B, T, D)

        if not last:
            attn_ctx = attend(q_c, k_c, v_c).reshape(B, CTX_LEN, MLA_HEADS * MLA_V)
            out_ctx = merge_branches(fourier_mix(pf_c), attn_ctx, y_ctx, ga_c, gb_c, gc_c,
                                     w_proj_a[l], w_proj_b[l], w_proj_c[l], w_out[l])
            ctx = ctx + cg1 * out_ctx
            m_ctx = rmsnorm(ctx, norm2_g[l]) * (1.0 + csc2) + csh2
            ctx = ctx + cg2 * moe(m_ctx.reshape(B * CTX_LEN, D), *moe_w).reshape(B, CTX_LEN, D)

    return rmsnorm(x, final_norm_g)


_drawn_inputs = setup_inputs


def setup_inputs(seed=0):
    import zlib

    import numpy as np

    out = dict(_drawn_inputs(seed))
    spreads = {}
    factors = {'norm1_g': 4.141,
     'q_norm_g': 8.0,
     'kv_norm_g': 8.0,
     'rwkv_w_up': 8.0,
     'rwkv_k_k': 4.017,
     'rwkv_gn_g': 33.91,
     'rwkv_gn_b': 25.24,
     'final_norm_g': 29.107,
     'norm2_g': 3.555}
    for name, (base, spread) in spreads.items():
        noise = np.random.default_rng([zlib.crc32(name.encode()), seed]).standard_normal(out[name].shape)
        drawn = base * np.exp(spread * noise) if base else spread * noise
        out[name] = __import__('jax').numpy.asarray(drawn.astype(out[name].dtype))
    for name, factor in factors.items():
        out[name] = (out[name] * factor).astype(out[name].dtype)
    return out
```

```python
from contextlib import ExitStack
import math

import numpy as np

import concourse.bass as bass
from concourse import mybir

F32 = mybir.dt.float32
ALU = mybir.AluOpType
ACT = mybir.ActivationFunctionType
AX_X = mybir.AxisListType.X
P = 128

D = 1024
KD = D // P
DEPTH = 2
SEQ, CTX = 256, 256
T = SEQ + CTX
GRID_W = 64
FG, FGD = 4, 128
HEADS, NOPE, ROPE, VD = 8, 64, 32, 64
QK = NOPE + ROPE
QL, KVL = 384, 256
SCALE = QK ** -0.5
RH, RN = 8, 64
RD = RH * RN
RJ = RD // P
RIN = 3 * RD + 64 + 64 + 128
RT = RIN // P
NE, NG, EPG, FF = 16, 4, 4, 512
FK = FF // P
EPS = 1e-6
GN_EPS = 64e-5
DECAY = math.exp(-0.5)
CH = 64
NCH = SEQ // CH
LEVELS = [2, 4, 8, 16, 32]

C_F, C_Q = 0, 512
C_KV = C_Q + QL
C_R = C_KV + KVL + ROPE
C_G = C_R + RIN
IN_DIM = C_G + 3 * D

VEC = {}
_n = 0
for _name, _w in (("n1", 8), ("n2", 8), ("bada", 48), ("qg", 3), ("kvg", 2), ("mu", RT), ("w0", 8), ("a0", 8),
                  ("kk", 4), ("ka", 4), ("rk", 4), ("gng", 4), ("gnb", 4)):
    VEC[_name] = _n
    _n += _w
NVEC = _n

CON = {}
_n = 0
for _name, _w in (("ident", P), ("ones", P), ("heads", P), ("rot", P), ("strict0", CH), ("strict1", CH),
                  ("incl0", CH), ("incl1", CH), ("pair0", CH), ("pair1", CH), ("eye", CH), ("lev1", CH),
                  *((f"lev{b}", CH) for b in LEVELS), ("reset", RJ * CH), ("prio", NE), ("cos", SEQ), ("sin", SEQ)):
    CON[_name] = _n
    _n += _w
NCON = _n
NDFT = 2 * FGD + 4 * SEQ
HW = 3 * QK + 2 * NOPE

NSLOT = 3
N_ADA = 12
L_F, L_Q, L_KV, L_DFT, L_UKV, L_R, L_K, L_V, L_WAG, L_LORA = range(N_ADA, N_ADA + 10)
L_MERGE = L_LORA + 1
L_OUT = L_MERGE + 12
L_EXP = L_OUT + 2
PER_LAYER = L_EXP + 3 * (NE + 1)
assert N_ADA % NSLOT == 0 and L_EXP % NSLOT == 0 and PER_LAYER % NSLOT == 0
ROUNDS = PER_LAYER // NSLOT


def build(nc, xT, cT, vec, fng, rb, rw, w_ada, w_in, headw, w_ukv, lora, w_a, w_b, w_c, w_out,
          eg, eu, ed, sg, su, sd, con, dft, out, stop=None):
    comb_d = nc.dram_tensor("comb_rows", [DEPTH, NE, T], F32).ap()
    width = [T, SEQ]
    with ExitStack() as ctx:
        def sb(name, shape):
            return ctx.enter_context(nc.sbuf_tensor(name, shape, F32))

        sems = {}

        def sem(name):
            if name not in sems:
                sems[name] = ctx.enter_context(nc.semaphore(name))
            return sems[name]

        ps = ctx.enter_context(nc.psum_tensor("ps", [P, 8, 512], F32))
        X = sb("X", [P, KD, T])
        H = sb("H", [P, KD, T])
        W = sb("W", [P, NSLOT, 4096])
        cons = sb("cons", [P, NCON])
        vecs = sb("vecs", [P, DEPTH, NVEC])
        fngs = sb("fngs", [P, KD])
        rbs = sb("rbs", [P, NE])
        rws = sb("rws", [P, KD, NE])
        epst = sb("epst", [P, 3])
        csil = sb("csil", [P, KD, 2])
        mod = sb("mod", [P, 48, 2])
        gsc = sb("gsc", [P, 2, KD, 2])
        dummy = sb("marks", [P, 4])
        small = sb("small", [P, 8])
        WORK = 29184
        work = sb("work", [P, WORK])

        def con_(name, w=CH):
            return cons[:, CON[name]:CON[name] + w]

        ident, ones, hsum = con_("ident", P), con_("ones", P), con_("heads", P)
        rot = cons[:, CON["rot"]:CON["rot"] + QK]

        def place(at, n, w=T):
            assert at + n * w <= WORK
            return work[:, at:at + n * w].rearrange("p (j n) -> p j n", n=w)

        FO, AO, Y = place(0, 4), place(2048, 4), place(4096, 4)
        GX, WA = place(6144, 1), place(6656, 1)
        TOP = 7168
        ROW = place(TOP, 3)
        RS = place(TOP, 2)
        FZ, FA = place(TOP, 4), place(TOP + 2048, 2)
        CQ, CKV = place(TOP + 3072, 3), place(TOP + 4608, 2)
        KR, VT = place(TOP + 5632, 1), place(TOP + 6144, 4)
        SQ, RQ = place(TOP + 8192, 5), place(TOP + 10752, 2)
        RP = place(TOP + 11776, 2)
        Qh, Kh, Pb, PT = (place(TOP + 12800 + 1024 * n, 2) for n in range(4))
        Vh, WH = place(TOP + 16896, 2, 256), place(TOP + 17408, 2, HW)
        R, V, KK = (place(TOP + 2048 * n, 4) for n in range(3))
        B = [place(TOP + 2048 * (3 + d), 4) for d in range(2)]
        K1 = place(TOP + 2048 * 5, 4)
        KDs = [place(TOP + 2048 * 6, 4), K1]
        LW = [place(TOP + 2048 * (7 + d), 4) for d in range(2)]
        SCR = TOP + 2048 * 9
        PP = work[:, SCR:SCR + 2 * 2 * 258].rearrange("p (b s n) -> p b s n", b=2, s=2)
        TS = place(SCR + 1032, 2)
        spare = [work[:, SCR + 256 * n:SCR + 256 * (n + 1)] for n in range(12)] + \
                [W[:, 1 + n // 16, 256 * (n % 16):256 * (n % 16) + 256] for n in range(32)]
        SB = {}
        for name in ("lw", "L", "E1", "E2", "E3", "Rq", "Kk", "Vc", "Bt", "Kt", "Vt", "MT", "X", "XT", "BT", "P",
                     "Gak", "Grb", "Grk", "RHS", "U", "S"):
            SB[name] = [spare.pop(0).rearrange("p (j n) -> p j n", n=CH) for d in range(2)]
        M, SG = place(TOP, 8), place(TOP + 4096, 2)
        TM = place(TOP + 5120, 1)
        ACC, HS, CB = place(TOP, 8), place(TOP + 4096, 4), place(TOP + 6144, 1)
        RO = TOP + 6656
        rt = [work[:, RO + 128 * n:RO + 128 * n + 128] for n in range(10)]
        CT = work[:, RO + 1280:RO + 1280 + T]

        def slot(n):
            return W[:, n % NSLOT, :]

        def loaded(eng, l, n, more=0):
            eng.wait_ge(sem(f"slot_loaded{n % NSLOT}"), 16 * (ROUNDS * l + n // NSLOT + 1 + more))

        four = [2 * FG, FG]
        nqt = [T // P, SEQ // P]
        PH = {"act": 0, "dve": 0, "pool": 0, "pe": 0}

        class Chain:

            def __init__(self, eng, name):
                self.eng, self.s, self.n, self.var = eng, sem(name), 0, 0

            def __call__(self, ins):
                self.n += 1
                ins.then_inc(self.s, 1)
                self.eng.wait_ge(self.s, self.var + self.n)

            def loop(self, i, per):
                self.start, self.per, self.var = self.n, per, i * per

            def end(self, times):
                assert self.n - self.start == self.per, (self.n - self.start, self.per)
                self.n, self.var = self.start + self.per * times, 0

        def handover(who, eng, ins=None):
            PH[who] += 1
            if ins is not None:
                ins.then_inc(sem(f"stage_{who}"), 1)
            for n in ("act", "dve", "pool"):
                eng.wait_ge(sem(f"stage_{n}"), PH[who])

        def wait(eng, name, count):
            if not (isinstance(count, int) and count == 0):
                eng.wait_ge(sem(name), count)

        def wait_apart(eng, name, count):
            eng.wait_ge(sem(name), count)
            eng.nop(nofuse=True)

        def over_pairs(mask):
            return mask.unsqueeze(1).broadcast_to([P, RJ, CH])

        block = ctx.enter_context(nc.Block())

        @block.sync
        def _(sp):
            for dst, src in ((X[:].rearrange("p k t -> p (k t)"), xT), (csil[:].rearrange("p k t -> p (k t)"), cT),
                             (cons[:], con), (vecs[:].rearrange("p l n -> p (l n)"), vec), (fngs[:], fng),
                             (rbs[:], rb), (rws[:].rearrange("p k e -> p (k e)"), rw)):
                sp.dma_start(dst, src).then_inc(sem("params"), 16)

            def rows(ap, k):
                return ap.rearrange("(k p) n -> p k n", k=k)

            def load(l, n, src, k, w, reader=None, count=0, more=0):
                if reader:
                    sp.wait_ge(sem(reader), count)
                sp.dma_start(slot(n)[:, 0:k * w].rearrange("p (k n) -> p k n", k=k), src)\
                    .then_inc(sem(f"slot_loaded{n % NSLOT}"), 16)

            for l in range(DEPTH):
                def ada(g):
                    return rows(w_ada[l, :, bass.ds(g * 512, 512)], KD), KD, 512
                for s in range(NSLOT):
                    reader = ("down_ready", 8 * (NE + 1) * l) if s == 2 else ("up_ready", 4 * (NE + 1) * l)
                    load(l, s, *ada(s), *(reader if l else ()))
                with sp.Fori(1, N_ADA // NSLOT) as i:
                    for s in range(NSLOT):
                        load(l, s, *ada(i * NSLOT + s), "ada_rows", N_ADA * l + (i - 1) * NSLOT + s + 1)
                at = N_ADA * (l + 1)
                load(l, L_F, rows(w_in[l, :, C_F:C_F + 512], KD), KD, 512, "ada_rows", at - 2)
                load(l, L_Q, rows(w_in[l, :, C_Q:C_Q + QL], KD), KD, QL, "ada_rows", at - 1)
                load(l, L_KV, rows(w_in[l, :, C_KV:C_KV + KVL + ROPE], KD), KD, KVL + ROPE, "ada_rows", at)
                load(l, L_DFT, dft.rearrange("p (k n) -> p k n", k=1), 1, NDFT, "ina_ready", 10 * l + 4)
                load(l, L_UKV, rows(w_ukv[l], 2), 2, 1024, "ina_ready", 10 * l + 7)
                load(l, L_R, rows(w_in[l, :, C_R:C_R + 512], KD), KD, 512, "ina_ready", 10 * l + 10)
                for b in range(2):
                    if l:
                        sp.wait_ge(sem(f"heads_made{b}"), l * (HEADS // 2))
                    sp.dma_start(WH[:, b, :], headw[l, b, :, :]).then_inc(sem(f"headw_loaded{b}"), 16)
                with sp.Fori(1, HEADS // 2) as i:
                    for b in range(2):
                        sp.wait_ge(sem(f"heads_made{b}"), l * (HEADS // 2) + i)
                        sp.dma_start(WH[:, b, :], headw[l, bass.ds(2 * i + b, 1), :, :].rearrange("h p n -> p (h n)"))\
                            .then_inc(sem(f"headw_loaded{b}"), 16)
                load(l, L_K, rows(w_in[l, :, C_R + 512:C_R + 1024], KD), KD, 512, "fourier_ready", sum(four[:l + 1]))
                load(l, L_V, rows(w_in[l, :, C_R + 1024:C_R + 1536], KD), KD, 512, "values_ready", 4 * (l + 1))
                load(l, L_WAG, rows(w_in[l, :, C_R + 1536:C_R + 1792], KD), KD, 256, "rin_ready", RT * l + 4)
                load(l, L_LORA, lora[l].rearrange("p (k n) -> p k n", k=1), 1, 1536, "rin_ready", RT * l + 8)

                def gate(b, g):
                    return rows(w_in[l, :, bass.ds(C_G + b * D + g * 512, 512)], KD), KD, 512

                def proj(b, g):
                    return rows((w_a, w_b, w_c)[b][l, :, bass.ds(g * 512, 512)], 4), 4, 512
                load(l, L_MERGE, *gate(0, 0), "scan_over", l + 1)
                load(l, L_MERGE + 1, *proj(0, 0))
                load(l, L_MERGE + 2, *gate(1, 0), "post_over", l + 1)
                load(l, L_MERGE + 3, *proj(1, 0), "merge_gate", 24 * l + 4)
                load(l, L_MERGE + 4, *gate(2, 0), "merge_proj", 24 * l + 4)
                load(l, L_MERGE + 5, *proj(2, 0), "merge_gate", 24 * l + 8)
                load(l, L_MERGE + 6, *gate(0, 1), "merge_proj", 24 * l + 8)
                load(l, L_MERGE + 7, *proj(0, 1), "merge_gate", 24 * l + 12)
                load(l, L_MERGE + 8, *gate(1, 1), "merge_proj", 24 * l + 12)
                load(l, L_MERGE + 9, *proj(1, 1), "merge_gate", 24 * l + 16)
                load(l, L_MERGE + 10, *gate(2, 1), "merge_proj", 24 * l + 16)
                load(l, L_MERGE + 11, *proj(2, 1), "merge_gate", 24 * l + 20)
                for g, reader in enumerate((("merge_proj", 24 * l + 20), ("merge_gate", 24 * l + 24))):
                    load(l, L_OUT + g, rows(w_out[l, :, g * 512:g * 512 + 512], KD), KD, 512, *reader)
                load(l, L_EXP, rows(sg[l], KD), KD, 512, "merge_proj", 24 * l + 24)
                load(l, L_EXP + 1, rows(su[l], KD), KD, 512, "out_ready", KD * l + 4)
                load(l, L_EXP + 2, rows(sd[l], FK), FK, 1024, "out_ready", KD * l + 8)
                sp.wait_ge(sem("comb_rows"), l + 1)
                sp.dma_start(comb_d[l, :, 0:width[l]], CT[0:NE, 0:width[l]]).then_inc(sem("comb_out"), 16)
                sp.wait_ge(sem("comb_out"), 16 * (l + 1))
                ut, dt = 4 * (NE + 1) * l, 8 * (NE + 1) * l
                with sp.Fori(0, NE) as e:
                    for n, src in ((0, eg), (1, eu)):
                        load(l, L_EXP + n, rows(src[l, bass.ds(e, 1), :, :].rearrange("e d f -> (e d) f"), KD), KD, 512,
                             "up_ready", ut + 4 * (e + 1))
                    sp.wait_ge(sem("hidden_ready"), FK * ((NE + 1) * l + e + 1))
                    sp.dma_start(CB[:, 0, 0:width[l]],
                                 comb_d[l, bass.ds(e, 1), 0:width[l]].rearrange("e t -> (e t)").partition_broadcast(P))\
                        .then_inc(sem("comb_loaded"), 16)
                    load(l, L_EXP + 2, rows(ed[l, bass.ds(e, 1), :, :].rearrange("e f d -> (e f) d"), FK), FK, 1024,
                         "down_ready", dt + 8 * (e + 1))
            sp.wait_ge(sem("result"), 1)
            sp.dma_start(out, H[:, :, 0:SEQ]).then_inc(sem("stored"), 16)
            sp.wait_ge(sem("stored"), 16)

        @block.tensor
        def _(pe):
            mm = nc.tensor.matmul
            pe.wait_ge(sem("params"), 16 * 7)
            pe.wait_ge(sem("csil"), 1)

            def product(bank, w, lhs, rhs, n, M=P):
                for k in range(n):
                    ins = mm(ps[0:M, bank, 0:w], lhs(k), rhs(k), start=(k == 0), stop=(k == n - 1))
                return ins

            def weights(n, w, j):
                return lambda k: slot(n)[:, k * w + j * P:k * w + j * P + P]

            norms = 0

            def sum_squares(w):
                nonlocal norms
                for k in range(KD):
                    pe.wait_ge(sem("squares"), KD * norms + k + 1)
                    ins = mm(ps[:, 0, 0:w], ones, H[:, k, 0:w], start=(k == 0), stop=(k == KD - 1))
                ins.then_inc(sem("sumsq"), 1)
                norms += 1
                handover("pe", pe)

            for l in range(DEPTH):
                w = width[l]

                with pe.Fori(0, N_ADA // NSLOT) as i:
                    at = N_ADA * l + i * NSLOT

                    def turn(s):
                        wait_apart(pe, "ada_copied", at + s + 1)
                        for q in range(4):
                            ins = pe.transpose(ps[:, 3 + s, 2 * q:2 * q + 2], ROW[0:2, s, q * P:q * P + P],
                                               cons[0:2, CON["ident"]:CON["ident"] + 2])
                        ins.then_inc(sem("ada_cols"), 1)

                    pe.wait_ge(sem("ada_mod"), at + 1)
                    for s in range(NSLOT):
                        loaded(pe, l, s, i)
                        product(s, 512, lambda k: csil[:, k, :], lambda k: slot(s)[:, k * 512:k * 512 + 512], KD, 2)\
                            .then_inc(sem("ada_rows"), 1)
                        if s:
                            turn(s - 1)
                    turn(NSLOT - 1)
                handover("pe", pe)
                if stop == "ada":
                    return
                sum_squares(T)
                if stop == "norm1":
                    return

                o = 10 * l
                for n, cw, tiles in ((L_F, 512, 4), (L_Q, QL, 3), (L_KV, KVL + ROPE, 3)):
                    loaded(pe, l, n)
                    ww = T if n == L_KV else w
                    for j in range(tiles):
                        b = o - 10 * l
                        if b >= 8:
                            pe.wait_ge(sem("ina_copied"), o - 7)
                        if n == L_KV and j == 2:
                            ins = product(b % 8, ww, lambda k: slot(n)[:, k * cw + KVL - NOPE:k * cw + KVL + ROPE],
                                          lambda k: H[:, k, 0:ww], KD, QK)
                        else:
                            ins = product(b % 8, ww, weights(n, cw, j), lambda k: H[:, k, 0:ww], KD)
                        ins.then_inc(sem("ina_ready"), 1)
                        o += 1
                handover("pe", pe)
                if stop == "ina":
                    return

                loaded(pe, l, L_DFT)
                units = [(g, q) for g in range(FG) for q in range(four[l] // FG)]
                base = sum(four[:l])

                def over_tokens(u):
                    pe.wait_ge(sem("fourier_mid"), base + u + 1)
                    if u >= 2:
                        pe.wait_ge(sem("fourier_out"), base + u - 1)
                    for n in range(4):
                        c, t = n // 2, n % 2
                        ins = mm(ps[:, 2 + u % 2, 0:SEQ], FA[:, u % 2, t * 256 + c * FGD:t * 256 + c * FGD + FGD],
                                 slot(L_DFT)[:, 256 + n * SEQ:256 + n * SEQ + SEQ], start=(n == 0), stop=(n == 3))
                    ins.then_inc(sem("fourier_ready"), 1)

                for u, (g, q) in enumerate(units):
                    if u >= 2:
                        pe.wait_ge(sem("fourier_mid"), base + u - 1)
                    for t in range(2):
                        ins = mm(ps[:, u % 2, t * 256:t * 256 + 256], FZ[:, g, q * SEQ + t * P:q * SEQ + t * P + P],
                                 slot(L_DFT)[:, 0:256], start=True, stop=True)
                    ins.then_inc(sem("fourier_first"), 1)
                    if u:
                        over_tokens(u - 1)
                over_tokens(len(units) - 1)
                handover("pe", pe)
                if stop == "fourier":
                    return

                pe.wait_ge(sem("lora_squares"), 5 * l + 3)
                product(0, w, lambda k: ones, lambda k: SQ[:, k, 0:w], 3).then_inc(sem("lora_sums"), 1)
                pe.wait_ge(sem("lora_squares"), 5 * l + 5)
                product(1, T, lambda k: ones, lambda k: SQ[:, 3 + k, :], 2).then_inc(sem("lora_sums"), 1)
                mm(ps[0:QK, 2, 0:SEQ], rot[0:QK, :], KR[0:QK, 0, 0:SEQ], start=True, stop=True)\
                    .then_inc(sem("key_turned"), 1)
                pe.wait_ge(sem("lora_normed"), l + 1)
                loaded(pe, l, L_UKV)
                for t in range(T // P):
                    vals = [slot(L_UKV)[:, k * 1024:k * 1024 + 1024].rearrange("p (h n) -> p h n", n=NOPE + VD)[:, :, NOPE:]
                            for k in range(2)]
                    product(4 + t, HEADS * VD, lambda k: CKV[:, k, t * P:t * P + P], lambda k: vals[k], 2)\
                        .then_inc(sem("values_ready"), 1)
                handover("pe", pe)
                if stop == "lora":
                    return

                n_q = nqt[l]
                with pe.Fori(0, HEADS // 2) as i:
                    for b in range(2):
                        h = l * HEADS + 2 * i + b
                        qbase = HEADS * sum(nqt[:l]) + (2 * i + b) * n_q
                        pe.wait_ge(sem(f"headw_loaded{b}"), 16 * (l * (HEADS // 2) + i + 1))
                        product(0, w, lambda k: WH[:, b, k * QK:k * QK + QK], lambda k: CQ[:, k, 0:w], 3, QK)
                        product(1, T, lambda k: WH[:, b, 3 * QK + k * NOPE:3 * QK + k * NOPE + NOPE],
                                lambda k: CKV[:, k, :], 2, NOPE).then_inc(sem(f"heads_made{b}"), 1)
                        pe.wait_ge(sem("heads_copied"), 2 * h + 2)
                        mm(ps[0:QK, 2, 0:SEQ], rot[0:QK, :], Qh[0:QK, b, 0:SEQ], start=True, stop=True)\
                            .then_inc(sem("query_turned"), 1)
                        pe.wait_ge(sem("query_done"), h + 1)

                        def keys(q):
                            return (0, T) if q < SEQ // P else (SEQ, T)

                        def scores(q):
                            k0, k1 = keys(q)
                            mm(ps[:, 3 + q % 2, k0:k1], Qh[0:QK, b, q * P:q * P + P], Kh[0:QK, b, k0:k1],
                               start=True, stop=True).then_inc(sem("scores_ready"), 1)

                        def values(q):
                            pe.wait_ge(sem("probs_copied"), qbase + q + 1)
                            if q == 0:
                                pe.wait_ge(sem("heads_out"), h + 1)
                            first = keys(q)[0] // P
                            for c in range(first, T // P):
                                ins = mm(ps[b * VD:b * VD + VD, 7, q * P:q * P + P],
                                         Vh[:, b, c * VD:c * VD + VD], PT[:, q % 2, c * P:c * P + P],
                                         start=(c == first), stop=(c == T // P - 1))
                            if q == n_q - 1:
                                ins.then_inc(sem("attention_ready"), 1)

                        scores(0)
                        for q in range(n_q):
                            if q + 1 < n_q:
                                scores(q + 1)
                            pe.wait_ge(sem("probs_ready"), qbase + q + 1)
                            for c in range(keys(q)[0] // P, T // P):
                                ins = pe.transpose(ps[:, 5 + q % 2, c * P:c * P + P], Pb[:, q % 2, c * P:c * P + P], ident)
                            ins.then_inc(sem("probs_turned"), 1)
                            if q:
                                values(q - 1)
                        values(n_q - 1)
                handover("pe", pe)
                if stop == "attn":
                    return

                for o in range(RT):
                    n, j = L_R + o // 4, o % 4
                    if j == 0:
                        loaded(pe, l, n)
                    if o >= 8:
                        pe.wait_ge(sem("rin_copied"), RT * l + o - 7)
                    product(o % 8, T, weights(n, 256 if n == L_WAG else 512, j), lambda k: H[:, k, :], KD)\
                        .then_inc(sem("rin_ready"), 1)
                handover("pe", pe)
                if stop == "rin":
                    return

                for j in range(RJ):
                    pe.wait_ge(sem("key_squares"), RJ * l + j + 1)
                    mm(ps[:, j, :], hsum, B[0][:, j, :], start=True, stop=True).then_inc(sem("key_sums"), 1)
                loaded(pe, l, L_LORA)
                pe.wait_ge(sem("decay_input"), l + 1)
                for u in range(2 * RJ):
                    j, d = u // 2, u % 2
                    for half in range(2):
                        if 2 * u + half >= 4:
                            pe.wait_ge(sem("lora_gates"), 16 * l + 2 * u + half - 3)
                        r = slice(64 * half, 64 * half + 64)
                        mm(ps[:, 4 + (2 * u + half) % 4, :], slot(L_LORA)[r, d * RD + j * P:d * RD + j * P + P], WA[r, 0, :],
                           start=True, stop=True).then_inc(sem("lora_up"), 1)
                handover("pe", pe)
                if stop == "pre":
                    return

                for s in range(2):
                    with pe.Fori(0, NCH) as c:
                        step = (2 * l + s) * NCH + c

                        def region(d, n):
                            return ps[:, 4 * d + n // 2, (n % 2) * 256:(n % 2) * 256 + 256].rearrange("p (j n) -> p j n", n=CH)

                        def pairs(out, *terms):
                            for j in range(RJ):
                                for hh in (slice(0, 64), slice(64, 128)):
                                    for n, (lhs, rhs) in enumerate(terms):
                                        r = rhs[hh, 0:CH] if len(rhs.shape) == 2 else rhs[hh, j, :]
                                        ins = mm(out[hh, j, :], lhs[hh, j, :], r, start=(n == 0), stop=(n == len(terms) - 1))
                            return ins

                        b_ = lambda name, d: SB[name][d]
                        eye = con_("eye")
                        for d in range(2):
                            wait_apart(pe, f"scaled{d}", 2 * step + 2)
                            pairs(region(d, 0), (b_("E2", d), b_("E3", d)))
                            pairs(region(d, 1), (b_("E3", d), b_("E2", d)))
                            pairs(region(d, 2), (b_("Kk", d), b_("E3", d)))
                            pairs(region(d, 3), (b_("E2", d), b_("Rq", d)))
                            pairs(region(d, 4), (b_("Kk", d), b_("Rq", d)))
                            pairs(region(d, 5), (b_("E2", d), eye))
                            pairs(region(d, 6), (b_("Kk", d), eye))
                            pairs(region(d, 7), (b_("Vc", d), eye)).then_inc(sem(f"grams{d}"), 1)
                        for n in range(len(LEVELS)):
                            last = n == len(LEVELS) - 1
                            for d in range(2):
                                wait_apart(pe, f"blocks{d}", step * (len(LEVELS) + 1) + n + 2)
                                wait_apart(pe, f"inverse{d}", step * (len(LEVELS) + 1) + n + 1)
                                pairs(region(d, 0), (b_("BT", d), b_("X", d))).then_inc(sem(f"joined{d}"), 1)
                            for d in range(2):
                                wait_apart(pe, f"joined_copied{d}", step * len(LEVELS) + n + 1)
                                if n == 0:
                                    wait_apart(pe, f"masked{d}", step + 1)
                                if not last:
                                    pairs(region(d, 2), (b_("XT", d), b_("P", d)))
                                pairs(region(d, 3), (b_("P", d), b_("XT", d))).then_inc(sem(f"grown{d}"), 1)
                        for d in range(2):
                            wait_apart(pe, f"turned{d}", step + 1)
                            wait_apart(pe, f"inverse{d}", step * (len(LEVELS) + 1) + len(LEVELS) + 1)
                            wait_apart(pe, f"state{d}", step + l + 1)
                            pairs(region(d, 4), (b_("E3", d), b_("S", d)), (b_("Gak", d), b_("Vt", d))).then_inc(sem(f"rhs{d}"), 1)
                        for d in range(2):
                            wait_apart(pe, f"rhs_copied{d}", step + 1)
                            pairs(region(d, 5), (b_("XT", d), b_("RHS", d))).then_inc(sem(f"u{d}"), 1)
                        for d in range(2):
                            wait_apart(pe, f"u_copied{d}", step + 1)
                            pairs(region(d, 6), (b_("S", d), b_("Rq", d)), (b_("U", d), b_("Grb", d)),
                                  (b_("Vt", d), b_("Grk", d)))
                            pairs(region(d, 7), (b_("Bt", d), b_("U", d)), (b_("Kt", d), b_("Vt", d)))\
                                .then_inc(sem(f"step{d}"), 1)
                handover("pe", pe)
                if stop == "scan":
                    return

                for j in range(RJ):
                    pe.wait_ge(sem("bonus_input"), RJ * l + j + 1)
                    mm(ps[:, 4 * (j % 2), :], hsum, TS[:, 0, :], start=True, stop=True)
                    mm(ps[:, 4 * (j % 2) + 1, :], hsum, Y[:, j, :], start=True, stop=True)
                    mm(ps[:, 4 * (j % 2) + 2, :], slot(L_LORA)[:, 1024 + j * P:1024 + j * P + P], GX[:, 0, :],
                       start=True, stop=True).then_inc(sem("head_sums"), 1)
                    pe.wait_ge(sem("centred_squares"), RJ * l + j + 1)
                    mm(ps[:, 4 * (j % 2) + 3, :], hsum, TS[:, 1, :], start=True, stop=True).then_inc(sem("head_vars"), 1)
                handover("pe", pe)
                if stop == "post":
                    return

                o = 24 * l
                for g in range(2):
                    for b, branch in enumerate((FO, AO, Y)):
                        n = L_MERGE + 6 * g + 2 * b
                        loaded(pe, l, n)
                        loaded(pe, l, n + 1)
                        for j in range(4):
                            if o - 24 * l >= 4:
                                pe.wait_ge(sem("merged"), o - 3)
                            product(2 * (o % 4), w, weights(n, 512, j), lambda k: H[:, k, 0:w], KD)\
                                .then_inc(sem("merge_gate"), 1)
                            product(2 * (o % 4) + 1, w, weights(n + 1, 512, j), lambda k: branch[:, k, 0:w], 4)\
                                .then_inc(sem("merge_proj"), 1)
                            o += 1
                handover("pe", pe)
                if stop == "merge":
                    return
                for j in range(KD):
                    if j % 4 == 0:
                        loaded(pe, l, L_OUT + j // 4)
                    product(j, w, weights(L_OUT + j // 4, 512, j % 4), lambda k: M[:, k, 0:w], KD)\
                        .then_inc(sem("out_ready"), 1)
                handover("pe", pe)
                sum_squares(w)
                if stop == "norm2":
                    return

                for t in range(w // P):
                    for k in range(KD):
                        ins = mm(ps[:, 0, t * NE:t * NE + NE], H[:, k, t * P:t * P + P], rws[:, k, :],
                                 start=(k == 0), stop=(k == KD - 1))
                ins.then_inc(sem("router_ready"), 1)
                pe.wait_ge(sem("combine_ready"), l + 1)
                for t in range(w // P):
                    ins = pe.transpose(ps[0:NE, 1, t * P:t * P + P], rt[9][:, t * NE:t * NE + NE], ident)
                ins.then_inc(sem("combine_turned"), 1)
                handover("pe", pe)
                if stop == "router":
                    return

                def expert(e):
                    ub, db = 4 * ((NE + 1) * l + e), 8 * ((NE + 1) * l + e)
                    loaded(pe, l, L_EXP, e)
                    loaded(pe, l, L_EXP + 1, e)
                    for j in range(FK):
                        if j >= 2:
                            pe.wait_ge(sem("hidden_ready"), ub + j - 1)
                        product(2 * (j % 2), w, weights(L_EXP, 512, j), lambda k: H[:, k, 0:w], KD)\
                            .then_inc(sem("gate_ready"), 1)
                        product(2 * (j % 2) + 1, w, weights(L_EXP + 1, 512, j), lambda k: H[:, k, 0:w], KD)\
                            .then_inc(sem("up_ready"), 1)
                    loaded(pe, l, L_EXP + 2, e)
                    pe.wait_ge(sem("hidden_ready"), ub + FK)
                    for j in range(KD):
                        wait(pe, "down_added", db + max(j - 3, 0))
                        product(4 + j % 4, w, weights(L_EXP + 2, 1024, j), lambda k: HS[:, k, 0:w], FK)\
                            .then_inc(sem("down_ready"), 1)

                expert(0)
                with pe.Fori(0, NE) as e:
                    expert(e + 1)
                handover("pe", pe)
                if stop == "moe":
                    return
            sum_squares(SEQ)

        @block.scalar
        def _(act):
            link = Chain(act, "act_order")

            def rsqrt(out, x, n, eps):
                link(act.activation(out, x, ACT.Ln, bias=epst[:, eps:eps + 1], scale=1.0 / n))
                return act.activation(out, out, ACT.Exp, scale=-0.5)

            norms = 0

            def norm(w):
                nonlocal norms
                for k in range(KD):
                    act.activation(H[:, k, 0:w], X[:, k, 0:w], ACT.Square).then_inc(sem("squares"), 1)
                norms += 1
                act.wait_ge(sem("sumsq"), norms)
                rsqrt(RS[:, 0, 0:w], ps[:, 0, 0:w], D, 0).then_inc(sem("rstd"), 1)
                handover("act", act, act.copy(dummy[:, 1:2], epst[:, 0:1]))

            act.wait_ge(sem("params"), 16 * 7)
            act.wait_ge(sem("eps"), 3)
            act.activation(csil[:], csil[:], ACT.Silu).then_inc(sem("csil"), 1)
            act.preload_act_table_set("natural_log_exp_and_others")

            for l in range(DEPTH):
                w = width[l]
                handover("act", act, act.copy(dummy[:, 1:2], epst[:, 0:1]))
                if stop == "ada":
                    return
                norm(T)
                if stop == "norm1":
                    return

                dst = [FZ[:, j, 0:w] for j in range(4)] + [CQ[:, j, 0:w] for j in range(3)] + \
                      [CKV[:, j, :] for j in range(2)] + [KR[0:QK, 0, :]]
                for o, out_ in enumerate(dst):
                    act.wait_ge(sem("ina_ready"), 10 * l + o + 1)
                    act.copy(out_, ps[0:out_.shape[0], o % 8, 0:out_.shape[1]]).then_inc(sem("ina_copied"), 1)
                handover("act", act, act.copy(dummy[:, 1:2], epst[:, 0:1]))
                if stop == "ina":
                    return

                base = sum(four[:l])
                for u, (g, q) in enumerate((g, q) for g in range(FG) for q in range(four[l] // FG)):
                    act.wait_ge(sem("fourier_ready"), base + u + 1)
                    act.copy(FO[:, g, q * SEQ:q * SEQ + SEQ], ps[:, 2 + u % 2, 0:SEQ]).then_inc(sem("fourier_out"), 1)
                handover("act", act, act.copy(dummy[:, 1:2], epst[:, 0:1]))
                if stop == "fourier":
                    return

                for k in range(3):
                    act.activation(SQ[:, k, 0:w], CQ[:, k, 0:w], ACT.Square).then_inc(sem("lora_squares"), 1)
                for k in range(2):
                    act.activation(SQ[:, 3 + k, :], CKV[:, k, :], ACT.Square).then_inc(sem("lora_squares"), 1)
                act.wait_ge(sem("lora_sums"), 2 * l + 1)
                rsqrt(RQ[:, 0, 0:w], ps[:, 0, 0:w], QL, 0).then_inc(sem("lora_rstd"), 1)
                act.wait_ge(sem("lora_sums"), 2 * l + 2)
                rsqrt(RQ[:, 1, :], ps[:, 1, :], KVL, 0).then_inc(sem("lora_rstd"), 1)
                for t in range(T // P):
                    act.wait_ge(sem("values_ready"), 4 * l + t + 1)
                    act.copy(VT[:, t, :], ps[:, 4 + t, :])
                handover("act", act, act.copy(dummy[:, 1:2], epst[:, 0:1]))
                if stop == "lora":
                    return

                n_q = nqt[l]
                with act.Fori(0, HEADS // 2) as i:
                    for b in range(2):
                        h = l * HEADS + 2 * i + b
                        qbase = HEADS * sum(nqt[:l]) + (2 * i + b) * n_q
                        act.wait_ge(sem(f"heads_made{b}"), l * (HEADS // 2) + i + 1)
                        act.copy(Qh[0:QK, b, 0:w], ps[0:QK, 0, 0:w]).then_inc(sem("heads_copied"), 1)
                        act.copy(Kh[0:NOPE, b, :], ps[0:NOPE, 1, :]).then_inc(sem("heads_copied"), 1)

                        def exps(q):
                            k0 = 0 if q < SEQ // P else SEQ
                            act.wait_ge(sem("probs_max"), qbase + q + 1)
                            if q >= 2:
                                act.wait_ge(sem("probs_turned"), qbase + q - 1)
                            act.activation(Pb[:, q % 2, k0:T], ps[:, 3 + q % 2, k0:T], ACT.Exp, scale=SCALE,
                                           bias=small[:, 2 + q % 2:3 + q % 2],
                                           accum_out=small[:, 4 + q % 2:5 + q % 2]).then_inc(sem("probs_exp"), 1)

                        exps(0)
                        for q in range(n_q):
                            if q + 1 < n_q:
                                exps(q + 1)
                            k0 = 0 if q < SEQ // P else SEQ
                            act.wait_ge(sem("probs_turned"), qbase + q + 1)
                            act.copy(PT[:, q % 2, k0:T], ps[:, 5 + q % 2, k0:T]).then_inc(sem("probs_copied"), 1)
                handover("act", act, act.copy(dummy[:, 1:2], epst[:, 0:1]))
                if stop == "attn":
                    return

                for o in range(RT):
                    act.wait_ge(sem("rin_ready"), RT * l + o + 1)
                    act.wait_ge(sem("rin_padded"), l + 1)
                    if o >= 2:
                        act.wait_ge(sem("rin_mixed"), RT * l + o - 1)
                    act.copy(PP[:, o % 2, :, 1:SEQ + 1], ps[:, o % 8, :].rearrange("p (s n) -> p s n", s=2))\
                       .then_inc(sem("rin_copied"), 1)
                handover("act", act, act.copy(dummy[:, 1:2], epst[:, 0:1]))
                if stop == "rin":
                    return

                for j in range(RJ):
                    act.wait_ge(sem("key_sums"), RJ * l + j + 1)
                    rsqrt(B[1][:, j, :], ps[:, j, :], 1, 1).then_inc(sem("key_rstd"), 1)
                act.activation(WA[0:64, 0, :], WA[0:64, 0, :], ACT.Tanh).then_inc(sem("decay_input"), 1)
                act.activation(GX[:, 0, :], GX[:, 0, :], ACT.Sigmoid)
                for u in range(2 * RJ):
                    j, d = u // 2, u % 2
                    for half, (out_, v) in enumerate(((LW[d][:, j, :], "w0"), (TS[:, u % 2, :], "a0"))):
                        act.wait_ge(sem("lora_up"), 16 * l + 2 * u + half + 1)
                        if half and u >= 2:
                            act.wait_ge(sem("rates_used"), 8 * l + u - 1)
                        col = VEC[v] + d * RJ + j
                        act.activation(out_, ps[:, 4 + (2 * u + half) % 4, :], ACT.Sigmoid, bias=vecs[:, l, col:col + 1])\
                           .then_inc(sem("lora_gates"), 1)
                act.preload_act_table_set("natural_log_exp_and_others")
                handover("act", act, act.copy(dummy[:, 1:2], epst[:, 0:1]))
                if stop == "pre":
                    return

                for s in range(2):
                    with act.Fori(0, NCH) as c:
                        step = (2 * l + s) * NCH + c
                        flat = lambda name, d: SB[name][d].rearrange("p j n -> p (j n)")
                        reg = lambda d, n: ps[:, 4 * d + n // 2, (n % 2) * 256:(n % 2) * 256 + 256]
                        for d in range(2):
                            act.wait_ge(sem(f"cumulated{d}"), step + 1)
                            act.activation(flat("E1", d), flat("L", d), ACT.Exp, scale=-DECAY).then_inc(sem(f"exps{d}"), 1)
                            act.activation(flat("E2", d), flat("L", d), ACT.Exp, scale=DECAY).then_inc(sem(f"exps{d}"), 1)
                            act.wait_ge(sem(f"before{d}"), step + 1)
                            act.activation(flat("E3", d), flat("E3", d), ACT.Exp, scale=-DECAY).then_inc(sem(f"exps{d}"), 1)
                        for d in range(2):
                            act.wait_ge(sem(f"grams{d}"), step + 1)
                            for n, name in ((6, "Kt"), (7, "Vt")):
                                ins = act.copy(flat(name, d), reg(d, n))
                            ins.then_inc(sem(f"turned{d}"), 1)
                        for n in range(len(LEVELS)):
                            for d in range(2):
                                act.wait_ge(sem(f"joined{d}"), step * len(LEVELS) + n + 1)
                                act.copy(flat("P", d), reg(d, 0)).then_inc(sem(f"joined_copied{d}"), 1)
                        for d in range(2):
                            act.wait_ge(sem(f"rhs{d}"), step + 1)
                            act.copy(flat("RHS", d), reg(d, 4)).then_inc(sem(f"rhs_copied{d}"), 1)
                        for d in range(2):
                            act.wait_ge(sem(f"u{d}"), step + 1)
                            act.copy(flat("U", d), reg(d, 5)).then_inc(sem(f"u_copied{d}"), 1)
                handover("act", act, act.copy(dummy[:, 1:2], epst[:, 0:1]))
                if stop == "scan":
                    return

                for j in range(RJ):
                    act.wait_ge(sem("head_vars"), RJ * l + j + 1)
                    rsqrt(B[0][:, j, :], ps[:, 4 * (j % 2) + 3, :], RN, 2).then_inc(sem("head_rstd"), 1)
                handover("act", act, act.copy(dummy[:, 1:2], epst[:, 0:1]))
                if stop == "post":
                    return

                act.preload_act_table_set("sigmoid_and_others")
                for o in range(24 * l, 24 * l + 24):
                    act.wait_ge(sem("merge_gate"), o + 1)
                    if o - 24 * l >= 2:
                        act.wait_ge(sem("merged"), o - 1)
                    act.activation(SG[:, o % 2, 0:w], ps[:, 2 * (o % 4), 0:w], ACT.Sigmoid).then_inc(sem("merge_sigmoid"), 1)
                act.preload_act_table_set("natural_log_exp_and_others")
                handover("act", act, act.copy(dummy[:, 1:2], epst[:, 0:1]))
                if stop == "merge":
                    return
                handover("act", act, act.copy(dummy[:, 1:2], epst[:, 0:1]))
                norm(w)
                if stop == "norm2":
                    return

                act.wait_ge(sem("router_ready"), l + 1)
                act.activation(rt[0][:, 0:w // P * NE], ps[:, 0, 0:w // P * NE], ACT.Sigmoid).then_inc(sem("router_scores"), 1)
                act.preload_act_table_set("silu_and_others")
                handover("act", act, act.copy(dummy[:, 1:2], epst[:, 0:1]))
                if stop == "router":
                    return

                def expert(e):
                    ub = FK * ((NE + 1) * l + e)
                    for j in range(FK):
                        act.wait_ge(sem("gate_ready"), ub + j + 1)
                        act.activation(HS[:, j, 0:w], ps[:, 2 * (j % 2), 0:w], ACT.Silu).then_inc(sem("gate_silu"), 1)

                expert(0)
                with act.Fori(0, NE) as e:
                    expert(e + 1)
                act.preload_act_table_set("natural_log_exp_and_others")
                handover("act", act, act.copy(dummy[:, 1:2], epst[:, 0:1]))
                if stop == "moe":
                    return
            norm(SEQ)

        @block.vector
        def _(dve):
            link = Chain(dve, "dve_order")
            tt, stt, ts = dve.tensor_tensor, dve.scalar_tensor_tensor, dve.tensor_scalar

            def over():
                handover("dve", dve, dve.memset(dummy[:, 0:1], 0.0))

            norms = 0

            def norm(w, l, n):
                nonlocal norms
                norms += 1
                dve.wait_ge(sem("rstd"), norms)
                for k in range(KD):
                    link(tt(H[:, k, 0:w], X[:, k, 0:w], RS[:, 0, 0:w], ALU.mult))
                    for s in range(w // SEQ):
                        x = H[:, k, s * SEQ:s * SEQ + SEQ]
                        ts(x, x, gsc[:, n, k, s:s + 1], mod[:, 24 * n + k, s:s + 1], ALU.mult, ALU.add)
                over()

            dve.wait_ge(sem("params"), 16 * 7)
            for l in range(DEPTH):
                w = width[l]

                def vec_(name, j=0, n=1):
                    return vecs[:, l, VEC[name] + j:VEC[name] + j + n]

                with dve.Fori(0, N_ADA // NSLOT) as i:
                    at = N_ADA * l + i * NSLOT

                    def row(s):
                        dve.wait_ge(sem("ada_rows"), at + s + 1)
                        dve.tensor_copy(ROW[0:2, s, :], ps[0:2, s, :]).then_inc(sem("ada_copied"), 1)

                    def cols(s):
                        dve.wait_ge(sem("ada_cols"), at + s + 1)
                        c = (i * NSLOT + s) * 4
                        tt(mod[:, bass.ds(c, 4), :], ps[:, 3 + s, 0:8].rearrange("p (c q) -> p c q", q=2),
                           vecs[:, l, bass.ds(VEC["bada"] + c, 4)].unsqueeze(2).broadcast_to([P, 4, 2]), ALU.add)\
                            .then_inc(sem("ada_mod"), 1)
                    row(0)
                    row(1)
                    cols(0)
                    row(2)
                    cols(1)
                    cols(2)
                dve.wait_ge(sem("ada_mod"), N_ADA * (l + 1) + 1)
                for n, name in enumerate(("n1", "n2")):
                    for s in range(2):
                        stt(gsc[:, n, :, s], mod[:, 24 * n + 8:24 * n + 16, s], 1.0, vec_(name, 0, KD), ALU.add, ALU.mult)
                over()
                if stop == "ada":
                    return
                norm(T, l, 0)
                if stop == "norm1":
                    return
                over()
                if stop == "ina":
                    return

                base = sum(four[:l])
                for u in range(four[l]):
                    dve.wait_ge(sem("fourier_first"), base + u + 1)
                    if u >= 2:
                        dve.wait_ge(sem("fourier_ready"), base + u - 1)
                    dve.tensor_copy(FA[:, u % 2, :], ps[:, u % 2, :]).then_inc(sem("fourier_mid"), 1)
                over()
                if stop == "fourier":
                    return

                rr = slice(NOPE, QK)
                cos, sin = (cons[rr, CON[x]:CON[x] + SEQ] for x in ("cos", "sin"))
                dve.wait_ge(sem("key_turned"), l + 1)
                link(tt(RP[rr, 0, 0:SEQ], ps[rr, 2, 0:SEQ], sin, ALU.mult))
                link(tt(KR[rr, 0, 0:SEQ], KR[rr, 0, 0:SEQ], cos, ALU.mult))
                link(tt(KR[rr, 0, 0:SEQ], KR[rr, 0, 0:SEQ], RP[rr, 0, 0:SEQ], ALU.add))
                for b in range(2):
                    dve.tensor_copy(Kh[rr, b, :], KR[rr, 0, :])
                dve.wait_ge(sem("lora_rstd"), 2 * l + 1)
                for k in range(3):
                    stt(CQ[:, k, 0:w], CQ[:, k, 0:w], vec_("qg", k), RQ[:, 0, 0:w], ALU.mult, ALU.mult)
                dve.wait_ge(sem("lora_rstd"), 2 * l + 2)
                for k in range(2):
                    ins = stt(CKV[:, k, :], CKV[:, k, :], vec_("kvg", k), RQ[:, 1, :], ALU.mult, ALU.mult)
                ins.then_inc(sem("lora_normed"), 1)
                over()
                if stop == "lora":
                    return

                n_q = nqt[l]
                with dve.Fori(0, HEADS // 2) as i:
                    link.loop(i, 2 * (2 + 2 * n_q))
                    for b in range(2):
                        h = l * HEADS + 2 * i + b
                        qbase = HEADS * sum(nqt[:l]) + (2 * i + b) * n_q
                        dve.tensor_copy(Vh[:, b, :].rearrange("p (c n) -> p c n", n=VD),
                                        VT[:, :, bass.ds((2 * i + b) * VD, VD)])
                        dve.wait_ge(sem("query_turned"), h + 1)
                        link(tt(RP[rr, 0, 0:SEQ], ps[rr, 2, 0:SEQ], sin, ALU.mult))
                        link(tt(Qh[rr, b, 0:SEQ], Qh[rr, b, 0:SEQ], cos, ALU.mult))
                        tt(Qh[rr, b, 0:SEQ], Qh[rr, b, 0:SEQ], RP[rr, 0, 0:SEQ], ALU.add).then_inc(sem("query_done"), 1)

                        def largest(q):
                            k0 = 0 if q < SEQ // P else SEQ
                            dve.wait_ge(sem("scores_ready"), qbase + q + 1)
                            link(dve.tensor_reduce(small[:, q % 2:q % 2 + 1], ps[:, 3 + q % 2, k0:T], AX_X, ALU.max))
                            ts(small[:, 2 + q % 2:3 + q % 2], small[:, q % 2:q % 2 + 1], -SCALE, None, ALU.mult)\
                                .then_inc(sem("probs_max"), 1)

                        largest(0)
                        for q in range(n_q):
                            if q + 1 < n_q:
                                largest(q + 1)
                            k0 = 0 if q < SEQ // P else SEQ
                            dve.wait_ge(sem("probs_exp"), qbase + q + 1)
                            link(dve.reciprocal(small[:, 6 + q % 2:7 + q % 2], small[:, 4 + q % 2:5 + q % 2]))
                            ts(Pb[:, q % 2, k0:T], Pb[:, q % 2, k0:T], small[:, 6 + q % 2:7 + q % 2], None, ALU.mult)\
                                .then_inc(sem("probs_ready"), 1)
                        dve.wait_ge(sem("attention_ready"), h + 1)
                        half = slice(b * VD, b * VD + VD)
                        dve.tensor_copy(work[half, bass.ds(2048 + i * T, w)], ps[half, 7, 0:w])\
                           .then_inc(sem("heads_out"), 1)
                link.end(HEADS // 2)
                over()
                if stop == "attn":
                    return

                for o in range(RT):
                    dst = [R, K1, V][o // 4][:, o % 4, :] if o < 12 else (WA, GX)[o - 12][:, 0, :]
                    p = PP[:, o % 2, :, 1:SEQ + 1]
                    t = TS[:, 0, :].rearrange("p (s n) -> p s n", s=2)
                    dve.wait_ge(sem("rin_copied"), RT * l + o + 1)
                    link(tt(t, PP[:, o % 2, :, 0:SEQ], PP[:, o % 2, :, 2:SEQ + 2], ALU.add))
                    link(stt(t, t, 0.5, p, ALU.mult, ALU.subtract))
                    stt(dst.rearrange("p (s n) -> p s n", s=2), t, vec_("mu", o), p, ALU.mult, ALU.add)\
                        .then_inc(sem("rin_mixed"), 1)
                    dve.wait_ge(sem("rin_mixed"), RT * l + o + 1)
                over()
                if stop == "rin":
                    return

                for j in range(RJ):
                    link(ts(KK[:, j, :], K1[:, j, :], vec_("kk", j), None, ALU.mult))
                    tt(B[0][:, j, :], KK[:, j, :], KK[:, j, :], ALU.mult).then_inc(sem("key_squares"), 1)
                for j in range(RJ):
                    dve.wait_ge(sem("key_rstd"), RJ * l + j + 1)
                    link(tt(KK[:, j, :], KK[:, j, :], B[1][:, j, :], ALU.mult))
                for u in range(2 * RJ):
                    j, d = u // 2, u % 2
                    rate = TS[:, u % 2, :]
                    dve.wait_ge(sem("lora_gates"), 16 * l + 2 * u + 2)
                    link(tt(B[d][:, j, :], KK[:, j, :], rate, ALU.mult))
                    link(ts(rate, rate, -1.0, vec_("ka", j), ALU.add, ALU.mult))
                    stt(KDs[d][:, j, :], rate, 1.0, K1[:, j, :], ALU.add, ALU.mult).then_inc(sem("rates_used"), 1)
                link(dve.memset(Y[:, :, :], 0.0))
                for d in range(2):
                    dve.memset(SB["S"][d], 0.0).then_inc(sem(f"state{d}"), 1)
                over()
                if stop == "pre":
                    return

                for s in range(2):
                    with dve.Fori(0, NCH) as c:
                        link.loop(c, 2 + 2 * (2 + 1 + len(LEVELS) - 1 + 2))
                        step = (2 * l + s) * NCH + c
                        flat = lambda name, d: SB[name][d].rearrange("p j n -> p (j n)")
                        reg = lambda d, n: ps[:, 4 * d + n // 2, (n % 2) * 256:(n % 2) * 256 + 256]\
                            .rearrange("p (j n) -> p j n", n=CH)
                        b_ = lambda name, d: SB[name][d]
                        at = [(1 - s) * SEQ + c * CH, (1 - s) * SEQ + (NCH - 1) * CH - c * CH]
                        for d in range(2):
                            dve.wait_ge(sem(f"decays{d}"), step + 1)
                            if d == 0:
                                dve.tensor_tensor_scan(flat("L", 0), con_("reset", RJ * CH), flat("lw", 0), 0.0,
                                                       ALU.mult, ALU.add).then_inc(sem("cumulated0"), 1)
                            else:
                                link(dve.tensor_tensor_scan(flat("E1", 1), con_("reset", RJ * CH), flat("lw", 1), 0.0,
                                                            ALU.mult, ALU.add))
                                link(tt(b_("E3", 1), b_("lw", 1), b_("E1", 1), ALU.subtract))
                                tt(b_("L", 1), b_("E3", 1), b_("E1", 1)[:, :, CH - 1:CH].broadcast_to([P, RJ, CH]), ALU.add)\
                                    .then_inc(sem("cumulated1"), 1)
                        for d in range(2):
                            cols = bass.ds(at[d], CH)
                            wait_apart(dve, f"exps{d}", 3 * step + 3)
                            tt(b_("Kk", d), KDs[d][:, :, cols], b_("E2", d), ALU.mult)
                            link(tt(b_("E3", d), KK[:, :, cols], b_("E3", d), ALU.mult))
                            link(tt(b_("E2", d), B[d][:, :, cols], b_("E2", d), ALU.mult))
                            ts(b_("E3", d), b_("E3", d), -1.0, None, ALU.mult).then_inc(sem(f"scaled{d}"), 1)
                        for d in range(2):
                            dve.wait_ge(sem(f"grams{d}"), step + 1)
                            tt(b_("MT", d), reg(d, 0), over_pairs(con_(f"strict{d}")), ALU.mult).then_inc(sem(f"coupling{d}"), 1)
                            link(tt(b_("X", d), reg(d, 1), over_pairs(con_(f"pair{d}")), ALU.mult))
                            tt(b_("X", d), b_("X", d), over_pairs(con_("eye")), ALU.add).then_inc(sem(f"inverse{d}"), 1)
                            tt(b_("Gak", d), reg(d, 2), over_pairs(con_(f"strict{d}")), ALU.mult)
                            tt(b_("Grb", d), reg(d, 3), over_pairs(con_(f"incl{d}")), ALU.mult)
                            dve.tensor_copy(b_("Bt", d), reg(d, 5))
                            tt(b_("Grk", d), reg(d, 4), over_pairs(con_(f"incl{d}")), ALU.mult).then_inc(sem(f"masked{d}"), 1)
                        for n in range(len(LEVELS)):
                            for d in range(2):
                                dve.wait_ge(sem(f"grown{d}"), step * len(LEVELS) + n + 1)
                                if n < len(LEVELS) - 1:
                                    link(tt(b_("X", d), b_("X", d), reg(d, 2), ALU.add))
                                tt(b_("XT", d), b_("XT", d), reg(d, 3), ALU.add).then_inc(sem(f"inverse{d}"), 1)
                        for d in range(2):
                            cols = bass.ds(at[d], CH)
                            end = CH - 1 if d == 0 else 0
                            wait_apart(dve, f"step{d}", step + 2)
                            link(tt(Y[:, :, cols], Y[:, :, cols], reg(d, 6), ALU.add))
                            link(tt(b_("S", d), b_("S", d), reg(d, 7), ALU.add))
                            tt(b_("S", d), b_("S", d), b_("E1", d)[:, :, end:end + 1].broadcast_to([P, RJ, CH]), ALU.mult)\
                                .then_inc(sem(f"state{d}"), 1)
                            dve.wait_ge(sem(f"state{d}"), step + l + 2)
                    link.end(NCH)
                over()
                if stop == "scan":
                    return

                for j in range(RJ):
                    bank = 4 * (j % 2)
                    link(tt(B[0][:, j, :], KDs[0][:, j, :], KDs[1][:, j, :], ALU.add))
                    stt(TS[:, 0, :], R[:, j, :], vec_("rk", j), B[0][:, j, :], ALU.mult, ALU.mult)\
                        .then_inc(sem("bonus_input"), 1)
                    dve.wait_ge(sem("head_sums"), RJ * l + j + 1)
                    y = KK[:, j, :]
                    link(stt(y, ps[:, bank + 1, :], -1.0 / RN, Y[:, j, :], ALU.mult, ALU.add))
                    tt(TS[:, 1, :], y, y, ALU.mult).then_inc(sem("centred_squares"), 1)
                    link(tt(B[1][:, j, :], ps[:, bank, :], V[:, j, :], ALU.mult))
                    dve.wait_ge(sem("head_rstd"), RJ * l + j + 1)
                    link(tt(y, y, B[0][:, j, :], ALU.mult))
                    link(ts(y, y, vec_("gng", j), vec_("gnb", j), ALU.mult, ALU.add))
                    link(tt(y, y, B[1][:, j, :], ALU.add))
                    link(tt(Y[:, j, :], y, ps[:, bank + 2, :], ALU.mult))
                over()
                if stop == "post":
                    return

                o = 24 * l
                for g in range(2):
                    for b in range(3):
                        for j in range(4):
                            dve.wait_ge(sem("merge_sigmoid"), o + 1)
                            dve.wait_ge(sem("merge_proj"), o + 1)
                            m = M[:, 4 * g + j, 0:w]
                            gate, proj = SG[:, o % 2, 0:w], ps[:, 2 * (o % 4) + 1, 0:w]
                            if b == 0:
                                tt(m, gate, proj, ALU.mult).then_inc(sem("merged"), 1)
                            else:
                                link(tt(TM[:, 0, 0:w], gate, proj, ALU.mult))
                                tt(m, m, TM[:, 0, 0:w], ALU.add).then_inc(sem("merged"), 1)
                                dve.wait_ge(sem("merged"), o + 1)
                            o += 1
                over()
                if stop == "merge":
                    return
                for j in range(KD):
                    dve.wait_ge(sem("out_ready"), KD * l + j + 1)
                    for s in range(w // SEQ):
                        x = X[:, j, s * SEQ:s * SEQ + SEQ]
                        stt(x, ps[:, j, s * SEQ:s * SEQ + SEQ], mod[:, 16 + j, s:s + 1], x, ALU.mult, ALU.add)
                over()
                norm(w, l, 1)
                if stop == "norm2":
                    return

                nt = w // P
                v3 = lambda x, n, q: x[:, 0:n * q].rearrange("p (n q) -> p n q", q=q)
                wide = lambda x, n, q: x[:, 0:n].unsqueeze(2).broadcast_to([P, n, q])
                prio = cons[:, CON["prio"]:CON["prio"] + NE]
                ng = nt * NG
                dve.wait_ge(sem("router_scores"), l + 1)
                sel = v3(rt[1], nt, NE)
                link(tt(sel, v3(rt[0], nt, NE), rbs[:, :].unsqueeze(1).broadcast_to([P, nt, NE]), ALU.add))
                x4, pr = v3(rt[1], ng, EPG), v3(rt[2], ng, 6)
                tt(pr[:, :, 0:3], x4[:, :, 0:3], x4[:, :, 1:4], ALU.add)
                tt(pr[:, :, 3:5], x4[:, :, 0:2], x4[:, :, 2:4], ALU.add)
                link(tt(pr[:, :, 5:6], x4[:, :, 0:1], x4[:, :, 3:4], ALU.add))
                link(dve.tensor_reduce(rt[3][:, 0:ng], pr, AX_X, ALU.max))

                def first_largest(out_, x, n, q, pri):
                    link(dve.tensor_reduce(rt[4][:, 0:n], v3(x, n, q), AX_X, ALU.max))
                    link(tt(v3(rt[5], n, q), v3(x, n, q), wide(rt[4], n, q), ALU.is_equal))
                    link(tt(v3(rt[5], n, q), v3(rt[5], n, q), pri.unsqueeze(1).broadcast_to([P, n, q]), ALU.mult))
                    link(dve.tensor_reduce(rt[4][:, 0:n], v3(rt[5], n, q), AX_X, ALU.max))
                    link(tt(v3(out_, n, q), v3(rt[5], n, q), wide(rt[4], n, q), ALU.is_equal))

                first_largest(rt[6], rt[3], nt, NG, prio[:, 0:NG])
                link(ts(rt[7][:, 0:ng], rt[6][:, 0:ng], 1e30, -1e30, ALU.mult, ALU.add))
                link(tt(x4, x4, wide(rt[6], ng, EPG), ALU.mult))
                link(tt(x4, x4, wide(rt[7], ng, EPG), ALU.add))
                first_largest(rt[6], rt[1], nt, NE, prio)
                link(stt(rt[1][:, 0:nt * NE], rt[6][:, 0:nt * NE], -1e35, rt[1][:, 0:nt * NE], ALU.mult, ALU.add))
                first_largest(rt[7], rt[1], nt, NE, prio)
                link(tt(rt[6][:, 0:nt * NE], rt[6][:, 0:nt * NE], rt[7][:, 0:nt * NE], ALU.add))
                link(tt(rt[8][:, 0:nt * NE], rt[6][:, 0:nt * NE], rt[0][:, 0:nt * NE], ALU.mult))
                link(dve.tensor_reduce(rt[4][:, 0:nt], v3(rt[8], nt, NE), AX_X, ALU.add))
                link(dve.reciprocal(rt[3][:, 0:nt], rt[4][:, 0:nt]))
                tt(v3(rt[9], nt, NE), v3(rt[8], nt, NE), wide(rt[3], nt, NE), ALU.mult).then_inc(sem("combine_ready"), 1)
                dve.wait_ge(sem("combine_turned"), l + 1)
                dve.tensor_copy(CT[0:NE, 0:w], ps[0:NE, 1, 0:w]).then_inc(sem("comb_rows"), 1)
                over()
                if stop == "router":
                    return

                def expert(e, shared):
                    ub, db = FK * ((NE + 1) * l + e), KD * ((NE + 1) * l + e)
                    if not shared:
                        dve.wait_ge(sem("comb_loaded"), 16 * (l * NE + e))
                    for j in range(FK):
                        hid = HS[:, j, 0:w]
                        dve.wait_ge(sem("gate_silu"), ub + j + 1)
                        dve.wait_ge(sem("up_ready"), ub + j + 1)
                        up = ps[:, 2 * (j % 2) + 1, 0:w]
                        if shared:
                            tt(hid, hid, up, ALU.mult).then_inc(sem("hidden_ready"), 1)
                        else:
                            link(tt(hid, hid, up, ALU.mult))
                            tt(hid, hid, CB[:, 0, 0:w], ALU.mult).then_inc(sem("hidden_ready"), 1)
                    for j in range(KD):
                        dve.wait_ge(sem("down_ready"), db + j + 1)
                        a, y = ACC[:, j, 0:w], ps[:, 4 + j % 4, 0:w]
                        if shared:
                            dve.tensor_copy(a, y).then_inc(sem("down_added"), 1)
                        else:
                            dve.wait_ge(sem("down_added"), db + j - KD + 1)
                            tt(a, a, y, ALU.add).then_inc(sem("down_added"), 1)

                expert(0, True)
                with dve.Fori(0, NE) as e:
                    link.loop(e, FK)
                    expert(e + 1, False)
                link.end(NE)
                dve.wait_ge(sem("down_added"), KD * (NE + 1) * (l + 1))
                for j in range(KD):
                    for s in range(w // SEQ):
                        x = X[:, j, s * SEQ:s * SEQ + SEQ]
                        stt(x, ACC[:, j, s * SEQ:s * SEQ + SEQ], mod[:, 40 + j, s:s + 1], x, ALU.mult, ALU.add)
                over()
                if stop == "moe":
                    return
            dve.wait_ge(sem("rstd"), 2 * DEPTH + 1)
            for k in range(KD):
                ins = stt(H[:, k, 0:SEQ], X[:, k, 0:SEQ], fngs[:, k:k + 1], RS[:, 0, 0:SEQ], ALU.mult, ALU.mult)
            ins.then_inc(sem("result"), 1)
            over()

        @block.gpsimd
        def _(pool):
            tt = pool.tensor_tensor
            over = lambda: handover("pool", pool, pool.memset(dummy[:, 2:3], 0.0))
            for n, eps in enumerate((EPS, 1e-12, GN_EPS)):
                pool.memset(epst[:, n:n + 1], eps).then_inc(sem("eps"), 1)
            for n, name in enumerate(("ada_mod", "heads_out", "step0", "step1")):
                pool.memset(small[:, n:n + 1], 0.0).then_inc(sem(name), 1)
            pool.wait_ge(sem("params"), 16 * 7)
            for l in range(DEPTH):
                for stage in ("ada", "norm1", "ina", "fourier", "lora", "attn"):
                    over()
                    if stop == stage:
                        return
                for col in (0, SEQ + 1):
                    ins = pool.memset(PP[:, :, :, col:col + 1], 0.0)
                ins.then_inc(sem("rin_padded"), 1)
                over()
                if stop == "rin":
                    return
                over()
                if stop == "pre":
                    return

                for s in range(2):
                    with pool.Fori(0, NCH) as c:
                        step = (2 * l + s) * NCH + c
                        b_ = lambda name, d: SB[name][d]
                        at = [(1 - s) * SEQ + c * CH, (1 - s) * SEQ + (NCH - 1) * CH - c * CH]
                        for d in range(2):
                            wait_apart(pool, f"step{d}", step + 1)
                            wait_apart(pool, f"state{d}", step + l + 1)
                            pool.tensor_copy(b_("lw", d), LW[d][:, :, bass.ds(at[d], CH)]).then_inc(sem(f"decays{d}"), 1)
                            pool.tensor_copy(b_("Vc", d), V[:, :, bass.ds(at[d], CH)])
                        for d in range(2):
                            pool.wait_ge(sem(f"cumulated{d}"), step + 1)
                            tt(b_("E3", d), b_("L", d), b_("lw", d), ALU.subtract).then_inc(sem(f"before{d}"), 1)
                            wait_apart(pool, f"exps{d}", 3 * step + 1)
                            tt(b_("Rq", d), R[:, :, bass.ds(at[d], CH)], b_("E1", d), ALU.mult).then_inc(sem(f"scaled{d}"), 1)
                        for d in range(2):
                            pool.wait_ge(sem(f"coupling{d}"), step + 1)
                            tt(b_("XT", d), b_("MT", d), over_pairs(con_("lev1")), ALU.mult).then_inc(sem(f"pool_order{d}"), 1)
                            pool.wait_ge(sem(f"pool_order{d}"), step + 1)
                            tt(b_("XT", d), b_("XT", d), over_pairs(con_("eye")), ALU.add).then_inc(sem(f"blocks{d}"), 1)
                        for n, b in enumerate(LEVELS):
                            for d in range(2):
                                if n:
                                    pool.wait_ge(sem(f"joined{d}"), step * len(LEVELS) + n)
                                tt(b_("BT", d), b_("MT", d), over_pairs(con_(f"lev{b}")), ALU.mult)\
                                    .then_inc(sem(f"blocks{d}"), 1)
                over()
                pool.memset(dummy[:, 3:4], 0.0).then_inc(sem("scan_over"), 1)
                if stop == "scan":
                    return
                over()
                pool.memset(dummy[:, 3:4], 0.0).then_inc(sem("post_over"), 1)
                if stop == "post":
                    return
                for stage in ("merge", "out", "norm2", "router", "moe"):
                    over()
                    if stop == stage:
                        return
            over()


def constants():
    con = np.zeros((P, NCON), np.float64)

    def put(name, a):
        con[0:a.shape[0], CON[name]:CON[name] + a.shape[1]] = a

    part = np.arange(P)
    put("ident", np.eye(P))
    put("ones", np.ones((P, P)))
    put("heads", (part[:, None] // RN == part[None] // RN) * 1.0)
    rot = np.zeros((QK, QK))
    half = ROPE // 4
    for axis in range(2):
        for n in range(half):
            first = NOPE + axis * 2 * half + n
            rot[first + half, first] = -1.0
            rot[first, first + half] = 1.0
    put("rot", rot)
    a, b = np.arange(P)[:, None] % CH, np.arange(CH)[None]
    put("strict0", a < b)
    put("strict1", a > b)
    put("incl0", a <= b)
    put("incl1", a >= b)

    def level(n):
        return (a // (2 * n) == b // (2 * n)) & (a // n != b // n)
    put("pair0", (a > b) & level(1))
    put("pair1", (a < b) & level(1))
    put("eye", a == b)
    put("lev1", level(1))
    for n in LEVELS:
        put(f"lev{n}", level(n))
    put("reset", np.tile((np.arange(RJ * CH) % CH != 0) * 1.0, (P, 1)))
    put("prio", np.tile(np.arange(NE, 0, -1.0), (P, 1)))
    t = np.arange(SEQ)
    inv = (10000.0 ** (-np.arange(half, dtype=np.float32) / np.float32(half))).astype(np.float32)
    ang = np.stack([t // GRID_W, t % GRID_W], -1).astype(np.float32)[..., None] * inv
    ang = np.repeat(ang[:, :, None, :], 2, 2).reshape(SEQ, ROPE).T.astype(np.float64)
    con[NOPE:QK, CON["cos"]:CON["cos"] + SEQ] = np.cos(ang)
    con[NOPE:QK, CON["sin"]:CON["sin"] + SEQ] = np.sin(ang)
    ch = 2 * np.pi * np.outer(np.arange(FGD), np.arange(FGD)) / FGD
    tk = 2 * np.pi * np.outer(t, t) / SEQ
    ct, st = (f(tk) * SEQ ** -0.5 for f in (np.cos, np.sin))
    dft = np.concatenate([f(ch) * FGD ** -0.5 for f in (np.cos, np.sin)] +
                         [x[n * P:n * P + P] for x in (ct, -st) for n in range(2)], 1)
    return con.astype(np.float32), dft.astype(np.float32)


def kernel(**inputs):
    from concourse import bacc
    from concourse.bass_utils import run_bass_kernel_spmd

    a = {k: np.asarray(v) for k, v in inputs.items()}
    L = DEPTH

    def cols(x):
        x = x.reshape(*x.shape[:-1], -1, P)
        return np.moveaxis(x, -1, 0)

    tok = np.concatenate([a["x"][0], a["ctx"][0]], 0)
    xT = cols(tok).transpose(0, 2, 1).reshape(P, KD * T)
    cT = cols(np.stack([a["c"][0], a["c_ctx"]])).transpose(0, 2, 1).reshape(P, KD * 2)
    parts = [a["norm1_g"], a["norm2_g"], a["b_ada"], a["q_norm_g"], a["kv_norm_g"], a["rwkv_mu"],
             a["rwkv_w0"].reshape(L, -1), a["rwkv_a0"].reshape(L, -1), a["rwkv_k_k"], a["rwkv_k_a"],
             a["rwkv_r_k"].reshape(L, -1), a["rwkv_gn_g"], a["rwkv_gn_b"]]
    vec = np.concatenate([cols(x) for x in parts], 2).reshape(P, L * NVEC)
    con, dft = constants()
    uq = a["w_uq"].reshape(L, 3, P, HEADS, QK).transpose(0, 3, 2, 1, 4).reshape(L, HEADS, P, 3 * QK)
    uk = a["w_ukv"].reshape(L, 2, P, HEADS, NOPE + VD)[..., :NOPE].transpose(0, 3, 2, 1, 4).reshape(L, HEADS, P, 2 * NOPE)
    up = np.concatenate([a["rwkv_w_up"], a["rwkv_a_up"]], 2).transpose(0, 2, 1, 3).reshape(L, P, 2 * RD)
    arrays = dict(
        xT=xT, cT=cT, vec=vec, fng=cols(a["final_norm_g"]), rb=np.tile(a["router_b"][None], (P, 1)),
        rw=a["router_w"].reshape(KD, P, NE).transpose(1, 0, 2).reshape(P, KD * NE),
        w_ada=a["w_ada"], w_in=a["w_in"], headw=np.concatenate([uq, uk], 3), w_ukv=a["w_ukv"],
        lora=np.concatenate([up, a["rwkv_g_up"]], 2), w_a=a["w_proj_a"], w_b=a["w_proj_b"], w_c=a["w_proj_c"],
        w_out=a["w_out"], eg=a["exp_w_gate"], eu=a["exp_w_up"], ed=a["exp_w_down"], sg=a["sh_w_gate"],
        su=a["sh_w_up"], sd=a["sh_w_down"], con=con, dft=dft)
    arrays = {f"in_{k}": np.ascontiguousarray(v) for k, v in arrays.items()}
    nc = bacc.Bacc("TRN2", target_bir_lowering=False, num_devices=1)
    args = {k[3:]: nc.dram_tensor(k, v.shape, mybir.dt.from_np(v.dtype), kind="ExternalInput").ap()
            for k, v in arrays.items()}
    out = nc.dram_tensor("out", (P, KD, SEQ), F32, kind="ExternalOutput").ap()
    build(nc, **args, out=out)
    r = run_bass_kernel_spmd(nc, [arrays], core_ids=[0])
    y = np.asarray(r.results[0]["out"]).reshape(P, KD, SEQ)
    return y.transpose(2, 1, 0).reshape(1, SEQ, D)
```

```python
from contextlib import ExitStack
import math

import numpy as np

import concourse.bass as bass
from concourse import mybir

F32 = mybir.dt.float32
ALU = mybir.AluOpType
ACT = mybir.ActivationFunctionType
AX_X = mybir.AxisListType.X
P = 128

D = 1024
KD = D // P
DEPTH = 2
SEQ, CTX = 256, 256
T = SEQ + CTX
GRID_W = 64
FG, FGD = 4, 128
HEADS, NOPE, ROPE, VD = 8, 64, 32, 64
QK = NOPE + ROPE
QL, KVL = 384, 256
SCALE = QK ** -0.5
RH, RN = 8, 64
RD = RH * RN
RJ = RD // P
RIN = 3 * RD + 64 + 64 + 128
RT = RIN // P
NE, NG, EPG, FF = 16, 4, 4, 512
FK = FF // P
EPS = 1e-6
GN_EPS = 64e-5
DECAY = math.exp(-0.5)
CH = 64
NCH = SEQ // CH
TILES = [T * 2 // P + NE, SEQ * 2 // P + NE]
NTAB = max(TILES)
ZEROS = 256
LEVELS = [2, 4, 8, 16, 32]

C_F, C_Q = 0, 512
C_KV = C_Q + QL
C_R = C_KV + KVL + ROPE
C_G = C_R + RIN
IN_DIM = C_G + 3 * D

VEC = {}
_n = 0
for _name, _w in (("n1", 8), ("n2", 8), ("bada", 48), ("qg", 3), ("kvg", 2), ("mu", RT), ("w0", 8), ("a0", 8),
                  ("kk", 4), ("ka", 4), ("rk", 4), ("gng", 4), ("gnb", 4)):
    VEC[_name] = _n
    _n += _w
NVEC = _n

CON = {}
_n = 0
for _name, _w in (("ident", P), ("ones", P), ("heads", P), ("rot", P), ("minus0", CH), ("minus1", CH),
                  ("incl0", CH), ("incl1", CH), ("before0", P), ("before1", P), ("pair0", P), ("pair1", P), ("same", P),
                  ("lev1", P), *((f"lev{b}", P) for b in LEVELS), ("reset", RJ * CH), ("prio", NE), ("before", P), ("iota", NTAB), ("cos", SEQ), ("sin", SEQ)):
    CON[_name] = _n
    _n += _w
NCON = _n
NDFT = 2 * FGD + 4 * SEQ
HW = 3 * QK + 2 * NOPE

NSLOT = 3
N_ADA = 12
L_F, L_Q, L_KV, L_DFT, L_UKV, L_R, L_K, L_V, L_WAG, L_LORA = range(N_ADA, N_ADA + 10)
L_MERGE = L_LORA + 1
L_OUT = L_MERGE + 12
L_EXP = L_OUT + 2
PER_LAYER = L_EXP + 3
assert N_ADA % NSLOT == 0 and L_EXP % NSLOT == 0 and PER_LAYER % NSLOT == 0
ROUNDS = PER_LAYER // NSLOT


def build(nc, xT, cT, vec, fng, rb, rw, w_ada, w_in, headw, w_ukv, lora, w_a, w_b, w_c, w_out,
          eg, eu, ed, sg, su, sd, con, dft, out, stop=None):
    xg = nc.dram_tensor("expert_rows", [(NTAB + 1) * P, D], F32).ap()
    width = [T, SEQ]
    with ExitStack() as ctx:
        def sb(name, shape):
            return ctx.enter_context(nc.sbuf_tensor(name, shape, F32))

        sems = {}

        def sem(name):
            if name not in sems:
                sems[name] = ctx.enter_context(nc.semaphore(name))
            return sems[name]

        ps = ctx.enter_context(nc.psum_tensor("ps", [P, 8, 512], F32))
        X = sb("X", [P, KD, T])
        H = sb("H", [P, KD, T])
        cons = sb("cons", [P, NCON])
        vecs = sb("vecs", [P, DEPTH, NVEC])
        fngs = sb("fngs", [P, KD])
        rbs = sb("rbs", [P, NE])
        rws = sb("rws", [P, KD, NE])
        epst = sb("epst", [P, 3])
        csil = sb("csil", [P, KD, 2])
        mod = sb("mod", [P, 48, 2])
        gsc = sb("gsc", [P, 2, KD, 2])
        dummy = sb("marks", [P, 4])
        small = sb("small", [P, 8])
        starts = sb("starts", [P, 16])
        WORK = 28928
        SETS = NSLOT * 4096
        memory = sb("memory", [P, SETS + WORK])
        W = memory[:, 0:SETS].rearrange("p (s n) -> p s n", s=NSLOT)
        work = memory[:, SETS:]
        zeros = work[:, WORK - ZEROS:]
        pos = ctx.enter_context(nc.sbuf_tensor("pos", [P, 2 * T // P], mybir.dt.int32))
        tile_expert = ctx.enter_context(nc.sbuf_tensor("tile_expert", [P, NTAB], mybir.dt.int32))
        tile_pairs = ctx.enter_context(nc.sbuf_tensor("tile_pairs", [P, DEPTH], mybir.dt.int32))

        def con_(name, w=CH):
            return cons[:, CON[name]:CON[name] + w]

        ident, ones, hsum = con_("ident", P), con_("ones", P), con_("heads", P)
        rot = cons[:, CON["rot"]:CON["rot"] + QK]

        def place(at, n, w=T):
            assert at + n * w <= WORK
            return work[:, at:at + n * w].rearrange("p (j n) -> p j n", n=w)

        FO, AO, Y = place(0, 4), place(2048, 4), place(4096, 4)
        GX, WA = place(6144, 1), place(6656, 1)
        TOP = 7168
        ROW = place(TOP, 3)
        RS = place(TOP, 2)
        FZ, FA = place(TOP, 4), place(TOP + 2048, 2)
        CQ, CKV = place(TOP + 3072, 3), place(TOP + 4608, 2)
        KR, VT = place(TOP + 5632, 1), place(TOP + 6144, 4)
        SQ, RQ = place(TOP + 8192, 5), place(TOP + 10752, 2)
        RP = place(TOP + 11776, 2)
        Qh, Kh, Pb, PT = (place(TOP + 12800 + 1024 * n, 2) for n in range(4))
        Vh, WH = place(TOP + 16896, 2, 256), place(TOP + 17408, 2, HW)
        R, V, KK = (place(TOP + 2048 * n, 4) for n in range(3))
        B = [place(TOP + 2048 * (3 + d), 4) for d in range(2)]
        K1 = place(TOP + 2048 * 5, 4)
        KDs = [place(TOP + 2048 * 6, 4), K1]
        LW = [place(TOP + 2048 * (7 + d), 4) for d in range(2)]
        SCR = TOP + 2048 * 9
        PP = work[:, SCR:SCR + 2 * 2 * 258].rearrange("p (b s n) -> p b s n", b=2, s=2)
        TS = place(SCR + 1032, 2)
        spare = [work[:, SCR + 512 * n:SCR + 512 * (n + 1)] for n in range(6)] + \
                [memory[:, 4096 * s_ + 512 * n:4096 * s_ + 512 * (n + 1)] for s_ in range(NSLOT)
                 for n in range(0 if s_ else 3, 8)]
        ER = [spare.pop(0).rearrange("p (x j n) -> p x j n", x=2, n=CH) for d in range(2)]
        SB = {"E3": [ER[d][:, 0] for d in range(2)], "Rq": [ER[d][:, 1] for d in range(2)]}
        for names in ((("lw", "MT"), ("L", "Grb")), (("E1",), ("E2", "Grk"))):
            for d in range(2):
                both = spare.pop(0)
                for x, same in enumerate(names):
                    for name in same:
                        SB.setdefault(name, []).append(both[:, 256 * x:256 * x + 256].rearrange("p (j n) -> p j n", n=CH))
        for same in (("bE2", "BT"), ("bKk", "Gak"), ("bV", "P", "RHS"), ("bE3",), ("Bt",), ("Kt",), ("Vt",), ("XT",),
                     ("X", "U"), ("S",)):
            for d in range(2):
                one = spare.pop(0).rearrange("p (j n) -> p j n", n=P)
                for name in same:
                    SB.setdefault(name, []).append(one)
        M, SG = place(TOP, 8), place(TOP + 4096, 2)
        TM = place(TOP + 5120, 1)
        W2 = work[:, 0:SETS].rearrange("p (s n) -> p s n", s=NSLOT)
        sets = [W, W2]
        MT_ = place(SETS, 4, D)
        YT = MT_
        HS = place(SETS + 4096, 4)
        XG, YG = place(SETS + 6144, 2, D), place(SETS + 8192, 2, D)
        XGT = place(SETS + 10240, KD, P)
        SIL, HID, HIDT = (place(SETS + 11264 + 512 * n, 1) for n in range(3))
        RO = SETS + 12800
        rt = [work[:, RO + 128 * n:RO + 128 * n + 128] for n in range(10)]
        small16 = [work[:, RO + 1280 + 16 * n:RO + 1296 + 16 * n] for n in range(8)]
        TAB = work[:, RO + 1408:RO + 1408 + NTAB * NE]
        assert RO + 1408 + NTAB * NE <= WORK - ZEROS

        def slot(n):
            return W[:, n % NSLOT, :]

        def loaded(eng, l, n, more=0):
            eng.wait_ge(sem(f"slot_loaded{n % NSLOT}"), 16 * (ROUNDS * l + n // NSLOT + 1 + more))

        four = [2 * FG, FG]
        nqt = [T // P, SEQ // P]
        PH = {"act": 0, "dve": 0, "pool": 0, "pe": 0}

        class Chain:

            def __init__(self, eng, name):
                self.eng, self.s, self.n, self.var = eng, sem(name), 0, 0

            def __call__(self, ins):
                self.n += 1
                ins.then_inc(self.s, 1)
                self.eng.wait_ge(self.s, self.var + self.n)

            def loop(self, i, per):
                self.start, self.per, self.var = self.n, per, i * per

            def end(self, times):
                assert self.n - self.start == self.per, (self.n - self.start, self.per)
                self.n, self.var = self.start + self.per * times, 0

        def handover(who, eng, ins=None):
            PH[who] += 1
            if ins is not None:
                ins.then_inc(sem(f"stage_{who}"), 1)
            for n in ("act", "dve", "pool"):
                eng.wait_ge(sem(f"stage_{n}"), PH[who])

        def wait(eng, name, count):
            if not (isinstance(count, int) and count == 0):
                eng.wait_ge(sem(name), count)

        def wait_apart(eng, name, count):
            eng.wait_ge(sem(name), count)
            eng.nop(nofuse=True)

        def pair_count(eng, l):
            return eng.value_load(tile_pairs[0:1, l:l + 1], min_val=1, max_val=TILES[l] // 2)

        def over_pairs(mask):
            return mask.unsqueeze(1).broadcast_to([P, RJ, mask.shape[1]])

        def both_heads(x):
            return x.unsqueeze(2).broadcast_to([P, RJ, 2, CH])

        def blocks(x):
            return x.rearrange("p j (h n) -> p j h n", h=2)

        def blocks_mask(name):
            return con_(name, P).rearrange("p (h n) -> p h n", h=2).unsqueeze(1).broadcast_to([P, RJ, 2, CH])

        block = ctx.enter_context(nc.Block())

        @block.sync
        def _(sp):
            for dst, src in ((X[:].rearrange("p k t -> p (k t)"), xT), (csil[:].rearrange("p k t -> p (k t)"), cT),
                             (cons[:], con), (vecs[:].rearrange("p l n -> p (l n)"), vec), (fngs[:], fng),
                             (rbs[:], rb), (rws[:].rearrange("p k e -> p (k e)"), rw)):
                sp.dma_start(dst, src).then_inc(sem("params"), 16)

            def rows(ap, k):
                return ap.rearrange("(k p) n -> p k n", k=k)

            def load(l, n, src, k, w, reader=None, count=0, more=0):
                if reader:
                    sp.wait_ge(sem(reader), count)
                sp.dma_start(slot(n)[:, 0:k * w].rearrange("p (k n) -> p k n", k=k), src)\
                    .then_inc(sem(f"slot_loaded{n % NSLOT}"), 16)

            pairs_before = 0
            for l in range(DEPTH):
                def ada(g):
                    return rows(w_ada[l, :, bass.ds(g * 512, 512)], KD), KD, 512
                for s in range(NSLOT):
                    its = pairs_before + 1
                    reader = ("tile_down0", its) if s == 2 else ("tile_up0", its)
                    load(l, s, *ada(s), *(reader if l else ()))
                with sp.Fori(1, N_ADA // NSLOT) as i:
                    for s in range(NSLOT):
                        load(l, s, *ada(i * NSLOT + s), "ada_rows", N_ADA * l + (i - 1) * NSLOT + s + 1)
                at = N_ADA * (l + 1)
                load(l, L_F, rows(w_in[l, :, C_F:C_F + 512], KD), KD, 512, "ada_rows", at - 2)
                load(l, L_Q, rows(w_in[l, :, C_Q:C_Q + QL], KD), KD, QL, "ada_rows", at - 1)
                load(l, L_KV, rows(w_in[l, :, C_KV:C_KV + KVL + ROPE], KD), KD, KVL + ROPE, "ada_rows", at)
                load(l, L_DFT, dft.rearrange("p (k n) -> p k n", k=1), 1, NDFT, "ina_ready", 10 * l + 4)
                load(l, L_UKV, rows(w_ukv[l], 2), 2, 1024, "ina_ready", 10 * l + 7)
                load(l, L_R, rows(w_in[l, :, C_R:C_R + 512], KD), KD, 512, "ina_ready", 10 * l + 10)
                for b in range(2):
                    if l:
                        sp.wait_ge(sem(f"heads_made{b}"), l * (HEADS // 2))
                    sp.dma_start(WH[:, b, :], headw[l, b, :, :]).then_inc(sem(f"headw_loaded{b}"), 16)
                with sp.Fori(1, HEADS // 2) as i:
                    for b in range(2):
                        sp.wait_ge(sem(f"heads_made{b}"), l * (HEADS // 2) + i)
                        sp.dma_start(WH[:, b, :], headw[l, bass.ds(2 * i + b, 1), :, :].rearrange("h p n -> p (h n)"))\
                            .then_inc(sem(f"headw_loaded{b}"), 16)
                load(l, L_K, rows(w_in[l, :, C_R + 512:C_R + 1024], KD), KD, 512, "fourier_ready", sum(four[:l + 1]))
                load(l, L_V, rows(w_in[l, :, C_R + 1024:C_R + 1536], KD), KD, 512, "values_ready", 4 * (l + 1))
                load(l, L_WAG, rows(w_in[l, :, C_R + 1536:C_R + 1792], KD), KD, 256, "rin_ready", RT * l + 4)
                load(l, L_LORA, lora[l].rearrange("p (k n) -> p k n", k=1), 1, 1536, "rin_ready", RT * l + 8)

                def gate(b, g):
                    return rows(w_in[l, :, bass.ds(C_G + b * D + g * 512, 512)], KD), KD, 512

                def proj(b, g):
                    return rows((w_a, w_b, w_c)[b][l, :, bass.ds(g * 512, 512)], 4), 4, 512
                if l == 0:
                    sp.wait_ge(sem("constants_set"), 4)
                    for at in range(0, D, ZEROS):
                        sp.dma_start(xg[:, at:at + ZEROS].rearrange("(n p) c -> p n c", p=P),
                                     zeros.unsqueeze(1).broadcast_to([P, NTAB + 1, ZEROS])).then_inc(sem("rows_zeroed"), 16)
                load(l, L_MERGE, *gate(0, 0), "scan_over", l + 1)
                load(l, L_MERGE + 1, *proj(0, 0))
                load(l, L_MERGE + 2, *gate(1, 0), "post_over", l + 1)
                load(l, L_MERGE + 3, *proj(1, 0), "merge_gate", 24 * l + 4)
                load(l, L_MERGE + 4, *gate(2, 0), "merge_proj", 24 * l + 4)
                load(l, L_MERGE + 5, *proj(2, 0), "merge_gate", 24 * l + 8)
                load(l, L_MERGE + 6, *gate(0, 1), "merge_proj", 24 * l + 8)
                load(l, L_MERGE + 7, *proj(0, 1), "merge_gate", 24 * l + 12)
                load(l, L_MERGE + 8, *gate(1, 1), "merge_proj", 24 * l + 12)
                load(l, L_MERGE + 9, *proj(1, 1), "merge_gate", 24 * l + 16)
                load(l, L_MERGE + 10, *gate(2, 1), "merge_proj", 24 * l + 16)
                load(l, L_MERGE + 11, *proj(2, 1), "merge_gate", 24 * l + 20)
                for g, reader in enumerate((("merge_proj", 24 * l + 20), ("merge_gate", 24 * l + 24))):
                    load(l, L_OUT + g, rows(w_out[l, :, g * 512:g * 512 + 512], KD), KD, 512, *reader)
                load(l, L_EXP, rows(sg[l], KD), KD, 512, "merge_proj", 24 * l + 24)
                load(l, L_EXP + 1, rows(su[l], KD), KD, 512, "out_ready", KD * l + 4)
                load(l, L_EXP + 2, rows(sd[l], FK), FK, 1024, "out_ready", KD * l + 8)
                sp.wait_ge(sem("route_ready"), l + 1)
                sp.wait_ge(sem("rows_placed"), 16 * sum(2 * n for n in nqt[:l + 1]))

                def token_rows(j, b):
                    sp.dma_start(XG[:, b, :], xg[bass.ds(j * P, P), :]).then_inc(sem(f"rows_loaded{b}"), 16)

                token_rows(0, 0)
                sp.wait_ge(sem("up_ready"), FK * (l + 1))
                pairs = pair_count(sp, l)
                with sp.Fori(0, pairs) as i:
                    it = pairs_before + i
                    for b in range(2):
                        e = sp.value_load(tile_expert[0:1, bass.ds(2 * i + b, 1)], min_val=0, max_val=NE - 1)
                        sp.wait_ge(sem(f"tile_up{b}"), it + 1)
                        for n, src in ((0, eg), (1, eu)):
                            sp.dma_start(sets[b][:, n, :].rearrange("p (k n) -> p k n", k=KD),
                                         rows(src[l, bass.ds(e, 1), :, :].rearrange("e d f -> (e d) f"), KD))\
                                .then_inc(sem(f"tile_loaded{n}{b}"), 16)
                        sp.wait_ge(sem(f"rows_turned{1 - b}"), it + 1 + b + (l if b else 0))
                        token_rows(2 * i + b + 1, 1 - b)
                        if b == 0:
                            sp.wait_ge(sem("down_ready"), KD * (l + 1))
                        sp.wait_ge(sem(f"tile_down{b}"), it + 1)
                        sp.dma_start(sets[b][:, 2, :].rearrange("p (k n) -> p k n", k=FK),
                                     rows(ed[l, bass.ds(e, 1), :, :].rearrange("e f d -> (e f) d"), FK))\
                            .then_inc(sem(f"tile_loaded2{b}"), 16)
                pairs_before = pairs_before + pairs
            sp.wait_ge(sem("result"), 1)
            sp.dma_start(out, H[:, :, 0:SEQ]).then_inc(sem("stored"), 16)
            sp.wait_ge(sem("stored"), 16)

        @block.tensor
        def _(pe):
            mm = nc.tensor.matmul
            pe.wait_ge(sem("params"), 16 * 7)
            pe.wait_ge(sem("csil"), 1)

            def product(bank, w, lhs, rhs, n, M=P):
                for k in range(n):
                    ins = mm(ps[0:M, bank, 0:w], lhs(k), rhs(k), start=(k == 0), stop=(k == n - 1))
                return ins

            def weights(n, w, j):
                return lambda k: slot(n)[:, k * w + j * P:k * w + j * P + P]

            norms = 0

            def sum_squares(w):
                nonlocal norms
                for k in range(KD):
                    pe.wait_ge(sem("squares"), KD * norms + k + 1)
                    ins = mm(ps[:, 0, 0:w], ones, H[:, k, 0:w], start=(k == 0), stop=(k == KD - 1))
                ins.then_inc(sem("sumsq"), 1)
                norms += 1
                handover("pe", pe)

            pairs_before = 0
            for l in range(DEPTH):
                w = width[l]

                with pe.Fori(0, N_ADA // NSLOT) as i:
                    at = N_ADA * l + i * NSLOT

                    def turn(s):
                        wait_apart(pe, "ada_copied", at + s + 1)
                        for q in range(4):
                            ins = pe.transpose(ps[:, 3 + s, 2 * q:2 * q + 2], ROW[0:2, s, q * P:q * P + P],
                                               cons[0:2, CON["ident"]:CON["ident"] + 2])
                        ins.then_inc(sem("ada_cols"), 1)

                    pe.wait_ge(sem("ada_mod"), at + 1)
                    for s in range(NSLOT):
                        loaded(pe, l, s, i)
                        product(s, 512, lambda k: csil[:, k, :], lambda k: slot(s)[:, k * 512:k * 512 + 512], KD, 2)\
                            .then_inc(sem("ada_rows"), 1)
                        if s:
                            turn(s - 1)
                    turn(NSLOT - 1)
                handover("pe", pe)
                if stop == "ada":
                    return
                sum_squares(T)
                if stop == "norm1":
                    return

                o = 10 * l
                for n, cw, tiles in ((L_F, 512, 4), (L_Q, QL, 3), (L_KV, KVL + ROPE, 3)):
                    loaded(pe, l, n)
                    ww = T if n == L_KV else w
                    for j in range(tiles):
                        b = o - 10 * l
                        if b >= 8:
                            pe.wait_ge(sem("ina_copied"), o - 7)
                        if n == L_KV and j == 2:
                            ins = product(b % 8, ww, lambda k: slot(n)[:, k * cw + KVL - NOPE:k * cw + KVL + ROPE],
                                          lambda k: H[:, k, 0:ww], KD, QK)
                        else:
                            ins = product(b % 8, ww, weights(n, cw, j), lambda k: H[:, k, 0:ww], KD)
                        ins.then_inc(sem("ina_ready"), 1)
                        o += 1
                handover("pe", pe)
                if stop == "ina":
                    return

                loaded(pe, l, L_DFT)
                units = [(g, q) for g in range(FG) for q in range(four[l] // FG)]
                base = sum(four[:l])

                def over_tokens(u):
                    pe.wait_ge(sem("fourier_mid"), base + u + 1)
                    if u >= 2:
                        pe.wait_ge(sem("fourier_out"), base + u - 1)
                    for n in range(4):
                        c, t = n // 2, n % 2
                        ins = mm(ps[:, 2 + u % 2, 0:SEQ], FA[:, u % 2, t * 256 + c * FGD:t * 256 + c * FGD + FGD],
                                 slot(L_DFT)[:, 256 + n * SEQ:256 + n * SEQ + SEQ], start=(n == 0), stop=(n == 3))
                    ins.then_inc(sem("fourier_ready"), 1)

                for u, (g, q) in enumerate(units):
                    if u >= 2:
                        pe.wait_ge(sem("fourier_mid"), base + u - 1)
                    for t in range(2):
                        ins = mm(ps[:, u % 2, t * 256:t * 256 + 256], FZ[:, g, q * SEQ + t * P:q * SEQ + t * P + P],
                                 slot(L_DFT)[:, 0:256], start=True, stop=True)
                    ins.then_inc(sem("fourier_first"), 1)
                    if u:
                        over_tokens(u - 1)
                over_tokens(len(units) - 1)
                handover("pe", pe)
                if stop == "fourier":
                    return

                pe.wait_ge(sem("lora_squares"), 5 * l + 3)
                product(0, w, lambda k: ones, lambda k: SQ[:, k, 0:w], 3).then_inc(sem("lora_sums"), 1)
                pe.wait_ge(sem("lora_squares"), 5 * l + 5)
                product(1, T, lambda k: ones, lambda k: SQ[:, 3 + k, :], 2).then_inc(sem("lora_sums"), 1)
                mm(ps[0:QK, 2, 0:SEQ], rot[0:QK, :], KR[0:QK, 0, 0:SEQ], start=True, stop=True)\
                    .then_inc(sem("key_turned"), 1)
                pe.wait_ge(sem("lora_normed"), l + 1)
                loaded(pe, l, L_UKV)
                for t in range(T // P):
                    vals = [slot(L_UKV)[:, k * 1024:k * 1024 + 1024].rearrange("p (h n) -> p h n", n=NOPE + VD)[:, :, NOPE:]
                            for k in range(2)]
                    product(4 + t, HEADS * VD, lambda k: CKV[:, k, t * P:t * P + P], lambda k: vals[k], 2)\
                        .then_inc(sem("values_ready"), 1)
                handover("pe", pe)
                if stop == "lora":
                    return

                n_q = nqt[l]
                with pe.Fori(0, HEADS // 2) as i:
                    for b in range(2):
                        h = l * HEADS + 2 * i + b
                        qbase = HEADS * sum(nqt[:l]) + (2 * i + b) * n_q
                        pe.wait_ge(sem(f"headw_loaded{b}"), 16 * (l * (HEADS // 2) + i + 1))
                        product(0, w, lambda k: WH[:, b, k * QK:k * QK + QK], lambda k: CQ[:, k, 0:w], 3, QK)
                        product(1, T, lambda k: WH[:, b, 3 * QK + k * NOPE:3 * QK + k * NOPE + NOPE],
                                lambda k: CKV[:, k, :], 2, NOPE).then_inc(sem(f"heads_made{b}"), 1)
                        pe.wait_ge(sem("heads_copied"), 2 * h + 2)
                        mm(ps[0:QK, 2, 0:SEQ], rot[0:QK, :], Qh[0:QK, b, 0:SEQ], start=True, stop=True)\
                            .then_inc(sem("query_turned"), 1)
                        pe.wait_ge(sem("query_done"), h + 1)

                        def keys(q):
                            return (0, T) if q < SEQ // P else (SEQ, T)

                        def scores(q):
                            k0, k1 = keys(q)
                            mm(ps[:, 3 + q % 2, k0:k1], Qh[0:QK, b, q * P:q * P + P], Kh[0:QK, b, k0:k1],
                               start=True, stop=True).then_inc(sem("scores_ready"), 1)

                        def values(q):
                            pe.wait_ge(sem("probs_copied"), qbase + q + 1)
                            if q == 0:
                                pe.wait_ge(sem("heads_out"), h + 1)
                            first = keys(q)[0] // P
                            for c in range(first, T // P):
                                ins = mm(ps[b * VD:b * VD + VD, 7, q * P:q * P + P],
                                         Vh[:, b, c * VD:c * VD + VD], PT[:, q % 2, c * P:c * P + P],
                                         start=(c == first), stop=(c == T // P - 1))
                            if q == n_q - 1:
                                ins.then_inc(sem("attention_ready"), 1)

                        scores(0)
                        for q in range(n_q):
                            if q + 1 < n_q:
                                scores(q + 1)
                            pe.wait_ge(sem("probs_ready"), qbase + q + 1)
                            for c in range(keys(q)[0] // P, T // P):
                                ins = pe.transpose(ps[:, 5 + q % 2, c * P:c * P + P], Pb[:, q % 2, c * P:c * P + P], ident)
                            ins.then_inc(sem("probs_turned"), 1)
                            if q:
                                values(q - 1)
                        values(n_q - 1)
                handover("pe", pe)
                if stop == "attn":
                    return

                for o in range(RT):
                    n, j = L_R + o // 4, o % 4
                    if j == 0:
                        loaded(pe, l, n)
                    if o >= 8:
                        pe.wait_ge(sem("rin_copied"), RT * l + o - 7)
                    product(o % 8, T, weights(n, 256 if n == L_WAG else 512, j), lambda k: H[:, k, :], KD)\
                        .then_inc(sem("rin_ready"), 1)
                handover("pe", pe)
                if stop == "rin":
                    return

                for j in range(RJ):
                    pe.wait_ge(sem("key_squares"), RJ * l + j + 1)
                    mm(ps[:, j, :], hsum, B[0][:, j, :], start=True, stop=True).then_inc(sem("key_sums"), 1)
                loaded(pe, l, L_LORA)
                pe.wait_ge(sem("decay_input"), l + 1)
                for u in range(2 * RJ):
                    j, d = u // 2, u % 2
                    for half in range(2):
                        if 2 * u + half >= 4:
                            pe.wait_ge(sem("lora_gates"), 16 * l + 2 * u + half - 3)
                        r = slice(64 * half, 64 * half + 64)
                        mm(ps[:, 4 + (2 * u + half) % 4, :], slot(L_LORA)[r, d * RD + j * P:d * RD + j * P + P], WA[r, 0, :],
                           start=True, stop=True).then_inc(sem("lora_up"), 1)
                handover("pe", pe)
                if stop == "pre":
                    return

                for s in range(2):
                    with pe.Fori(0, NCH) as c:
                        step = (2 * l + s) * NCH + c

                        def bank(d, n):
                            return ps[:, 4 * d + n, :].rearrange("p (j n) -> p j n", n=P)

                        def pairs(out, *terms):
                            for j in range(RJ):
                                for n, (lhs, rhs) in enumerate(terms):
                                    ins = mm(out[:, j, :], lhs[:, j, :], rhs[:, j, :], start=(n == 0), stop=(n == len(terms) - 1))
                            return ins

                        def turn(d, name):
                            for j in range(RJ):
                                ins = pe.transpose(bank(d, 3)[:, j, :], b_(name, d)[:, j, :], ident)
                            ins.then_inc(sem(f"grams{d}"), 1)

                        b_ = lambda name, d: SB[name][d]
                        for d in range(2):
                            wait_apart(pe, f"scaled{d}", 2 * step + 2)
                            for n, name in enumerate(("bE2", "bKk")):
                                both = ps[:, 4 * d + n, :].rearrange("p (x j n) -> p x j n", x=2, n=CH)
                                for j in range(RJ):
                                    mm(both[:, :, j, :], b_(name, d)[:, j, :], ER[d][:, :, j, :], start=True, stop=True)
                            pairs(bank(d, 2), (b_("bE3", d), b_("bE2", d)))
                            turn(d, "bE2")
                        for n, name in enumerate(("bKk", "bV")):
                            for d in range(2):
                                wait_apart(pe, f"turned{d}", 3 * step + n + 1)
                                turn(d, name)
                        for n in range(len(LEVELS)):
                            last = n == len(LEVELS) - 1
                            for d in range(2):
                                wait_apart(pe, f"blocks{d}", step * (len(LEVELS) + 1) + n + 2)
                                wait_apart(pe, f"inverse{d}", step * (len(LEVELS) + 1) + n + 1)
                                if n == 0:
                                    wait_apart(pe, f"turned{d}", 3 * step + 3)
                                pairs(bank(d, 3), (b_("BT", d), b_("X", d))).then_inc(sem(f"joined{d}"), 1)
                            for d in range(2):
                                wait_apart(pe, f"joined_copied{d}", step * len(LEVELS) + n + 1)
                                if n == 0:
                                    wait_apart(pe, f"masked{d}", step + 1)
                                if not last:
                                    pairs(bank(d, 2), (b_("XT", d), b_("P", d)))
                                pairs(bank(d, 1), (b_("P", d), b_("XT", d))).then_inc(sem(f"grown{d}"), 1)
                        for d in range(2):
                            wait_apart(pe, f"inverse{d}", step * (len(LEVELS) + 1) + len(LEVELS) + 1)
                            wait_apart(pe, f"state{d}", step + l + 1)
                            pairs(bank(d, 3), (b_("bE3", d), b_("S", d)), (b_("Gak", d), b_("Vt", d))).then_inc(sem(f"rhs{d}"), 1)
                        for d in range(2):
                            wait_apart(pe, f"rhs_copied{d}", step + 1)
                            pairs(bank(d, 3), (b_("XT", d), b_("RHS", d))).then_inc(sem(f"u{d}"), 1)
                        for d in range(2):
                            wait_apart(pe, f"u_copied{d}", step + 1)
                            if s or l < DEPTH - 1:
                                y = ps[:, 4 * d, 0:RJ * CH].rearrange("p (j n) -> p j n", n=CH)
                                pairs(y, (b_("S", d), b_("Rq", d)), (b_("U", d), b_("Grb", d)), (b_("Vt", d), b_("Grk", d)))
                            pairs(bank(d, 2), (b_("Bt", d), b_("U", d)), (b_("Kt", d), b_("Vt", d)))\
                                .then_inc(sem(f"step{d}"), 1)
                handover("pe", pe)
                if stop == "scan":
                    return

                for j in range(RJ):
                    pe.wait_ge(sem("bonus_input"), RJ * l + j + 1)
                    mm(ps[:, 4 * (j % 2), :], hsum, TS[:, 0, :], start=True, stop=True)
                    mm(ps[:, 4 * (j % 2) + 1, :], hsum, Y[:, j, :], start=True, stop=True)
                    mm(ps[:, 4 * (j % 2) + 2, :], slot(L_LORA)[:, 1024 + j * P:1024 + j * P + P], GX[:, 0, :],
                       start=True, stop=True).then_inc(sem("head_sums"), 1)
                    pe.wait_ge(sem("centred_squares"), RJ * l + j + 1)
                    mm(ps[:, 4 * (j % 2) + 3, :], hsum, TS[:, 1, :], start=True, stop=True).then_inc(sem("head_vars"), 1)
                handover("pe", pe)
                if stop == "post":
                    return

                o = 24 * l
                for g in range(2):
                    for b, branch in enumerate((FO, AO, Y)):
                        n = L_MERGE + 6 * g + 2 * b
                        loaded(pe, l, n)
                        loaded(pe, l, n + 1)
                        for j in range(4):
                            if o - 24 * l >= 4:
                                pe.wait_ge(sem("merged"), o - 3)
                            product(2 * (o % 4), w, weights(n, 512, j), lambda k: H[:, k, 0:w], KD)\
                                .then_inc(sem("merge_gate"), 1)
                            product(2 * (o % 4) + 1, w, weights(n + 1, 512, j), lambda k: branch[:, k, 0:w], 4)\
                                .then_inc(sem("merge_proj"), 1)
                            o += 1
                handover("pe", pe)
                if stop == "merge":
                    return
                for j in range(KD):
                    if j % 4 == 0:
                        loaded(pe, l, L_OUT + j // 4)
                    product(j, w, weights(L_OUT + j // 4, 512, j % 4), lambda k: M[:, k, 0:w], KD)\
                        .then_inc(sem("out_ready"), 1)
                handover("pe", pe)
                sum_squares(w)
                if stop == "norm2":
                    return

                nt = w // P
                for t in range(nt):
                    for k in range(KD):
                        ins = mm(ps[:, 7, t * NE:t * NE + NE], H[:, k, t * P:t * P + P], rws[:, k, :],
                                 start=(k == 0), stop=(k == KD - 1))
                ins.then_inc(sem("router_ready"), 1)
                for t in range(nt):
                    at = sum(nqt[:l]) + t
                    if t >= 2:
                        pe.wait_ge(sem("tokens_copied"), 2 * (at - 1))
                    for k in range(KD):
                        ins = pe.transpose(ps[:, 2 * (t % 2) + k // 4, (k % 4) * P:(k % 4) * P + P],
                                           H[:, k, t * P:t * P + P], ident)
                    ins.then_inc(sem("tokens_turned"), 1)
                pe.wait_ge(sem("tokens_copied"), 2 * sum(nqt[:l + 1]))

                loaded(pe, l, L_EXP)
                loaded(pe, l, L_EXP + 1)
                for j in range(FK):
                    if j >= 2:
                        pe.wait_ge(sem("hidden_ready"), FK * l + j - 1)
                    product(2 * (j % 2), w, weights(L_EXP, 512, j), lambda k: H[:, k, 0:w], KD)\
                        .then_inc(sem("gate_ready"), 1)
                    product(2 * (j % 2) + 1, w, weights(L_EXP + 1, 512, j), lambda k: H[:, k, 0:w], KD)\
                        .then_inc(sem("up_ready"), 1)
                pe.wait_ge(sem("chosen"), l + 1)
                for t in range(nt):
                    for q in range(t + 1):
                        mm(ps[:, 7, t * NE:t * NE + NE], cons[:, CON["before"]:CON["before"] + P] if q == t else ones,
                           rt[2][:, q * NE:q * NE + NE], start=(q == 0), stop=(q == t))
                for t in range(nt):
                    ins = mm(ps[:, 7, 128:128 + NE], ones, rt[2][:, t * NE:t * NE + NE], start=(t == 0), stop=(t == nt - 1))
                ins.then_inc(sem("ranked"), 1)
                loaded(pe, l, L_EXP + 2)
                pe.wait_ge(sem("hidden_ready"), FK * (l + 1))
                for j in range(KD):
                    if j >= 3:
                        pe.wait_ge(sem("down_added"), KD * l + j - 2)
                    product(4 + j % 3, w, weights(L_EXP + 2, 1024, j), lambda k: HS[:, k, 0:w], FK)\
                        .then_inc(sem("down_ready"), 1)
                pe.wait_ge(sem("down_added"), KD * (l + 1))

                def turn_rows(b):
                    for k in range(KD):
                        ins = pe.transpose(ps[:, k // 4, (k % 4) * P:(k % 4) * P + P], XG[:, b, k * P:k * P + P], ident)
                    return ins.then_inc(sem(f"rows_turned{b}"), 1)

                pe.wait_ge(sem("route_ready"), l + 1)
                pairs = pair_count(pe, l)
                pe.wait_ge(sem("rows_loaded0"), 16 * (pairs_before + l + 1))
                turn_rows(0)
                with pe.Fori(0, pairs) as i:
                    it = pairs_before + i
                    for b in range(2):
                        jt = 2 * it + b
                        pe.wait_ge(sem("rows_copied"), 2 * jt + 2 * l + 2)
                        pe.wait_ge(sem(f"tile_loaded0{b}"), 16 * (it + 1))
                        pe.wait_ge(sem(f"tile_loaded1{b}"), 16 * (it + 1))
                        for k in range(KD):
                            g_ = mm(ps[:, 2, :], XGT[:, k, :], sets[b][:, 0, k * 512:k * 512 + 512],
                                    start=(k == 0), stop=(k == KD - 1))
                            u_ = mm(ps[:, 3, :], XGT[:, k, :], sets[b][:, 1, k * 512:k * 512 + 512],
                                    start=(k == 0), stop=(k == KD - 1))
                        g_.then_inc(sem("tile_gate"), 1)
                        u_.then_inc(sem(f"tile_up{b}"), 1)
                        pe.wait_ge(sem(f"rows_loaded{1 - b}"), 16 * (it + 1 + b + (l if b else 0)))
                        turn_rows(1 - b)
                        pe.wait_ge(sem("tile_hidden"), jt + 1)
                        for k in range(FK):
                            ins = pe.transpose(ps[:, 4, k * P:k * P + P], HID[:, 0, k * P:k * P + P], ident)
                        ins.then_inc(sem("hidden_turned"), 1)
                        pe.wait_ge(sem("hidden_copied"), jt + 1)
                        pe.wait_ge(sem(f"tile_loaded2{b}"), 16 * (it + 1))
                        pe.wait_ge(sem("result_copied"), 2 * jt + 2)
                        for half in range(2):
                            for k in range(FK):
                                ins = mm(ps[:, 5 + half, :], HIDT[:, 0, k * P:k * P + P],
                                         sets[b][:, 2, k * D + half * 512:k * D + half * 512 + 512],
                                         start=(k == 0), stop=(k == FK - 1))
                            ins.then_inc(sem("tile_half") if half == 0 else sem(f"tile_down{b}"), 1)
                for t in range(nt):
                    pe.wait_ge(sem("choices_summed"), sum(nqt[:l]) + t + 1)
                    for k in range(KD):
                        ins = pe.transpose(ps[:, 2 * (t % 4) + k // 4, (k % 4) * P:(k % 4) * P + P],
                                           YT[:, 2 * (t % 2), k * P:k * P + P], ident)
                    ins.then_inc(sem("choices_turned"), 1)
                handover("pe", pe)
                pairs_before = pairs_before + pairs
                if stop == "moe":
                    return
            sum_squares(SEQ)

        @block.scalar
        def _(act):
            link = Chain(act, "act_order")

            def rsqrt(out, x, n, eps):
                link(act.activation(out, x, ACT.Ln, bias=epst[:, eps:eps + 1], scale=1.0 / n))
                return act.activation(out, out, ACT.Exp, scale=-0.5)

            norms = 0

            def norm(w):
                nonlocal norms
                for k in range(KD):
                    act.activation(H[:, k, 0:w], X[:, k, 0:w], ACT.Square).then_inc(sem("squares"), 1)
                norms += 1
                act.wait_ge(sem("sumsq"), norms)
                rsqrt(RS[:, 0, 0:w], ps[:, 0, 0:w], D, 0).then_inc(sem("rstd"), 1)
                handover("act", act, act.copy(dummy[:, 1:2], epst[:, 0:1]))

            act.wait_ge(sem("params"), 16 * 7)
            act.wait_ge(sem("constants_set"), 4)
            act.activation(csil[:], csil[:], ACT.Silu).then_inc(sem("csil"), 1)
            act.preload_act_table_set("natural_log_exp_and_others")

            pairs_before = 0
            for l in range(DEPTH):
                w = width[l]
                handover("act", act, act.copy(dummy[:, 1:2], epst[:, 0:1]))
                if stop == "ada":
                    return
                norm(T)
                if stop == "norm1":
                    return

                dst = [FZ[:, j, 0:w] for j in range(4)] + [CQ[:, j, 0:w] for j in range(3)] + \
                      [CKV[:, j, :] for j in range(2)] + [KR[0:QK, 0, :]]
                for o, out_ in enumerate(dst):
                    act.wait_ge(sem("ina_ready"), 10 * l + o + 1)
                    act.copy(out_, ps[0:out_.shape[0], o % 8, 0:out_.shape[1]]).then_inc(sem("ina_copied"), 1)
                handover("act", act, act.copy(dummy[:, 1:2], epst[:, 0:1]))
                if stop == "ina":
                    return

                base = sum(four[:l])
                for u, (g, q) in enumerate((g, q) for g in range(FG) for q in range(four[l] // FG)):
                    act.wait_ge(sem("fourier_ready"), base + u + 1)
                    act.copy(FO[:, g, q * SEQ:q * SEQ + SEQ], ps[:, 2 + u % 2, 0:SEQ]).then_inc(sem("fourier_out"), 1)
                handover("act", act, act.copy(dummy[:, 1:2], epst[:, 0:1]))
                if stop == "fourier":
                    return

                for k in range(3):
                    act.activation(SQ[:, k, 0:w], CQ[:, k, 0:w], ACT.Square).then_inc(sem("lora_squares"), 1)
                for k in range(2):
                    act.activation(SQ[:, 3 + k, :], CKV[:, k, :], ACT.Square).then_inc(sem("lora_squares"), 1)
                act.wait_ge(sem("lora_sums"), 2 * l + 1)
                rsqrt(RQ[:, 0, 0:w], ps[:, 0, 0:w], QL, 0).then_inc(sem("lora_rstd"), 1)
                act.wait_ge(sem("lora_sums"), 2 * l + 2)
                rsqrt(RQ[:, 1, :], ps[:, 1, :], KVL, 0).then_inc(sem("lora_rstd"), 1)
                for t in range(T // P):
                    act.wait_ge(sem("values_ready"), 4 * l + t + 1)
                    act.copy(VT[:, t, :], ps[:, 4 + t, :])
                handover("act", act, act.copy(dummy[:, 1:2], epst[:, 0:1]))
                if stop == "lora":
                    return

                n_q = nqt[l]
                with act.Fori(0, HEADS // 2) as i:
                    for b in range(2):
                        h = l * HEADS + 2 * i + b
                        qbase = HEADS * sum(nqt[:l]) + (2 * i + b) * n_q
                        act.wait_ge(sem(f"heads_made{b}"), l * (HEADS // 2) + i + 1)
                        act.copy(Qh[0:QK, b, 0:w], ps[0:QK, 0, 0:w]).then_inc(sem("heads_copied"), 1)
                        act.copy(Kh[0:NOPE, b, :], ps[0:NOPE, 1, :]).then_inc(sem("heads_copied"), 1)

                        def exps(q):
                            k0 = 0 if q < SEQ // P else SEQ
                            act.wait_ge(sem("probs_max"), qbase + q + 1)
                            if q >= 2:
                                act.wait_ge(sem("probs_turned"), qbase + q - 1)
                            act.activation(Pb[:, q % 2, k0:T], ps[:, 3 + q % 2, k0:T], ACT.Exp, scale=SCALE,
                                           bias=small[:, 2 + q % 2:3 + q % 2],
                                           accum_out=small[:, 4 + q % 2:5 + q % 2]).then_inc(sem("probs_exp"), 1)

                        exps(0)
                        for q in range(n_q):
                            if q + 1 < n_q:
                                exps(q + 1)
                            k0 = 0 if q < SEQ // P else SEQ
                            act.wait_ge(sem("probs_turned"), qbase + q + 1)
                            act.copy(PT[:, q % 2, k0:T], ps[:, 5 + q % 2, k0:T]).then_inc(sem("probs_copied"), 1)
                handover("act", act, act.copy(dummy[:, 1:2], epst[:, 0:1]))
                if stop == "attn":
                    return

                for o in range(RT):
                    act.wait_ge(sem("rin_ready"), RT * l + o + 1)
                    act.wait_ge(sem("rin_padded"), l + 1)
                    if o >= 2:
                        act.wait_ge(sem("rin_mixed"), RT * l + o - 1)
                    act.copy(PP[:, o % 2, :, 1:SEQ + 1], ps[:, o % 8, :].rearrange("p (s n) -> p s n", s=2))\
                       .then_inc(sem("rin_copied"), 1)
                handover("act", act, act.copy(dummy[:, 1:2], epst[:, 0:1]))
                if stop == "rin":
                    return

                for j in range(RJ):
                    act.wait_ge(sem("key_sums"), RJ * l + j + 1)
                    rsqrt(B[1][:, j, :], ps[:, j, :], 1, 1).then_inc(sem("key_rstd"), 1)
                act.activation(WA[0:64, 0, :], WA[0:64, 0, :], ACT.Tanh).then_inc(sem("decay_input"), 1)
                act.activation(GX[:, 0, :], GX[:, 0, :], ACT.Sigmoid)
                for u in range(2 * RJ):
                    j, d = u // 2, u % 2
                    for half, (out_, v) in enumerate(((LW[d][:, j, :], "w0"), (TS[:, u % 2, :], "a0"))):
                        act.wait_ge(sem("lora_up"), 16 * l + 2 * u + half + 1)
                        if half and u >= 2:
                            act.wait_ge(sem("rates_used"), 8 * l + u - 1)
                        col = VEC[v] + d * RJ + j
                        act.activation(out_, ps[:, 4 + (2 * u + half) % 4, :], ACT.Sigmoid, bias=vecs[:, l, col:col + 1])\
                           .then_inc(sem("lora_gates"), 1)
                act.preload_act_table_set("natural_log_exp_and_others")
                handover("act", act, act.copy(dummy[:, 1:2], epst[:, 0:1]))
                if stop == "pre":
                    return

                for s in range(2):
                    with act.Fori(0, NCH) as c:
                        step = (2 * l + s) * NCH + c
                        flat = lambda name, d: SB[name][d].rearrange("p j n -> p (j n)")
                        turned = lambda d: ps[:, 4 * d + 3, :]
                        for d in range(2):
                            act.wait_ge(sem(f"cumulated{d}"), step + 1)
                            act.activation(flat("E1", d), flat("L", d), ACT.Exp, scale=-DECAY).then_inc(sem(f"exps{d}"), 1)
                            act.activation(flat("E2", d), flat("L", d), ACT.Exp, scale=DECAY).then_inc(sem(f"exps{d}"), 1)
                            act.wait_ge(sem(f"before{d}"), step + 1)
                            act.activation(flat("E3", d), flat("E3", d), ACT.Exp, scale=-DECAY).then_inc(sem(f"exps{d}"), 1)
                        for n, name in enumerate(("Bt", "Kt", "Vt")):
                            for d in range(2):
                                act.wait_ge(sem(f"grams{d}"), 3 * step + n + 1)
                                act.copy(flat(name, d), turned(d)).then_inc(sem(f"turned{d}"), 1)
                        for n in range(len(LEVELS)):
                            for d in range(2):
                                act.wait_ge(sem(f"joined{d}"), step * len(LEVELS) + n + 1)
                                act.copy(flat("P", d), turned(d)).then_inc(sem(f"joined_copied{d}"), 1)
                        for d in range(2):
                            act.wait_ge(sem(f"rhs{d}"), step + 1)
                            act.copy(flat("RHS", d), turned(d)).then_inc(sem(f"rhs_copied{d}"), 1)
                        for d in range(2):
                            act.wait_ge(sem(f"u{d}"), step + 1)
                            act.copy(flat("U", d), turned(d)).then_inc(sem(f"u_copied{d}"), 1)
                handover("act", act, act.copy(dummy[:, 1:2], epst[:, 0:1]))
                if stop == "scan":
                    return

                for j in range(RJ):
                    act.wait_ge(sem("head_vars"), RJ * l + j + 1)
                    rsqrt(B[0][:, j, :], ps[:, 4 * (j % 2) + 3, :], RN, 2).then_inc(sem("head_rstd"), 1)
                handover("act", act, act.copy(dummy[:, 1:2], epst[:, 0:1]))
                if stop == "post":
                    return

                act.preload_act_table_set("sigmoid_and_others")
                for o in range(24 * l, 24 * l + 24):
                    act.wait_ge(sem("merge_gate"), o + 1)
                    if o - 24 * l >= 2:
                        act.wait_ge(sem("merged"), o - 1)
                    act.activation(SG[:, o % 2, 0:w], ps[:, 2 * (o % 4), 0:w], ACT.Sigmoid).then_inc(sem("merge_sigmoid"), 1)
                act.preload_act_table_set("natural_log_exp_and_others")
                handover("act", act, act.copy(dummy[:, 1:2], epst[:, 0:1]))
                if stop == "merge":
                    return
                handover("act", act, act.copy(dummy[:, 1:2], epst[:, 0:1]))
                norm(w)
                if stop == "norm2":
                    return

                nt = w // P
                act.wait_ge(sem("router_ready"), l + 1)
                act.activation(rt[0][:, 0:nt * NE], ps[:, 7, 0:nt * NE], ACT.Sigmoid).then_inc(sem("router_scores"), 1)
                for t in range(nt):
                    at = sum(nqt[:l]) + t
                    act.wait_ge(sem("tokens_turned"), at + 1)
                    for half in range(2):
                        act.copy(MT_[:, t, 512 * half:512 * half + 512], ps[:, 2 * (t % 2) + half, :])\
                           .then_inc(sem("tokens_copied"), 1)
                act.preload_act_table_set("silu_and_others")
                for j in range(FK):
                    act.wait_ge(sem("gate_ready"), FK * l + j + 1)
                    act.activation(HS[:, j, 0:w], ps[:, 2 * (j % 2), 0:w], ACT.Silu).then_inc(sem("gate_silu"), 1)

                def copy_rows(b, count):
                    act.wait_ge(sem(f"rows_turned{b}"), count)
                    act.copy(XGT[:, 0:4, :], ps[:, 0, :].rearrange("p (k n) -> p k n", n=P)).then_inc(sem("rows_copied"), 1)

                act.wait_ge(sem("route_ready"), l + 1)
                pairs = pair_count(act, l)
                copy_rows(0, pairs_before + l + 2)
                with act.Fori(0, pairs) as i:
                    it = pairs_before + i
                    for b in range(2):
                        jt = 2 * it + b
                        act.wait_ge(sem("tile_gate"), jt + 1)
                        act.activation(SIL[:, 0, :], ps[:, 2, :], ACT.Silu).then_inc(sem("tile_silu"), 1)
                        copy_rows(1 - b, it + 2 + b + (l if b else 0))
                        act.wait_ge(sem("hidden_turned"), jt + 1)
                        act.copy(HIDT[:, 0, :], ps[:, 4, :]).then_inc(sem("hidden_copied"), 1)
                        act.wait_ge(sem("tile_half"), jt + 1)
                        act.wait_ge(sem("result_free"), jt + 1)
                        act.copy(YG[:, b, 0:512], ps[:, 5, :]).then_inc(sem("result_copied"), 1)
                act.preload_act_table_set("natural_log_exp_and_others")
                handover("act", act, act.copy(dummy[:, 1:2], epst[:, 0:1]))
                pairs_before = pairs_before + pairs
                if stop == "moe":
                    return
            norm(SEQ)

        @block.vector
        def _(dve):
            link = Chain(dve, "dve_order")
            tt, stt, ts = dve.tensor_tensor, dve.scalar_tensor_tensor, dve.tensor_scalar

            def over():
                handover("dve", dve, dve.memset(dummy[:, 0:1], 0.0))

            norms = 0

            def norm(w, l, n):
                nonlocal norms
                norms += 1
                dve.wait_ge(sem("rstd"), norms)
                for k in range(KD):
                    link(tt(H[:, k, 0:w], X[:, k, 0:w], RS[:, 0, 0:w], ALU.mult))
                    for s in range(w // SEQ):
                        x = H[:, k, s * SEQ:s * SEQ + SEQ]
                        ts(x, x, gsc[:, n, k, s:s + 1], mod[:, 24 * n + k, s:s + 1], ALU.mult, ALU.add)
                over()

            dve.wait_ge(sem("params"), 16 * 7)
            pairs_before = 0
            for l in range(DEPTH):
                w = width[l]

                def vec_(name, j=0, n=1):
                    return vecs[:, l, VEC[name] + j:VEC[name] + j + n]

                with dve.Fori(0, N_ADA // NSLOT) as i:
                    at = N_ADA * l + i * NSLOT

                    def row(s):
                        dve.wait_ge(sem("ada_rows"), at + s + 1)
                        dve.tensor_copy(ROW[0:2, s, :], ps[0:2, s, :]).then_inc(sem("ada_copied"), 1)

                    def cols(s):
                        dve.wait_ge(sem("ada_cols"), at + s + 1)
                        c = (i * NSLOT + s) * 4
                        tt(mod[:, bass.ds(c, 4), :], ps[:, 3 + s, 0:8].rearrange("p (c q) -> p c q", q=2),
                           vecs[:, l, bass.ds(VEC["bada"] + c, 4)].unsqueeze(2).broadcast_to([P, 4, 2]), ALU.add)\
                            .then_inc(sem("ada_mod"), 1)
                    row(0)
                    row(1)
                    cols(0)
                    row(2)
                    cols(1)
                    cols(2)
                dve.wait_ge(sem("ada_mod"), N_ADA * (l + 1) + 1)
                for n, name in enumerate(("n1", "n2")):
                    for s in range(2):
                        stt(gsc[:, n, :, s], mod[:, 24 * n + 8:24 * n + 16, s], 1.0, vec_(name, 0, KD), ALU.add, ALU.mult)
                over()
                if stop == "ada":
                    return
                norm(T, l, 0)
                if stop == "norm1":
                    return
                over()
                if stop == "ina":
                    return

                base = sum(four[:l])
                for u in range(four[l]):
                    dve.wait_ge(sem("fourier_first"), base + u + 1)
                    if u >= 2:
                        dve.wait_ge(sem("fourier_ready"), base + u - 1)
                    dve.tensor_copy(FA[:, u % 2, :], ps[:, u % 2, :]).then_inc(sem("fourier_mid"), 1)
                over()
                if stop == "fourier":
                    return

                rr = slice(NOPE, QK)
                cos, sin = (cons[rr, CON[x]:CON[x] + SEQ] for x in ("cos", "sin"))
                dve.wait_ge(sem("key_turned"), l + 1)
                link(tt(RP[rr, 0, 0:SEQ], ps[rr, 2, 0:SEQ], sin, ALU.mult))
                link(tt(KR[rr, 0, 0:SEQ], KR[rr, 0, 0:SEQ], cos, ALU.mult))
                link(tt(KR[rr, 0, 0:SEQ], KR[rr, 0, 0:SEQ], RP[rr, 0, 0:SEQ], ALU.add))
                for b in range(2):
                    dve.tensor_copy(Kh[rr, b, :], KR[rr, 0, :])
                dve.wait_ge(sem("lora_rstd"), 2 * l + 1)
                for k in range(3):
                    stt(CQ[:, k, 0:w], CQ[:, k, 0:w], vec_("qg", k), RQ[:, 0, 0:w], ALU.mult, ALU.mult)
                dve.wait_ge(sem("lora_rstd"), 2 * l + 2)
                for k in range(2):
                    ins = stt(CKV[:, k, :], CKV[:, k, :], vec_("kvg", k), RQ[:, 1, :], ALU.mult, ALU.mult)
                ins.then_inc(sem("lora_normed"), 1)
                over()
                if stop == "lora":
                    return

                n_q = nqt[l]
                with dve.Fori(0, HEADS // 2) as i:
                    link.loop(i, 2 * (2 + 2 * n_q))
                    for b in range(2):
                        h = l * HEADS + 2 * i + b
                        qbase = HEADS * sum(nqt[:l]) + (2 * i + b) * n_q
                        dve.tensor_copy(Vh[:, b, :].rearrange("p (c n) -> p c n", n=VD),
                                        VT[:, :, bass.ds((2 * i + b) * VD, VD)])
                        dve.wait_ge(sem("query_turned"), h + 1)
                        link(tt(RP[rr, 0, 0:SEQ], ps[rr, 2, 0:SEQ], sin, ALU.mult))
                        link(tt(Qh[rr, b, 0:SEQ], Qh[rr, b, 0:SEQ], cos, ALU.mult))
                        tt(Qh[rr, b, 0:SEQ], Qh[rr, b, 0:SEQ], RP[rr, 0, 0:SEQ], ALU.add).then_inc(sem("query_done"), 1)

                        def largest(q):
                            k0 = 0 if q < SEQ // P else SEQ
                            dve.wait_ge(sem("scores_ready"), qbase + q + 1)
                            link(dve.tensor_reduce(small[:, q % 2:q % 2 + 1], ps[:, 3 + q % 2, k0:T], AX_X, ALU.max))
                            ts(small[:, 2 + q % 2:3 + q % 2], small[:, q % 2:q % 2 + 1], -SCALE, None, ALU.mult)\
                                .then_inc(sem("probs_max"), 1)

                        largest(0)
                        for q in range(n_q):
                            if q + 1 < n_q:
                                largest(q + 1)
                            k0 = 0 if q < SEQ // P else SEQ
                            dve.wait_ge(sem("probs_exp"), qbase + q + 1)
                            link(dve.reciprocal(small[:, 6 + q % 2:7 + q % 2], small[:, 4 + q % 2:5 + q % 2]))
                            ts(Pb[:, q % 2, k0:T], Pb[:, q % 2, k0:T], small[:, 6 + q % 2:7 + q % 2], None, ALU.mult)\
                                .then_inc(sem("probs_ready"), 1)
                        dve.wait_ge(sem("attention_ready"), h + 1)
                        half = slice(b * VD, b * VD + VD)
                        dve.tensor_copy(work[half, bass.ds(2048 + i * T, w)], ps[half, 7, 0:w])\
                           .then_inc(sem("heads_out"), 1)
                link.end(HEADS // 2)
                over()
                if stop == "attn":
                    return

                for o in range(RT):
                    dst = [R, K1, V][o // 4][:, o % 4, :] if o < 12 else (WA, GX)[o - 12][:, 0, :]
                    p = PP[:, o % 2, :, 1:SEQ + 1]
                    t = TS[:, 0, :].rearrange("p (s n) -> p s n", s=2)
                    dve.wait_ge(sem("rin_copied"), RT * l + o + 1)
                    link(tt(t, PP[:, o % 2, :, 0:SEQ], PP[:, o % 2, :, 2:SEQ + 2], ALU.add))
                    link(stt(t, t, 0.5, p, ALU.mult, ALU.subtract))
                    stt(dst.rearrange("p (s n) -> p s n", s=2), t, vec_("mu", o), p, ALU.mult, ALU.add)\
                        .then_inc(sem("rin_mixed"), 1)
                    dve.wait_ge(sem("rin_mixed"), RT * l + o + 1)
                over()
                if stop == "rin":
                    return

                for j in range(RJ):
                    link(ts(KK[:, j, :], K1[:, j, :], vec_("kk", j), None, ALU.mult))
                    tt(B[0][:, j, :], KK[:, j, :], KK[:, j, :], ALU.mult).then_inc(sem("key_squares"), 1)
                for j in range(RJ):
                    dve.wait_ge(sem("key_rstd"), RJ * l + j + 1)
                    link(tt(KK[:, j, :], KK[:, j, :], B[1][:, j, :], ALU.mult))
                for u in range(2 * RJ):
                    j, d = u // 2, u % 2
                    rate = TS[:, u % 2, :]
                    dve.wait_ge(sem("lora_gates"), 16 * l + 2 * u + 2)
                    link(tt(B[d][:, j, :], KK[:, j, :], rate, ALU.mult))
                    link(ts(rate, rate, -1.0, vec_("ka", j), ALU.add, ALU.mult))
                    stt(KDs[d][:, j, :], rate, 1.0, K1[:, j, :], ALU.add, ALU.mult).then_inc(sem("rates_used"), 1)
                link(dve.memset(Y[:, :, :], 0.0))
                for d in range(2):
                    for name in ("bE2", "bKk", "bV", "S"):
                        ins = dve.memset(SB[name][d], 0.0)
                    ins.then_inc(sem(f"state{d}"), 1)
                over()
                if stop == "pre":
                    return

                for s in range(2):
                    with dve.Fori(0, NCH) as c:
                        stream = s == 1 or l < DEPTH - 1
                        link.loop(c, 2 + 2 * (1 + 1 + len(LEVELS) - 1 + 1 + stream))
                        step = (2 * l + s) * NCH + c
                        flat = lambda name, d: SB[name][d].rearrange("p j n -> p (j n)")
                        bank = lambda d, n: ps[:, 4 * d + n, :].rearrange("p (j n) -> p j n", n=P)
                        half = lambda d, n, x: ps[:, 4 * d + n, 256 * x:256 * x + 256].rearrange("p (j n) -> p j n", n=CH)
                        b_ = lambda name, d: SB[name][d]
                        at = [(1 - s) * SEQ + c * CH, (1 - s) * SEQ + (NCH - 1) * CH - c * CH]
                        for d in range(2):
                            dve.wait_ge(sem(f"decays{d}"), step + 1)
                            if d == 0:
                                dve.tensor_tensor_scan(flat("L", 0), con_("reset", RJ * CH), flat("lw", 0), 0.0,
                                                       ALU.mult, ALU.add).then_inc(sem("cumulated0"), 1)
                            else:
                                link(dve.tensor_tensor_scan(flat("E1", 1), con_("reset", RJ * CH), flat("lw", 1), 0.0,
                                                            ALU.mult, ALU.add))
                                link(tt(b_("E3", 1), b_("lw", 1), b_("E1", 1), ALU.subtract))
                                tt(b_("L", 1), b_("E3", 1), b_("E1", 1)[:, :, CH - 1:CH].broadcast_to([P, RJ, CH]), ALU.add)\
                                    .then_inc(sem("cumulated1"), 1)
                        for d in range(2):
                            cols = bass.ds(at[d], CH)
                            wait_apart(dve, f"exps{d}", 3 * step + 3)
                            link(tt(b_("E3", d), KK[:, :, cols], b_("E3", d), ALU.mult))
                            for h in range(2):
                                hh = slice(64 * h, 64 * h + 64)
                                tt(blocks(b_("bKk", d))[hh, :, h, :], KDs[d][hh, :, cols], b_("E2", d)[hh], ALU.mult)
                                tt(blocks(b_("bE2", d))[hh, :, h, :], B[d][hh, :, cols], b_("E2", d)[hh], ALU.mult)
                            tt(blocks(b_("bE3", d)), both_heads(b_("E3", d)), blocks_mask("same"), ALU.mult)\
                                .then_inc(sem(f"scaled{d}"), 1)
                        for d in range(2):
                            dve.wait_ge(sem(f"grams{d}"), 3 * step + 1)
                            tt(b_("MT", d), half(d, 0, 0), over_pairs(con_(f"minus{d}")), ALU.mult).then_inc(sem(f"coupling{d}"), 1)
                            link(tt(b_("X", d), bank(d, 2), over_pairs(con_(f"pair{d}", P)), ALU.mult))
                            tt(b_("X", d), b_("X", d), over_pairs(ident), ALU.add).then_inc(sem(f"inverse{d}"), 1)
                        for d in range(2):
                            tt(b_("Grb", d), half(d, 0, 1), over_pairs(con_(f"incl{d}")), ALU.mult)
                            dve.wait_ge(sem(f"grams{d}"), 3 * step + 2)
                            tt(blocks(b_("Gak", d)), both_heads(half(d, 1, 0)), blocks_mask(f"before{d}"), ALU.mult)
                            tt(b_("Grk", d), half(d, 1, 1), over_pairs(con_(f"incl{d}")), ALU.mult).then_inc(sem(f"masked{d}"), 1)
                        for n in range(len(LEVELS)):
                            for d in range(2):
                                dve.wait_ge(sem(f"grown{d}"), step * len(LEVELS) + n + 1)
                                if n < len(LEVELS) - 1:
                                    link(tt(b_("X", d), b_("X", d), bank(d, 2), ALU.add))
                                tt(b_("XT", d), b_("XT", d), bank(d, 1), ALU.add).then_inc(sem(f"inverse{d}"), 1)
                        for d in range(2):
                            cols = bass.ds(at[d], CH)
                            end = CH - 1 if d == 0 else 0
                            wait_apart(dve, f"step{d}", step + 2)
                            if stream:
                                link(tt(Y[:, :, cols], Y[:, :, cols], half(d, 0, 0), ALU.add))
                            link(tt(b_("S", d), b_("S", d), bank(d, 2), ALU.add))
                            tt(b_("S", d), b_("S", d), b_("E1", d)[:, :, end:end + 1].broadcast_to([P, RJ, P]), ALU.mult)\
                                .then_inc(sem(f"state{d}"), 1)
                            dve.wait_ge(sem(f"state{d}"), step + l + 2)
                    link.end(NCH)
                over()
                if stop == "scan":
                    return

                for j in range(RJ):
                    bank = 4 * (j % 2)
                    link(tt(B[0][:, j, :], KDs[0][:, j, :], KDs[1][:, j, :], ALU.add))
                    stt(TS[:, 0, :], R[:, j, :], vec_("rk", j), B[0][:, j, :], ALU.mult, ALU.mult)\
                        .then_inc(sem("bonus_input"), 1)
                    dve.wait_ge(sem("head_sums"), RJ * l + j + 1)
                    y = KK[:, j, :]
                    link(stt(y, ps[:, bank + 1, :], -1.0 / RN, Y[:, j, :], ALU.mult, ALU.add))
                    tt(TS[:, 1, :], y, y, ALU.mult).then_inc(sem("centred_squares"), 1)
                    link(tt(B[1][:, j, :], ps[:, bank, :], V[:, j, :], ALU.mult))
                    dve.wait_ge(sem("head_rstd"), RJ * l + j + 1)
                    link(tt(y, y, B[0][:, j, :], ALU.mult))
                    link(ts(y, y, vec_("gng", j), vec_("gnb", j), ALU.mult, ALU.add))
                    link(tt(y, y, B[1][:, j, :], ALU.add))
                    link(tt(Y[:, j, :], y, ps[:, bank + 2, :], ALU.mult))
                over()
                if stop == "post":
                    return

                o = 24 * l
                for g in range(2):
                    for b in range(3):
                        for j in range(4):
                            dve.wait_ge(sem("merge_sigmoid"), o + 1)
                            dve.wait_ge(sem("merge_proj"), o + 1)
                            m = M[:, 4 * g + j, 0:w]
                            gate, proj = SG[:, o % 2, 0:w], ps[:, 2 * (o % 4) + 1, 0:w]
                            if b == 0:
                                tt(m, gate, proj, ALU.mult).then_inc(sem("merged"), 1)
                            else:
                                link(tt(TM[:, 0, 0:w], gate, proj, ALU.mult))
                                tt(m, m, TM[:, 0, 0:w], ALU.add).then_inc(sem("merged"), 1)
                                dve.wait_ge(sem("merged"), o + 1)
                            o += 1
                over()
                if stop == "merge":
                    return
                for j in range(KD):
                    dve.wait_ge(sem("out_ready"), KD * l + j + 1)
                    for s in range(w // SEQ):
                        x = X[:, j, s * SEQ:s * SEQ + SEQ]
                        stt(x, ps[:, j, s * SEQ:s * SEQ + SEQ], mod[:, 16 + j, s:s + 1], x, ALU.mult, ALU.add)
                over()
                norm(w, l, 1)
                if stop == "norm2":
                    return

                nt = w // P
                v3 = lambda x, n, q: x[:, 0:n * q].rearrange("p (n q) -> p n q", q=q)
                wide = lambda x, n, q: x[:, 0:n].unsqueeze(2).broadcast_to([P, n, q])
                prio = cons[:, CON["prio"]:CON["prio"] + NE]
                ng = nt * NG
                dve.wait_ge(sem("router_scores"), l + 1)
                sel = v3(rt[1], nt, NE)
                link(tt(sel, v3(rt[0], nt, NE), rbs[:, :].unsqueeze(1).broadcast_to([P, nt, NE]), ALU.add))
                x4, pr = v3(rt[1], ng, EPG), v3(rt[2], ng, 6)
                tt(pr[:, :, 0:3], x4[:, :, 0:3], x4[:, :, 1:4], ALU.add)
                tt(pr[:, :, 3:5], x4[:, :, 0:2], x4[:, :, 2:4], ALU.add)
                link(tt(pr[:, :, 5:6], x4[:, :, 0:1], x4[:, :, 3:4], ALU.add))
                link(dve.tensor_reduce(rt[3][:, 0:ng], pr, AX_X, ALU.max))

                def first_largest(out_, x, n, q, pri):
                    link(dve.tensor_reduce(rt[4][:, 0:n], v3(x, n, q), AX_X, ALU.max))
                    link(tt(v3(rt[5], n, q), v3(x, n, q), wide(rt[4], n, q), ALU.is_equal))
                    link(tt(v3(rt[5], n, q), v3(rt[5], n, q), pri.unsqueeze(1).broadcast_to([P, n, q]), ALU.mult))
                    link(dve.tensor_reduce(rt[4][:, 0:n], v3(rt[5], n, q), AX_X, ALU.max))
                    link(tt(v3(out_, n, q), v3(rt[5], n, q), wide(rt[4], n, q), ALU.is_equal))

                first_largest(rt[6], rt[3], nt, NG, prio[:, 0:NG])
                link(ts(rt[7][:, 0:ng], rt[6][:, 0:ng], 1e30, -1e30, ALU.mult, ALU.add))
                link(tt(x4, x4, wide(rt[6], ng, EPG), ALU.mult))
                link(tt(x4, x4, wide(rt[7], ng, EPG), ALU.add))
                first_largest(rt[6], rt[1], nt, NE, prio)
                link(stt(rt[1][:, 0:nt * NE], rt[6][:, 0:nt * NE], -1e35, rt[1][:, 0:nt * NE], ALU.mult, ALU.add))
                first_largest(rt[7], rt[1], nt, NE, prio)
                n16 = nt * NE
                link(tt(rt[2][:, 0:n16], rt[6][:, 0:n16], rt[7][:, 0:n16], ALU.add))
                tt(rt[8][:, 0:n16], rt[2][:, 0:n16], rt[0][:, 0:n16], ALU.mult).then_inc(sem("chosen"), 1)
                dve.wait_ge(sem("chosen"), l + 1)
                link(dve.tensor_reduce(rt[4][:, 0:nt], v3(rt[8], nt, NE), AX_X, ALU.add))
                link(dve.reciprocal(rt[3][:, 0:nt], rt[4][:, 0:nt]))
                link(tt(v3(rt[9], nt, NE), v3(rt[8], nt, NE), wide(rt[3], nt, NE), ALU.mult))
                choice = small16[4:6]
                for c in range(2):
                    link(tt(rt[5][:, 0:n16], rt[6 + c][:, 0:n16], rt[9][:, 0:n16], ALU.mult))
                    link(dve.tensor_reduce(choice[c][:, 0:nt], v3(rt[5], nt, NE), AX_X, ALU.add))

                for j in range(FK):
                    dve.wait_ge(sem("gate_silu"), FK * l + j + 1)
                    dve.wait_ge(sem("up_ready"), FK * l + j + 1)
                    tt(HS[:, j, 0:w], HS[:, j, 0:w], ps[:, 2 * (j % 2) + 1, 0:w], ALU.mult).then_inc(sem("hidden_ready"), 1)

                dve.wait_ge(sem("ranked"), l + 1)
                count, tiles, upto, base = small16[0:4]
                link(dve.tensor_copy(count, ps[:, 7, 128:128 + NE]))
                link(ts(tiles, count, 0.0, None, ALU.is_gt))
                for q in range(1, T // P):
                    link(stt(tiles, count, float(q * P), tiles, ALU.is_gt, ALU.add))
                link(dve.tensor_tensor_scan(upto, ones[:, 0:NE], tiles, 0.0, ALU.mult, ALU.add))
                link(tt(base, upto, tiles, ALU.subtract))
                link(ts(base, base, float(P), None, ALU.mult))
                link(tt(v3(rt[3], nt, NE), ps[:, 7, 0:n16].rearrange("p (n q) -> p n q", q=NE),
                        base.unsqueeze(1).broadcast_to([P, nt, NE]), ALU.add))
                for c in range(2):
                    link(tt(rt[5][:, 0:n16], rt[6 + c][:, 0:n16], rt[3][:, 0:n16], ALU.mult))
                    link(dve.tensor_reduce(small16[6 + c][:, 0:nt], v3(rt[5], nt, NE), AX_X, ALU.add))
                    dve.tensor_copy(pos[:, c * nt:c * nt + nt], small16[6 + c][:, 0:nt]).then_inc(sem("placed"), 1)
                tab = TAB.rearrange("p (n e) -> p n e", e=NE)
                link(tt(tab, upto.unsqueeze(1).broadcast_to([P, NTAB, NE]),
                        cons[:, CON["iota"]:CON["iota"] + NTAB].unsqueeze(2).broadcast_to([P, NTAB, NE]), ALU.is_le))
                link(dve.tensor_reduce(rt[4][:, 0:NTAB], tab, AX_X, ALU.add))
                link(ts(rt[4][:, 0:NTAB], rt[4][:, 0:NTAB], float(NE - 1), None, ALU.min))
                link(dve.tensor_copy(tile_expert[:, :], rt[4][:, 0:NTAB]))
                link(tt(rt[5][:, 0:NTAB // 2], cons[:, CON["iota"]:CON["iota"] + NTAB].rearrange("p (n b) -> p n b", b=2)[:, :, 0],
                        upto[:, NE - 1:NE].broadcast_to([P, NTAB // 2]), ALU.is_lt))
                link(dve.tensor_reduce(rt[5][:, 64:65], rt[5][:, 0:NTAB // 2], AX_X, ALU.add))
                dve.tensor_copy(tile_pairs[:, l:l + 1], rt[5][:, 64:65]).then_inc(sem("route_ready"), 1)
                dve.wait_ge(sem("route_ready"), l + 1)

                for j in range(KD):
                    dve.wait_ge(sem("down_ready"), KD * l + j + 1)
                    for s in range(nt // 2):
                        x = X[:, j, s * SEQ:s * SEQ + SEQ]
                        ins = stt(x, ps[:, 4 + j % 3, s * SEQ:s * SEQ + SEQ], mod[:, 40 + j, s:s + 1], x, ALU.mult, ALU.add)
                    ins.then_inc(sem("down_added"), 1)
                dve.wait_ge(sem("down_added"), KD * (l + 1))

                def copy_rows(b, count):
                    dve.wait_ge(sem(f"rows_turned{b}"), count)
                    dve.tensor_copy(XGT[:, 4:8, :], ps[:, 1, :].rearrange("p (k n) -> p k n", n=P))\
                       .then_inc(sem("rows_copied"), 1)

                pairs = pair_count(dve, l)
                copy_rows(0, pairs_before + l + 2)
                with dve.Fori(0, pairs) as i:
                    it = pairs_before + i
                    for b in range(2):
                        jt = 2 * it + b
                        dve.wait_ge(sem("tile_silu"), jt + 1)
                        dve.wait_ge(sem(f"tile_up{b}"), it + 2)
                        tt(HID[:, 0, :], SIL[:, 0, :], ps[:, 3, :], ALU.mult).then_inc(sem("tile_hidden"), 1)
                        copy_rows(1 - b, it + 2 + b + (l if b else 0))
                        dve.wait_ge(sem(f"tile_down{b}"), it + 2)
                        dve.wait_ge(sem("result_free"), jt + 1)
                        dve.tensor_copy(YG[:, b, 512:1024], ps[:, 6, :]).then_inc(sem("result_copied"), 1)

                for t in range(nt):
                    at = sum(nqt[:l]) + t
                    dve.wait_ge(sem(f"choices_loaded{t % 2}"), 32 * (at // 2 + 1))
                    y1, y2 = YT[:, 2 * (t % 2), :], YT[:, 2 * (t % 2) + 1, :]
                    link(ts(y1, y1, choice[0][:, t:t + 1], None, ALU.mult))
                    stt(y1, y2, choice[1][:, t:t + 1], y1, ALU.mult, ALU.add).then_inc(sem("choices_summed"), 1)
                    dve.wait_ge(sem("choices_turned"), at + 1)
                    for k in range(KD):
                        x = X[:, k, t * P:t * P + P]
                        stt(x, ps[:, 2 * (t % 4) + k // 4, (k % 4) * P:(k % 4) * P + P], mod[:, 40 + k, t // 2:t // 2 + 1],
                            x, ALU.mult, ALU.add)
                over()
                pairs_before = pairs_before + pairs
                if stop == "moe":
                    return
            dve.wait_ge(sem("rstd"), 2 * DEPTH + 1)
            for k in range(KD):
                ins = stt(H[:, k, 0:SEQ], X[:, k, 0:SEQ], fngs[:, k:k + 1], RS[:, 0, 0:SEQ], ALU.mult, ALU.mult)
            ins.then_inc(sem("result"), 1)
            over()

        @block.gpsimd
        def _(pool):
            tt = pool.tensor_tensor
            over = lambda: handover("pool", pool, pool.memset(dummy[:, 2:3], 0.0))
            for n, eps in enumerate((EPS, 1e-12, GN_EPS)):
                pool.memset(epst[:, n:n + 1], eps).then_inc(sem("constants_set"), 1)
            pool.memset(zeros, 0.0).then_inc(sem("constants_set"), 1)
            for n, (name, count) in enumerate((
                    ("ada_mod", 1), ("heads_out", 1), ("step0", 1), ("step1", 1), ("tile_up0", 1), ("tile_up1", 1),
                    ("rows_turned0", 1), ("rows_turned1", 1), ("tile_down0", 1), ("tile_down1", 1), ("result_copied", 2),
                    ("result_free", 2))):
                pool.memset(starts[:, n:n + 1], 0.0).then_inc(sem(name), count)
            pool.wait_ge(sem("params"), 16 * 7)
            pairs_before = 0
            for l in range(DEPTH):
                for stage in ("ada", "norm1", "ina", "fourier", "lora", "attn"):
                    over()
                    if stop == stage:
                        return
                for col in (0, SEQ + 1):
                    ins = pool.memset(PP[:, :, :, col:col + 1], 0.0)
                ins.then_inc(sem("rin_padded"), 1)
                over()
                if stop == "rin":
                    return
                over()
                if stop == "pre":
                    return

                for s in range(2):
                    with pool.Fori(0, NCH) as c:
                        step = (2 * l + s) * NCH + c
                        b_ = lambda name, d: SB[name][d]
                        at = [(1 - s) * SEQ + c * CH, (1 - s) * SEQ + (NCH - 1) * CH - c * CH]
                        for d in range(2):
                            wait_apart(pool, f"step{d}", step + 1)
                            wait_apart(pool, f"state{d}", step + l + 1)
                            pool.tensor_copy(b_("lw", d), LW[d][:, :, bass.ds(at[d], CH)]).then_inc(sem(f"decays{d}"), 1)
                            tt(blocks(b_("bV", d)), both_heads(V[:, :, bass.ds(at[d], CH)]), blocks_mask("heads"), ALU.mult)
                        for d in range(2):
                            pool.wait_ge(sem(f"cumulated{d}"), step + 1)
                            tt(b_("E3", d), b_("L", d), b_("lw", d), ALU.subtract).then_inc(sem(f"before{d}"), 1)
                            wait_apart(pool, f"exps{d}", 3 * step + 1)
                            tt(b_("Rq", d), R[:, :, bass.ds(at[d], CH)], b_("E1", d), ALU.mult).then_inc(sem(f"scaled{d}"), 1)
                        for d in range(2):
                            pool.wait_ge(sem(f"coupling{d}"), step + 1)
                            tt(blocks(b_("XT", d)), both_heads(b_("MT", d)), blocks_mask("lev1"), ALU.mult).then_inc(sem(f"pool_order{d}"), 1)
                            pool.wait_ge(sem(f"pool_order{d}"), step + 1)
                            tt(b_("XT", d), b_("XT", d), over_pairs(ident), ALU.add).then_inc(sem(f"blocks{d}"), 1)
                        for n, b in enumerate(LEVELS):
                            for d in range(2):
                                if n:
                                    pool.wait_ge(sem(f"joined{d}"), step * len(LEVELS) + n)
                                tt(blocks(b_("BT", d)), both_heads(b_("MT", d)), blocks_mask(f"lev{b}"), ALU.mult)\
                                    .then_inc(sem(f"blocks{d}"), 1)
                over()
                pool.memset(dummy[:, 3:4], 0.0).then_inc(sem("scan_over"), 1)
                if stop == "scan":
                    return
                over()
                pool.memset(dummy[:, 3:4], 0.0).then_inc(sem("post_over"), 1)
                if stop == "post":
                    return
                for stage in ("merge", "out", "norm2"):
                    over()
                    if stop == stage:
                        return

                nt = nqt[l]
                pool.wait_ge(sem("rows_zeroed"), 16 * D // ZEROS)
                pool.wait_ge(sem("tokens_copied"), 2 * sum(nqt[:l + 1]))
                for c in range(2):
                    pool.wait_ge(sem("placed"), 2 * l + c + 1)
                    for t in range(nt):
                        pool.indirect_dma_start(xg, bass.IndirectOffsetOnAxis(pos[:, c * nt + t:c * nt + t + 1], 0),
                                                MT_[:, t, :], None).then_inc(sem("rows_placed"), 16)
                pool.wait_ge(sem("route_ready"), l + 1)
                pairs = pair_count(pool, l)
                with pool.Fori(0, pairs) as i:
                    it = pairs_before + i
                    for b in range(2):
                        pool.wait_ge(sem("result_copied"), 4 * it + 2 * b + 4)
                        pool.dma_start(xg[bass.ds((2 * i + b) * P, P), :], YG[:, b, :]).then_inc(sem("result_stored"), 16)
                        pool.wait_ge(sem("result_free"), 2 * it + b + 2)
                        wait_apart(pool, "result_stored", 32 * it + 16 * (b + 1))
                        pool.memset(starts[:, 15:16], 0.0).then_inc(sem("result_free"), 1)
                pool.wait_ge(sem("rows_placed"), 16 * sum(2 * n for n in nqt[:l + 1]))
                for t in range(nt):
                    at = sum(nqt[:l]) + t
                    if t >= 2:
                        pool.wait_ge(sem("choices_turned"), at - 1)
                    for c in range(2):
                        pool.indirect_dma_start(YT[:, 2 * (t % 2) + c, :], None, xg,
                                                bass.IndirectOffsetOnAxis(pos[:, c * nt + t:c * nt + t + 1], 0))\
                            .then_inc(sem(f"choices_loaded{t % 2}"), 16)
                over()
                pairs_before = pairs_before + pairs
                if stop == "moe":
                    return
            over()


def constants():
    con = np.zeros((P, NCON), np.float64)

    def put(name, a):
        con[0:a.shape[0], CON[name]:CON[name] + a.shape[1]] = a

    part = np.arange(P)
    put("ident", np.eye(P))
    put("ones", np.ones((P, P)))
    put("heads", (part[:, None] // RN == part[None] // RN) * 1.0)
    rot = np.zeros((QK, QK))
    half = ROPE // 4
    for axis in range(2):
        for n in range(half):
            first = NOPE + axis * 2 * half + n
            rot[first + half, first] = -1.0
            rot[first, first + half] = 1.0
    put("rot", rot)
    a, b = np.arange(P)[:, None] % CH, np.arange(CH)[None]
    put("minus0", -1.0 * (a < b))
    put("minus1", -1.0 * (a > b))
    put("incl0", a <= b)
    put("incl1", a >= b)
    a, b = part[:, None], part[None]
    same = a // CH == b // CH

    def level(n):
        return (a // (2 * n) == b // (2 * n)) & (a // n != b // n)
    put("before0", -1.0 * (same & (a < b)))
    put("before1", -1.0 * (same & (a > b)))
    put("pair0", (a > b) & level(1))
    put("pair1", (a < b) & level(1))
    put("same", -1.0 * same)
    put("lev1", level(1))
    for n in LEVELS:
        put(f"lev{n}", level(n))
    put("reset", np.tile((np.arange(RJ * CH) % CH != 0) * 1.0, (P, 1)))
    put("before", part[:, None] < part[None])
    put("iota", np.tile(np.arange(NTAB), (P, 1)))
    put("prio", np.tile(np.arange(NE, 0, -1.0), (P, 1)))
    t = np.arange(SEQ)
    inv = (10000.0 ** (-np.arange(half, dtype=np.float32) / np.float32(half))).astype(np.float32)
    ang = np.stack([t // GRID_W, t % GRID_W], -1).astype(np.float32)[..., None] * inv
    ang = np.repeat(ang[:, :, None, :], 2, 2).reshape(SEQ, ROPE).T.astype(np.float64)
    con[NOPE:QK, CON["cos"]:CON["cos"] + SEQ] = np.cos(ang)
    con[NOPE:QK, CON["sin"]:CON["sin"] + SEQ] = np.sin(ang)
    ch = 2 * np.pi * np.outer(np.arange(FGD), np.arange(FGD)) / FGD
    tk = 2 * np.pi * np.outer(t, t) / SEQ
    ct, st = (f(tk) * SEQ ** -0.5 for f in (np.cos, np.sin))
    dft = np.concatenate([f(ch) * FGD ** -0.5 for f in (np.cos, np.sin)] +
                         [x[n * P:n * P + P] for x in (ct, -st) for n in range(2)], 1)
    return con.astype(np.float32), dft.astype(np.float32)


def kernel(**inputs):
    from concourse import bacc
    from concourse.bass_utils import run_bass_kernel_spmd

    a = {k: np.asarray(v) for k, v in inputs.items()}
    L = DEPTH

    def cols(x):
        x = x.reshape(*x.shape[:-1], -1, P)
        return np.moveaxis(x, -1, 0)

    tok = np.concatenate([a["x"][0], a["ctx"][0]], 0)
    xT = cols(tok).transpose(0, 2, 1).reshape(P, KD * T)
    cT = cols(np.stack([a["c"][0], a["c_ctx"]])).transpose(0, 2, 1).reshape(P, KD * 2)
    parts = [a["norm1_g"], a["norm2_g"], a["b_ada"], a["q_norm_g"], a["kv_norm_g"], a["rwkv_mu"],
             a["rwkv_w0"].reshape(L, -1), a["rwkv_a0"].reshape(L, -1), a["rwkv_k_k"], a["rwkv_k_a"],
             a["rwkv_r_k"].reshape(L, -1), a["rwkv_gn_g"], a["rwkv_gn_b"]]
    vec = np.concatenate([cols(x) for x in parts], 2).reshape(P, L * NVEC)
    con, dft = constants()
    uq = a["w_uq"].reshape(L, 3, P, HEADS, QK).transpose(0, 3, 2, 1, 4).reshape(L, HEADS, P, 3 * QK)
    uk = a["w_ukv"].reshape(L, 2, P, HEADS, NOPE + VD)[..., :NOPE].transpose(0, 3, 2, 1, 4).reshape(L, HEADS, P, 2 * NOPE)
    up = np.concatenate([a["rwkv_w_up"], a["rwkv_a_up"]], 2).transpose(0, 2, 1, 3).reshape(L, P, 2 * RD)
    arrays = dict(
        xT=xT, cT=cT, vec=vec, fng=cols(a["final_norm_g"]), rb=np.tile(a["router_b"][None], (P, 1)),
        rw=a["router_w"].reshape(KD, P, NE).transpose(1, 0, 2).reshape(P, KD * NE),
        w_ada=a["w_ada"], w_in=a["w_in"], headw=np.concatenate([uq, uk], 3), w_ukv=a["w_ukv"],
        lora=np.concatenate([up, a["rwkv_g_up"]], 2), w_a=a["w_proj_a"], w_b=a["w_proj_b"], w_c=a["w_proj_c"],
        w_out=a["w_out"], eg=a["exp_w_gate"], eu=a["exp_w_up"], ed=a["exp_w_down"], sg=a["sh_w_gate"],
        su=a["sh_w_up"], sd=a["sh_w_down"], con=con, dft=dft)
    arrays = {f"in_{k}": np.ascontiguousarray(v) for k, v in arrays.items()}
    nc = bacc.Bacc("TRN2", target_bir_lowering=False, num_devices=1)
    args = {k[3:]: nc.dram_tensor(k, v.shape, mybir.dt.from_np(v.dtype), kind="ExternalInput").ap()
            for k, v in arrays.items()}
    out = nc.dram_tensor("out", (P, KD, SEQ), F32, kind="ExternalOutput").ap()
    build(nc, **args, out=out)
    r = run_bass_kernel_spmd(nc, [arrays], core_ids=[0])
    y = np.asarray(r.results[0]["out"]).reshape(P, KD, SEQ)
    return y.transpose(2, 1, 0).reshape(1, SEQ, D)
```

```python
from contextlib import ExitStack
import math

import numpy as np

import concourse.bass as bass
from concourse import mybir

F32 = mybir.dt.float32
ALU = mybir.AluOpType
ACT = mybir.ActivationFunctionType
AX_X = mybir.AxisListType.X
P = 128

D = 1024
KD = D // P
DEPTH = 2
SEQ, CTX = 256, 256
T = SEQ + CTX
GRID_W = 64
FG, FGD = 4, 128
HEADS, NOPE, ROPE, VD = 8, 64, 32, 64
QK = NOPE + ROPE
QL, KVL = 384, 256
SCALE = QK ** -0.5
RH, RN = 8, 64
RD = RH * RN
RJ = RD // P
RIN = 3 * RD + 64 + 64 + 128
RT = RIN // P
NE, NG, EPG, FF = 16, 4, 4, 512
FK = FF // P
EPS = 1e-6
GN_EPS = 64e-5
DECAY = math.exp(-0.5)
CH = 64
NCH = SEQ // CH
TILES = [T * 2 // P + NE, SEQ * 2 // P + NE]
NTAB = max(TILES)
ZEROS = 256
LEVELS = [2, 4, 8, 16, 32]

C_F, C_Q = 0, 512
C_KV = C_Q + QL
C_R = C_KV + KVL + ROPE
C_G = C_R + RIN
IN_DIM = C_G + 3 * D

VEC = {}
_n = 0
for _name, _w in (("n1", 8), ("n2", 8), ("bada", 48), ("qg", 3), ("kvg", 2), ("mu", RT), ("w0", 8), ("a0", 8),
                  ("kk", 4), ("ka", 4), ("rk", 4), ("gng", 4), ("gnb", 4)):
    VEC[_name] = _n
    _n += _w
NVEC = _n

CON = {}
_n = 0
for _name, _w in (("ident", P), ("ones", P), ("groups", 2), ("heads", P), ("rot", P), ("minus0", CH), ("minus1", CH),
                  ("incl0", CH), ("incl1", CH), ("before0", P), ("before1", P), ("pair0", P), ("pair1", P), ("same", P),
                  ("lev1", P), *((f"lev{b}", P) for b in LEVELS), ("reset", RJ * CH), ("prio", NE),
                  ("before", P), ("iota", NTAB), ("cos", SEQ), ("sin", SEQ)):
    CON[_name] = _n
    _n += _w
NCON = _n
NDFT = 2 * FGD + 4 * SEQ
HW = 3 * QK + 2 * NOPE

NSLOT = 3
N_ADA = 12
L_F, L_Q, L_KV, L_DFT, L_UKV, L_R, L_K, L_V, L_WAG, L_LORA = range(N_ADA, N_ADA + 10)
L_MERGE = L_LORA + 1
L_OUT = L_MERGE + 12
L_EXP = L_OUT + 2
PER_LAYER = L_EXP + 3
assert N_ADA % NSLOT == 0 and L_EXP % NSLOT == 0 and PER_LAYER % NSLOT == 0
ROUNDS = PER_LAYER // NSLOT


def build(nc, xT, cT, vec, fng, rb, rw, w_ada, w_in, headw, w_ukv, lora, w_a, w_b, w_c, w_out,
          eg, eu, ed, sg, su, sd, con, dft, out):
    xg = nc.dram_tensor("expert_rows", [(NTAB + 1) * P, D], F32).ap()
    width = [T, SEQ]
    with ExitStack() as ctx:
        def sb(name, shape):
            return ctx.enter_context(nc.sbuf_tensor(name, shape, F32))

        sems = {}

        def sem(name):
            if name not in sems:
                sems[name] = ctx.enter_context(nc.semaphore(name))
            return sems[name]

        ps = ctx.enter_context(nc.psum_tensor("ps", [P, 8, 512], F32))
        X = sb("X", [P, KD, T])
        H = sb("H", [P, KD, T])
        cons = sb("cons", [P, NCON])
        vecs = sb("vecs", [P, DEPTH, NVEC])
        fngs = sb("fngs", [P, KD])
        rbs = sb("rbs", [P, NE])
        rws = sb("rws", [P, KD, NE])
        epst = sb("epst", [P, 3])
        csil = sb("csil", [P, KD, 2])
        mod = sb("mod", [P, 48, 2])
        gsc = sb("gsc", [P, 2, KD, 2])
        dummy = sb("marks", [P, 4])
        small = sb("small", [P, 8])
        starts = sb("starts", [P, 16])
        total = sb("total", [P, 2, RJ])
        WORK = 28928
        SETS = NSLOT * 4096
        memory = sb("memory", [P, SETS + WORK])
        W = memory[:, 0:SETS].rearrange("p (s n) -> p s n", s=NSLOT)
        work = memory[:, SETS:]
        zeros = work[:, WORK - ZEROS:]
        pos = ctx.enter_context(nc.sbuf_tensor("pos", [P, 2 * T // P], mybir.dt.int32))
        tile_expert = ctx.enter_context(nc.sbuf_tensor("tile_expert", [P, NTAB], mybir.dt.int32))
        tile_pairs = ctx.enter_context(nc.sbuf_tensor("tile_pairs", [P, DEPTH], mybir.dt.int32))

        def con_(name, w=CH):
            return cons[:, CON[name]:CON[name] + w]

        ident, ones, hsum = con_("ident", P), con_("ones", P), con_("heads", P)
        rot = cons[:, CON["rot"]:CON["rot"] + QK]

        def place(at, n, w=T):
            assert at + n * w <= WORK
            return work[:, at:at + n * w].rearrange("p (j n) -> p j n", n=w)

        FO, AO, Y = place(0, 4), place(2048, 4), place(4096, 4)
        GX, WA = place(6144, 1), place(6656, 1)
        TOP = 7168
        ROW = place(TOP, 3)
        CP = place(TOP + 1536, KD, 32)
        RS = place(TOP, 2)
        FZ, FA = place(TOP, 4), place(TOP + 2048, 2)
        CQ, CKV = place(TOP + 3072, 3), place(TOP + 4608, 2)
        KR, VT = place(TOP + 5632, 1), place(TOP + 6144, 4)
        SQ, RQ = place(TOP + 8192, 5), place(TOP + 10752, 2)
        RP = place(TOP + 11776, 2)
        Qh, Kh, Pb, PT = (place(TOP + 12800 + 1024 * n, 2) for n in range(4))
        Vh, WH = place(TOP + 16896, 2, 256), place(TOP + 17408, 2, HW)
        R, V, KK = (place(TOP + 2048 * n, 4) for n in range(3))
        B = [place(TOP + 2048 * (3 + d), 4) for d in range(2)]
        K1 = place(TOP + 2048 * 5, 4)
        KDs = [place(TOP + 2048 * 6, 4), K1]
        LW = [place(TOP + 2048 * (7 + d), 4) for d in range(2)]
        SCR = TOP + 2048 * 9
        PP = work[:, SCR:SCR + 2 * 2 * 258].rearrange("p (b s n) -> p b s n", b=2, s=2)
        TS = place(SCR + 1032, 2)
        DA = place(SCR, 2)
        spare = [work[:, SCR + 512 * n:SCR + 512 * (n + 1)] for n in range(6)] + \
                [memory[:, 4096 * s_ + 512 * n:4096 * s_ + 512 * (n + 1)] for s_ in range(NSLOT)
                 for n in range(0 if s_ else 3, 8)]
        ER = [spare.pop(0).rearrange("p (x j n) -> p x j n", x=2, n=CH) for d in range(2)]
        SB = {"E3": [ER[d][:, 0] for d in range(2)], "Rq": [ER[d][:, 1] for d in range(2)]}
        for names in ((("MT",), ("Grb",)), (("E1",), ("E2", "Grk"))):
            for d in range(2):
                both = spare.pop(0)
                for x, same in enumerate(names):
                    for name in same:
                        SB.setdefault(name, []).append(both[:, 256 * x:256 * x + 256].rearrange("p (j n) -> p j n", n=CH))
        for name, both in (("lw", spare.pop(0)), ("L", WA[:, 0, :])):
            SB[name] = [both[:, 256 * d:256 * d + 256].rearrange("p (j n) -> p j n", n=CH) for d in range(2)]
        for same in (("bE2", "BT"), ("bKk", "Gak"), ("bV", "P", "RHS"), ("bE3",), ("Bt",), ("Kt",), ("Vt",), ("XT",),
                     ("X", "U"), ("S",)):
            for d in range(2):
                one = spare.pop(0).rearrange("p (j n) -> p j n", n=P)
                for name in same:
                    SB.setdefault(name, []).append(one)
        M, SG = place(TOP, 8), place(TOP + 4096, 2)
        TM = place(TOP + 5120, 1)
        W2 = work[:, 0:SETS].rearrange("p (s n) -> p s n", s=NSLOT)
        sets = [W, W2]
        MT_ = place(SETS, 4, D)
        YT = MT_
        HS = place(SETS + 4096, 4)
        XG, YG = place(SETS + 6144, 2, D), place(SETS + 8192, 2, D)
        XGT = place(SETS + 10240, KD, P)
        SIL, HID, HIDT = (place(SETS + 11264 + 512 * n, 1) for n in range(3))
        RO = SETS + 12800
        rt = [work[:, RO + 128 * n:RO + 128 * n + 128] for n in range(10)]
        small16 = [work[:, RO + 1280 + 16 * n:RO + 1296 + 16 * n] for n in range(8)]
        TAB = work[:, RO + 1408:RO + 1408 + NTAB * NE]
        assert RO + 1408 + NTAB * NE <= WORK - ZEROS

        def slot(n):
            return W[:, n % NSLOT, :]

        def loaded(eng, l, n, more=0):
            eng.wait_ge(sem(f"slot_loaded{n % NSLOT}"), 16 * (ROUNDS * l + n // NSLOT + 1 + more))

        four = [2 * FG, FG]
        nqt = [T // P, SEQ // P]
        PH = {"act": 0, "dve": 0, "pool": 0, "pe": 0}

        class Chain:

            def __init__(self, eng, name):
                self.eng, self.s, self.n, self.var = eng, sem(name), 0, 0

            def __call__(self, ins):
                self.n += 1
                ins.then_inc(self.s, 1)
                self.eng.wait_ge(self.s, self.var + self.n)

            def loop(self, i, per):
                self.start, self.per, self.var = self.n, per, i * per

            def end(self, times):
                assert self.n - self.start == self.per, (self.n - self.start, self.per)
                self.n, self.var = self.start + self.per * times, 0

        def handover(who, eng, ins=None):
            PH[who] += 1
            if ins is not None:
                ins.then_inc(sem(f"stage_{who}"), 1)
            for n in ("act", "dve", "pool"):
                eng.wait_ge(sem(f"stage_{n}"), PH[who])

        def wait(eng, name, count):
            if not (isinstance(count, int) and count == 0):
                eng.wait_ge(sem(name), count)

        def wait_apart(eng, name, count):
            eng.wait_ge(sem(name), count)
            eng.nop(nofuse=True)

        def pair_count(eng, l):
            return eng.value_load(tile_pairs[0:1, l:l + 1], min_val=1, max_val=TILES[l] // 2)

        def head_rounds(eng, body, before=None, after=None):
            with eng.Fori(0, HEADS // 2 - 1) as i:
                if before:
                    before(i)
                for b in range(2):
                    body(i, b, (i + b, 1 - b))
                if after:
                    after()
            for b in range(2):
                body(HEADS // 2 - 1, b, None if b else (HEADS // 2 - 1, 1))

        def scan_steps(eng, l, body):
            def columns(s, c):
                return [(1 - s) * SEQ + c * CH, (1 - s) * SEQ + (NCH - 1) * CH - c * CH]
            for s in range(2):
                with eng.Fori(0, NCH - 1) as c:
                    body(s, c, (2 * l + s) * NCH + c, columns(s, c), columns(s, c + 1))
                c = NCH - 1
                body(s, c, (2 * l + s) * NCH + c, columns(s, c), columns(1, 0) if s == 0 else None)

        def first_columns():
            return [SEQ, SEQ + (NCH - 1) * CH]

        def over_pairs(mask):
            return mask.unsqueeze(1).broadcast_to([P, RJ, mask.shape[1]])

        def both_heads(x):
            return x.unsqueeze(2).broadcast_to([P, RJ, 2, CH])

        def blocks(x):
            return x.rearrange("p j (h n) -> p j h n", h=2)

        def blocks_mask(name):
            return con_(name, P).rearrange("p (h n) -> p h n", h=2).unsqueeze(1).broadcast_to([P, RJ, 2, CH])

        block = ctx.enter_context(nc.Block())

        @block.sync
        def _(sp):
            for dst, src in ((X[:].rearrange("p k t -> p (k t)"), xT), (csil[:].rearrange("p k t -> p (k t)"), cT),
                             (cons[:], con), (vecs[:].rearrange("p l n -> p (l n)"), vec), (fngs[:], fng),
                             (rbs[:], rb), (rws[:].rearrange("p k e -> p (k e)"), rw)):
                sp.dma_start(dst, src).then_inc(sem("params"), 16)

            def rows(ap, k):
                return ap.rearrange("(k p) n -> p k n", k=k)

            def load(l, n, src, k, w, reader=None, count=0, more=0):
                if reader:
                    sp.wait_ge(sem(reader), count)
                sp.dma_start(slot(n)[:, 0:k * w].rearrange("p (k n) -> p k n", k=k), src)\
                    .then_inc(sem(f"slot_loaded{n % NSLOT}"), 16)

            pairs_before = 0
            for l in range(DEPTH):
                def ada(g):
                    return rows(w_ada[l, :, bass.ds(g * 512, 512)], KD), KD, 512
                for s in range(NSLOT):
                    its = pairs_before + 1
                    reader = ("tile_down0", its) if s == 2 else ("tile_up0", its)
                    load(l, s, *ada(s), *(reader if l else ()))
                with sp.Fori(1, N_ADA // NSLOT) as i:
                    for s in range(NSLOT):
                        load(l, s, *ada(i * NSLOT + s), "ada_rows", N_ADA * l + (i - 1) * NSLOT + s + 1)
                at = N_ADA * (l + 1)
                load(l, L_F, rows(w_in[l, :, C_F:C_F + 512], KD), KD, 512, "ada_rows", at - 2)
                load(l, L_Q, rows(w_in[l, :, C_Q:C_Q + QL], KD), KD, QL, "ada_rows", at - 1)
                load(l, L_KV, rows(w_in[l, :, C_KV:C_KV + KVL + ROPE], KD), KD, KVL + ROPE, "ada_rows", at)
                load(l, L_DFT, dft.rearrange("p (k n) -> p k n", k=1), 1, NDFT, "ina_ready", 10 * l + 4)
                load(l, L_UKV, rows(w_ukv[l], 2), 2, 1024, "ina_ready", 10 * l + 7)
                load(l, L_R, rows(w_in[l, :, C_R:C_R + 512], KD), KD, 512, "ina_ready", 10 * l + 10)
                for b in range(2):
                    if l:
                        sp.wait_ge(sem(f"heads_made{b}"), l * (HEADS // 2))
                    sp.dma_start(WH[:, b, :], headw[l, b, :, :]).then_inc(sem(f"headw_loaded{b}"), 16)
                with sp.Fori(1, HEADS // 2) as i:
                    for b in range(2):
                        sp.wait_ge(sem(f"heads_made{b}"), l * (HEADS // 2) + i)
                        sp.dma_start(WH[:, b, :], headw[l, bass.ds(2 * i + b, 1), :, :].rearrange("h p n -> p (h n)"))\
                            .then_inc(sem(f"headw_loaded{b}"), 16)
                load(l, L_K, rows(w_in[l, :, C_R + 512:C_R + 1024], KD), KD, 512, "fourier_ready", sum(four[:l + 1]))
                load(l, L_V, rows(w_in[l, :, C_R + 1024:C_R + 1536], KD), KD, 512, "values_ready", 4 * (l + 1))
                load(l, L_WAG, rows(w_in[l, :, C_R + 1536:C_R + 1792], KD), KD, 256, "rin_ready", RT * l + 4)
                load(l, L_LORA, lora[l].rearrange("p (k n) -> p k n", k=1), 1, 1536, "rin_ready", RT * l + 8)

                def gate(b, g):
                    return rows(w_in[l, :, bass.ds(C_G + b * D + g * 512, 512)], KD), KD, 512

                def proj(b, g):
                    return rows((w_a, w_b, w_c)[b][l, :, bass.ds(g * 512, 512)], 4), 4, 512
                if l == 0:
                    sp.wait_ge(sem("constants_set"), 4)
                    for at in range(0, D, ZEROS):
                        sp.dma_start(xg[:, at:at + ZEROS].rearrange("(n p) c -> p n c", p=P),
                                     zeros.unsqueeze(1).broadcast_to([P, NTAB + 1, ZEROS])).then_inc(sem("rows_zeroed"), 16)
                load(l, L_MERGE, *gate(0, 0), "scan_over", l + 1)
                load(l, L_MERGE + 1, *proj(0, 0))
                load(l, L_MERGE + 2, *gate(1, 0), "post_over", l + 1)
                load(l, L_MERGE + 3, *proj(1, 0), "merge_gate", 24 * l + 4)
                load(l, L_MERGE + 4, *gate(2, 0), "merge_proj", 24 * l + 4)
                load(l, L_MERGE + 5, *proj(2, 0), "merge_gate", 24 * l + 8)
                load(l, L_MERGE + 6, *gate(0, 1), "merge_proj", 24 * l + 8)
                load(l, L_MERGE + 7, *proj(0, 1), "merge_gate", 24 * l + 12)
                load(l, L_MERGE + 8, *gate(1, 1), "merge_proj", 24 * l + 12)
                load(l, L_MERGE + 9, *proj(1, 1), "merge_gate", 24 * l + 16)
                load(l, L_MERGE + 10, *gate(2, 1), "merge_proj", 24 * l + 16)
                load(l, L_MERGE + 11, *proj(2, 1), "merge_gate", 24 * l + 20)
                for g, reader in enumerate((("merge_proj", 24 * l + 20), ("merge_gate", 24 * l + 24))):
                    load(l, L_OUT + g, rows(w_out[l, :, g * 512:g * 512 + 512], KD), KD, 512, *reader)
                load(l, L_EXP, rows(sg[l], KD), KD, 512, "merge_proj", 24 * l + 24)
                load(l, L_EXP + 1, rows(su[l], KD), KD, 512, "out_ready", KD * l + 4)
                load(l, L_EXP + 2, rows(sd[l], FK), FK, 1024, "out_ready", KD * l + 8)
                sp.wait_ge(sem("route_ready"), l + 1)
                sp.wait_ge(sem("rows_placed"), 16 * sum(2 * n for n in nqt[:l + 1]))

                def token_rows(j, b):
                    sp.dma_start(XG[:, b, :], xg[bass.ds(j * P, P), :]).then_inc(sem(f"rows_loaded{b}"), 16)

                token_rows(0, 0)
                sp.wait_ge(sem("up_ready"), FK * (l + 1))
                pairs = pair_count(sp, l)
                with sp.Fori(0, pairs) as i:
                    it = pairs_before + i
                    for b in range(2):
                        e = sp.value_load(tile_expert[0:1, bass.ds(2 * i + b, 1)], min_val=0, max_val=NE - 1)
                        sp.wait_ge(sem(f"tile_up{b}"), it + 1)
                        for n, src in ((0, eg), (1, eu)):
                            sp.dma_start(sets[b][:, n, :].rearrange("p (k n) -> p k n", k=KD),
                                         rows(src[l, bass.ds(e, 1), :, :].rearrange("e d f -> (e d) f"), KD))\
                                .then_inc(sem(f"tile_loaded{n}{b}"), 16)
                        sp.wait_ge(sem(f"rows_turned{1 - b}"), it + 1 + b + (l if b else 0))
                        token_rows(2 * i + b + 1, 1 - b)
                        if b == 0:
                            sp.wait_ge(sem("down_ready"), KD * (l + 1))
                        sp.wait_ge(sem(f"tile_down{b}"), it + 1)
                        sp.dma_start(sets[b][:, 2, :].rearrange("p (k n) -> p k n", k=FK),
                                     rows(ed[l, bass.ds(e, 1), :, :].rearrange("e f d -> (e f) d"), FK))\
                            .then_inc(sem(f"tile_loaded2{b}"), 16)
                pairs_before = pairs_before + pairs
            sp.wait_ge(sem("result"), 1)
            sp.dma_start(out, H[:, :, 0:SEQ]).then_inc(sem("stored"), 16)
            sp.wait_ge(sem("stored"), 16)

        @block.tensor
        def _(pe):
            mm = nc.tensor.matmul
            pe.wait_ge(sem("params"), 16 * 7)

            def product(bank, w, lhs, rhs, n, M=P):
                for k in range(n):
                    ins = mm(ps[0:M, bank, 0:w], lhs(k), rhs(k), start=(k == 0), stop=(k == n - 1))
                return ins

            def weights(n, w, j):
                return lambda k: slot(n)[:, k * w + j * P:k * w + j * P + P]

            norms = 0

            def sum_squares(w):
                nonlocal norms
                for k in range(KD):
                    pe.wait_ge(sem(f"squares{k % 2}"), KD // 2 * norms + k // 2 + 1)
                    ins = mm(ps[:, 0, 0:w], ones, H[:, k, 0:w], start=(k == 0), stop=(k == KD - 1))
                ins.then_inc(sem("sumsq"), 1)
                norms += 1
                handover("pe", pe)

            pairs_before = 0
            for l in range(DEPTH):
                w = width[l]

                pe.wait_ge(sem("csil"), l + 2)
                with pe.Fori(0, N_ADA // NSLOT) as i:
                    at = N_ADA * l + i * NSLOT

                    def turn(s):
                        wait_apart(pe, "ada_copied", at + s + 1)
                        for q in range(4):
                            ins = mm(ps[:, 3 + s, 2 * q:2 * q + 2], ROW[:, s, q * P:q * P + P], con_("groups", 2),
                                     start=True, stop=True)
                        ins.then_inc(sem("ada_cols"), 1)

                    pe.wait_ge(sem("ada_mod"), at + 1)
                    for s in range(NSLOT):
                        loaded(pe, l, s, i)
                        for k in range(KD):
                            g = k % 4
                            ins = mm(ps[32 * g:32 * g + 32, s, :], CP[:, k, :], slot(s)[:, k * 512:k * 512 + 512],
                                     start=(k < 4), stop=(k >= 4))
                        ins.then_inc(sem("ada_rows"), 1)
                        if s:
                            turn(s - 1)
                    turn(NSLOT - 1)
                handover("pe", pe)
                sum_squares(T)

                o = 10 * l
                for n, cw, tiles in ((L_F, 512, 4), (L_Q, QL, 3), (L_KV, KVL + ROPE, 3)):
                    loaded(pe, l, n)
                    ww = T if n == L_KV else w
                    for j in range(tiles):
                        b = o - 10 * l
                        if b >= 8:
                            pe.wait_ge(sem("ina_copied"), o - 7)
                        if n == L_KV and j == 2:
                            ins = product(b % 8, ww, lambda k: slot(n)[:, k * cw + KVL - NOPE:k * cw + KVL + ROPE],
                                          lambda k: H[:, k, 0:ww], KD, QK)
                        else:
                            ins = product(b % 8, ww, weights(n, cw, j), lambda k: H[:, k, 0:ww], KD)
                        ins.then_inc(sem("ina_ready"), 1)
                        o += 1
                handover("pe", pe)

                loaded(pe, l, L_DFT)
                units = [(g, q) for g in range(FG) for q in range(four[l] // FG)]
                base = sum(four[:l])

                def over_tokens(u):
                    pe.wait_ge(sem("fourier_mid"), base + u + 1)
                    if u >= 2:
                        pe.wait_ge(sem("fourier_out"), base + u - 1)
                    for n in range(4):
                        c, t = n // 2, n % 2
                        ins = mm(ps[:, 2 + u % 2, 0:SEQ], FA[:, u % 2, t * 256 + c * FGD:t * 256 + c * FGD + FGD],
                                 slot(L_DFT)[:, 256 + n * SEQ:256 + n * SEQ + SEQ], start=(n == 0), stop=(n == 3))
                    ins.then_inc(sem("fourier_ready"), 1)

                for u, (g, q) in enumerate(units):
                    if u >= 2:
                        pe.wait_ge(sem("fourier_mid"), base + u - 1)
                    for t in range(2):
                        ins = mm(ps[:, u % 2, t * 256:t * 256 + 256], FZ[:, g, q * SEQ + t * P:q * SEQ + t * P + P],
                                 slot(L_DFT)[:, 0:256], start=True, stop=True)
                    ins.then_inc(sem("fourier_first"), 1)
                    if u:
                        over_tokens(u - 1)
                over_tokens(len(units) - 1)
                handover("pe", pe)

                pe.wait_ge(sem("lora_squares"), 5 * l + 3)
                product(0, w, lambda k: ones, lambda k: SQ[:, k, 0:w], 3).then_inc(sem("lora_sums"), 1)
                pe.wait_ge(sem("lora_squares"), 5 * l + 5)
                product(1, T, lambda k: ones, lambda k: SQ[:, 3 + k, :], 2).then_inc(sem("lora_sums"), 1)
                mm(ps[0:QK, 2, 0:SEQ], rot[0:QK, :], KR[0:QK, 0, 0:SEQ], start=True, stop=True)\
                    .then_inc(sem("key_turned"), 1)
                pe.wait_ge(sem("lora_normed"), l + 1)
                loaded(pe, l, L_UKV)
                for t in range(T // P):
                    vals = [slot(L_UKV)[:, k * 1024:k * 1024 + 1024].rearrange("p (h n) -> p h n", n=NOPE + VD)[:, :, NOPE:]
                            for k in range(2)]
                    product(4 + t, HEADS * VD, lambda k: CKV[:, k, t * P:t * P + P], lambda k: vals[k], 2)\
                        .then_inc(sem("values_ready"), 1)
                handover("pe", pe)

                n_q = nqt[l]
                def make(i, b):
                    pe.wait_ge(sem(f"headw_loaded{b}"), 16 * (l * (HEADS // 2) + i + 1))
                    product(0, w, lambda k: WH[:, b, k * QK:k * QK + QK], lambda k: CQ[:, k, 0:w], 3, QK)
                    product(1, T, lambda k: WH[:, b, 3 * QK + k * NOPE:3 * QK + k * NOPE + NOPE],
                            lambda k: CKV[:, k, :], 2, NOPE).then_inc(sem(f"heads_made{b}"), 1)

                def rotate(i, b):
                    h = l * HEADS + 2 * i + b
                    pe.wait_ge(sem("heads_copied"), 2 * h + 2)
                    mm(ps[0:QK, 2, 0:SEQ], rot[0:QK, :], Qh[0:QK, b, 0:SEQ], start=True, stop=True)\
                        .then_inc(sem("query_turned"), 1)

                def attend(i, b, ahead):
                    h = l * HEADS + 2 * i + b
                    qbase = HEADS * sum(nqt[:l]) + (2 * i + b) * n_q
                    pe.wait_ge(sem("query_done"), h + 1)

                    def keys(q):
                        return (0, T) if q < SEQ // P else (SEQ, T)

                    def scores(q):
                        k0, k1 = keys(q)
                        mm(ps[:, 3 + q % 2, k0:k1], Qh[0:QK, b, q * P:q * P + P], Kh[0:QK, b, k0:k1],
                           start=True, stop=True).then_inc(sem("scores_ready"), 1)

                    def values(q):
                        pe.wait_ge(sem("probs_copied"), qbase + q + 1)
                        if q == 0:
                            pe.wait_ge(sem("heads_out"), h + 1)
                        first = keys(q)[0] // P
                        for c in range(first, T // P):
                            ins = mm(ps[b * VD:b * VD + VD, 7, q * P:q * P + P],
                                     Vh[:, b, c * VD:c * VD + VD], PT[:, q % 2, c * P:c * P + P],
                                     start=(c == first), stop=(c == T // P - 1))
                        if q == n_q - 1:
                            ins.then_inc(sem("attention_ready"), 1)

                    scores(0)
                    for q in range(n_q):
                        if q + 1 < n_q:
                            scores(q + 1)
                        if ahead and q == 0:
                            make(*ahead)
                        pe.wait_ge(sem("probs_ready"), qbase + q + 1)
                        for c in range(keys(q)[0] // P, T // P):
                            ins = pe.transpose(ps[:, 5 + q % 2, c * P:c * P + P], Pb[:, q % 2, c * P:c * P + P], ident)
                        ins.then_inc(sem("probs_turned"), 1)
                        if ahead and q == 0:
                            rotate(*ahead)
                        if q:
                            values(q - 1)
                    values(n_q - 1)

                make(0, 0)
                rotate(0, 0)
                head_rounds(pe, attend)
                handover("pe", pe)

                for o in range(RT):
                    n, j = L_R + o // 4, o % 4
                    if j == 0:
                        loaded(pe, l, n)
                    if o >= 8:
                        pe.wait_ge(sem("rin_copied"), RT * l + o - 7)
                    product(o % 8, T, weights(n, 256 if n == L_WAG else 512, j), lambda k: H[:, k, :], KD)\
                        .then_inc(sem("rin_ready"), 1)
                handover("pe", pe)

                for j in range(RJ):
                    pe.wait_ge(sem("key_squares"), RJ * l + j + 1)
                    mm(ps[:, j, :], hsum, B[0][:, j, :], start=True, stop=True).then_inc(sem("key_sums"), 1)
                loaded(pe, l, L_LORA)
                pe.wait_ge(sem("decay_input"), 2 * (l + 1))
                for u in range(2 * RJ):
                    j, d = u // 2, u % 2
                    for half in range(2):
                        if 2 * u + half >= 4:
                            pe.wait_ge(sem("lora_gates"), 16 * l + 2 * u + half - 3)
                        mm(ps[:, 4 + (2 * u + half) % 4, :], slot(L_LORA)[:, d * RD + j * P:d * RD + j * P + P], DA[:, half, :],
                           start=True, stop=True).then_inc(sem("lora_up"), 1)
                handover("pe", pe)

                def scan_step(s, c, step, at, ahead):

                    def bank(d, n):
                        return ps[:, 4 * d + n, :].rearrange("p (j n) -> p j n", n=P)

                    def pairs(out, *terms):
                        for j in range(RJ):
                            for n, (lhs, rhs) in enumerate(terms):
                                ins = mm(out[:, j, :], lhs[:, j, :], rhs[:, j, :], start=(n == 0), stop=(n == len(terms) - 1))
                        return ins

                    def turn(d, name):
                        for j in range(RJ):
                            ins = pe.transpose(bank(d, 3)[:, j, :], b_(name, d)[:, j, :], ident)
                        ins.then_inc(sem(f"grams{d}"), 1)

                    b_ = lambda name, d: SB[name][d]
                    for d in range(2):
                        wait_apart(pe, f"scaled{d}", 2 * step + 2)
                        for n, name in enumerate(("bE2", "bKk")):
                            both = ps[:, 4 * d + n, :].rearrange("p (x j n) -> p x j n", x=2, n=CH)
                            for j in range(RJ):
                                mm(both[:, :, j, :], b_(name, d)[:, j, :], ER[d][:, :, j, :], start=True, stop=True)
                        pairs(bank(d, 2), (b_("bE3", d), b_("bE2", d)))
                        turn(d, "bE2")
                    for n, name in enumerate(("bKk", "bV")):
                        for d in range(2):
                            wait_apart(pe, f"turned{d}", 3 * step + n + 1)
                            turn(d, name)
                    for n in range(len(LEVELS)):
                        last = n == len(LEVELS) - 1
                        for d in range(2):
                            wait_apart(pe, f"blocks{d}", step * len(LEVELS) + n + 1)
                            wait_apart(pe, f"inverse{d}", step * (len(LEVELS) + 1) + n + 1)
                            if n == 0:
                                wait_apart(pe, f"turned{d}", 3 * step + 3)
                            pairs(bank(d, 3), (b_("BT", d), b_("X", d))).then_inc(sem(f"joined{d}"), 1)
                        for d in range(2):
                            wait_apart(pe, f"joined_copied{d}", step * len(LEVELS) + n + 1)
                            if n == 0:
                                wait_apart(pe, f"masked{d}", step + 1)
                            if not last:
                                pairs(bank(d, 2), (b_("XT", d), b_("P", d)))
                            pairs(bank(d, 1), (b_("P", d), b_("XT", d))).then_inc(sem(f"grown{d}"), 1)
                    for d in range(2):
                        wait_apart(pe, f"inverse{d}", step * (len(LEVELS) + 1) + len(LEVELS) + 1)
                        wait_apart(pe, f"state{d}", step + l + 1)
                        pairs(bank(d, 3), (b_("bE3", d), b_("S", d)), (b_("Gak", d), b_("Vt", d))).then_inc(sem(f"rhs{d}"), 1)
                    for d in range(2):
                        wait_apart(pe, f"rhs_copied{d}", step + 1)
                        pairs(bank(d, 3), (b_("XT", d), b_("RHS", d))).then_inc(sem(f"u{d}"), 1)
                    for d in range(2):
                        wait_apart(pe, f"u_copied{d}", step + 1)
                        if s or l < DEPTH - 1:
                            y = ps[:, 4 * d, 0:RJ * CH].rearrange("p (j n) -> p j n", n=CH)
                            pairs(y, (b_("S", d), b_("Rq", d)), (b_("U", d), b_("Grb", d)), (b_("Vt", d), b_("Grk", d)))
                        pairs(bank(d, 2), (b_("Bt", d), b_("U", d)), (b_("Kt", d), b_("Vt", d)))\
                            .then_inc(sem(f"step{d}"), 1)

                scan_steps(pe, l, scan_step)
                handover("pe", pe)

                for j in range(RJ):
                    pe.wait_ge(sem("bonus_input"), RJ * l + j + 1)
                    mm(ps[:, 4 * (j % 2), :], hsum, TS[:, 0, :], start=True, stop=True)
                    mm(ps[:, 4 * (j % 2) + 1, :], hsum, Y[:, j, :], start=True, stop=True)
                    mm(ps[:, 4 * (j % 2) + 2, :], slot(L_LORA)[:, 1024 + j * P:1024 + j * P + P], GX[:, 0, :],
                       start=True, stop=True).then_inc(sem("head_sums"), 1)
                    pe.wait_ge(sem("centred_squares"), RJ * l + j + 1)
                    mm(ps[:, 4 * (j % 2) + 3, :], hsum, TS[:, 1, :], start=True, stop=True).then_inc(sem("head_vars"), 1)
                handover("pe", pe)

                o = 24 * l
                for g in range(2):
                    for b, branch in enumerate((FO, AO, Y)):
                        n = L_MERGE + 6 * g + 2 * b
                        loaded(pe, l, n)
                        loaded(pe, l, n + 1)
                        for j in range(4):
                            if o - 24 * l >= 4:
                                pe.wait_ge(sem("merged"), o - 3)
                            product(2 * (o % 4), w, weights(n, 512, j), lambda k: H[:, k, 0:w], KD)\
                                .then_inc(sem("merge_gate"), 1)
                            product(2 * (o % 4) + 1, w, weights(n + 1, 512, j), lambda k: branch[:, k, 0:w], 4)\
                                .then_inc(sem("merge_proj"), 1)
                            o += 1
                handover("pe", pe)
                for j in range(KD):
                    if j % 4 == 0:
                        loaded(pe, l, L_OUT + j // 4)
                    product(j, w, weights(L_OUT + j // 4, 512, j % 4), lambda k: M[:, k, 0:w], KD)\
                        .then_inc(sem("out_ready"), 1)
                handover("pe", pe)
                sum_squares(w)

                nt = w // P
                for t in range(nt):
                    for k in range(KD):
                        ins = mm(ps[:, 7, t * NE:t * NE + NE], H[:, k, t * P:t * P + P], rws[:, k, :],
                                 start=(k == 0), stop=(k == KD - 1))
                ins.then_inc(sem("router_ready"), 1)
                for t in range(nt):
                    at = sum(nqt[:l]) + t
                    if t >= 2:
                        pe.wait_ge(sem("tokens_copied"), 2 * (at - 1))
                    for k in range(KD):
                        ins = pe.transpose(ps[:, 2 * (t % 2) + k // 4, (k % 4) * P:(k % 4) * P + P],
                                           H[:, k, t * P:t * P + P], ident)
                    ins.then_inc(sem("tokens_turned"), 1)
                pe.wait_ge(sem("tokens_copied"), 2 * sum(nqt[:l + 1]))

                loaded(pe, l, L_EXP)
                loaded(pe, l, L_EXP + 1)
                for j in range(FK):
                    if j >= 2:
                        pe.wait_ge(sem("hidden_ready"), FK * l + j - 1)
                    product(2 * (j % 2), w, weights(L_EXP, 512, j), lambda k: H[:, k, 0:w], KD)\
                        .then_inc(sem("gate_ready"), 1)
                    product(2 * (j % 2) + 1, w, weights(L_EXP + 1, 512, j), lambda k: H[:, k, 0:w], KD)\
                        .then_inc(sem("up_ready"), 1)
                pe.wait_ge(sem("chosen"), l + 1)
                for t in range(nt):
                    for q in range(t + 1):
                        mm(ps[:, 7, t * NE:t * NE + NE], cons[:, CON["before"]:CON["before"] + P] if q == t else ones,
                           rt[2][:, q * NE:q * NE + NE], start=(q == 0), stop=(q == t))
                for t in range(nt):
                    ins = mm(ps[:, 7, 128:128 + NE], ones, rt[2][:, t * NE:t * NE + NE], start=(t == 0), stop=(t == nt - 1))
                ins.then_inc(sem("ranked"), 1)
                loaded(pe, l, L_EXP + 2)
                pe.wait_ge(sem("hidden_ready"), FK * (l + 1))
                for j in range(KD):
                    if j >= 3:
                        pe.wait_ge(sem("down_added"), KD * l + j - 2)
                    product(4 + j % 3, w, weights(L_EXP + 2, 1024, j), lambda k: HS[:, k, 0:w], FK)\
                        .then_inc(sem("down_ready"), 1)
                pe.wait_ge(sem("down_added"), KD * (l + 1))

                def turn_rows(b):
                    for k in range(KD):
                        ins = pe.transpose(ps[:, k // 4, (k % 4) * P:(k % 4) * P + P], XG[:, b, k * P:k * P + P], ident)
                    return ins.then_inc(sem(f"rows_turned{b}"), 1)

                pe.wait_ge(sem("route_ready"), l + 1)
                pairs = pair_count(pe, l)
                pe.wait_ge(sem("rows_loaded0"), 16 * (pairs_before + l + 1))
                turn_rows(0)
                with pe.Fori(0, pairs) as i:
                    it = pairs_before + i
                    for b in range(2):
                        jt = 2 * it + b
                        pe.wait_ge(sem("rows_copied"), 2 * jt + 2 * l + 2)
                        pe.wait_ge(sem(f"tile_loaded0{b}"), 16 * (it + 1))
                        for n in range(2):
                            if n:
                                pe.wait_ge(sem(f"tile_loaded1{b}"), 16 * (it + 1))
                            for k in range(KD):
                                ins = mm(ps[:, 2 + n, :], XGT[:, k, :], sets[b][:, n, k * 512:k * 512 + 512],
                                         start=(k == 0), stop=(k == KD - 1))
                            ins.then_inc(sem(f"tile_up{b}") if n else sem("tile_gate"), 1)
                        pe.wait_ge(sem(f"rows_loaded{1 - b}"), 16 * (it + 1 + b + (l if b else 0)))
                        turn_rows(1 - b)
                        pe.wait_ge(sem("tile_hidden"), jt + 1)
                        for k in range(FK):
                            ins = pe.transpose(ps[:, 4, k * P:k * P + P], HID[:, 0, k * P:k * P + P], ident)
                        ins.then_inc(sem("hidden_turned"), 1)
                        pe.wait_ge(sem("hidden_copied"), jt + 1)
                        pe.wait_ge(sem(f"tile_loaded2{b}"), 16 * (it + 1))
                        pe.wait_ge(sem("result_copied"), 2 * jt + 2)
                        for half in range(2):
                            for k in range(FK):
                                ins = mm(ps[:, 5 + half, :], HIDT[:, 0, k * P:k * P + P],
                                         sets[b][:, 2, k * D + half * 512:k * D + half * 512 + 512],
                                         start=(k == 0), stop=(k == FK - 1))
                            ins.then_inc(sem("tile_half") if half == 0 else sem(f"tile_down{b}"), 1)
                for t in range(nt):
                    pe.wait_ge(sem("choices_summed"), sum(nqt[:l]) + t + 1)
                    for k in range(KD):
                        ins = pe.transpose(ps[:, 2 * (t % 4) + k // 4, (k % 4) * P:(k % 4) * P + P],
                                           YT[:, 2 * (t % 2), k * P:k * P + P], ident)
                    ins.then_inc(sem("choices_turned"), 1)
                handover("pe", pe)
                pairs_before = pairs_before + pairs
            sum_squares(SEQ)

        @block.scalar
        def _(act):
            link = Chain(act, "act_order")

            def rsqrt(out, x, n, eps):
                link(act.activation(out, x, ACT.Ln, bias=epst[:, eps:eps + 1], scale=1.0 / n))
                return act.activation(out, out, ACT.Exp, scale=-0.5)

            norms = 0

            def norm(w, l=0, n=None):
                nonlocal norms
                for k in range(0, KD, 2):
                    act.activation(H[:, k, 0:w], X[:, k, 0:w], ACT.Square).then_inc(sem("squares0"), 1)
                norms += 1
                act.wait_ge(sem("sumsq"), norms)
                rsqrt(RS[:, 0, 0:w], ps[:, 0, 0:w], D, 0).then_inc(sem("rstd"), 1)
                if n is not None:
                    for k in range(KD):
                        act.wait_ge(sem("normed"), KD * (norms - 1) + k + 1)
                        for s in range(w // SEQ):
                            x = H[:, k, s * SEQ:s * SEQ + SEQ]
                            act.activation(x, x, ACT.Identity, scale=gsc[:, n, k, s:s + 1],
                                           bias=mod[:, 24 * n + k, s:s + 1])
                handover("act", act, act.copy(dummy[:, 1:2], epst[:, 0:1]))

            act.wait_ge(sem("params"), 16 * 7)
            act.wait_ge(sem("constants_set"), 4)
            act.activation(csil[:], csil[:], ACT.Silu).then_inc(sem("csil"), 1)
            act.preload_act_table_set("natural_log_exp_and_others")

            pairs_before = 0
            for l in range(DEPTH):
                w = width[l]
                handover("act", act, act.copy(dummy[:, 1:2], epst[:, 0:1]))
                norm(T, l, 0)

                dst = [FZ[:, j, 0:w] for j in range(4)] + [CQ[:, j, 0:w] for j in range(3)] + \
                      [CKV[:, j, :] for j in range(2)] + [KR[0:QK, 0, :]]
                for o, out_ in enumerate(dst):
                    act.wait_ge(sem("ina_ready"), 10 * l + o + 1)
                    act.copy(out_, ps[0:out_.shape[0], o % 8, 0:out_.shape[1]]).then_inc(sem("ina_copied"), 1)
                handover("act", act, act.copy(dummy[:, 1:2], epst[:, 0:1]))

                base = sum(four[:l])
                for u, (g, q) in enumerate((g, q) for g in range(FG) for q in range(four[l] // FG)):
                    act.wait_ge(sem("fourier_ready"), base + u + 1)
                    act.copy(FO[:, g, q * SEQ:q * SEQ + SEQ], ps[:, 2 + u % 2, 0:SEQ]).then_inc(sem("fourier_out"), 1)
                handover("act", act, act.copy(dummy[:, 1:2], epst[:, 0:1]))

                for k in range(3):
                    act.activation(SQ[:, k, 0:w], CQ[:, k, 0:w], ACT.Square).then_inc(sem("lora_squares"), 1)
                for k in range(2):
                    act.activation(SQ[:, 3 + k, :], CKV[:, k, :], ACT.Square).then_inc(sem("lora_squares"), 1)
                act.wait_ge(sem("lora_sums"), 2 * l + 1)
                rsqrt(RQ[:, 0, 0:w], ps[:, 0, 0:w], QL, 0).then_inc(sem("lora_rstd"), 1)
                act.wait_ge(sem("lora_sums"), 2 * l + 2)
                rsqrt(RQ[:, 1, :], ps[:, 1, :], KVL, 0).then_inc(sem("lora_rstd"), 1)
                for t in range(T // P):
                    act.wait_ge(sem("values_ready"), 4 * l + t + 1)
                    act.copy(VT[:, t, :], ps[:, 4 + t, :])
                handover("act", act, act.copy(dummy[:, 1:2], epst[:, 0:1]))

                n_q = nqt[l]
                def copy_head(i, b):
                    act.wait_ge(sem(f"heads_made{b}"), l * (HEADS // 2) + i + 1)
                    act.copy(Qh[0:QK, b, 0:w], ps[0:QK, 0, 0:w]).then_inc(sem("heads_copied"), 1)
                    act.copy(Kh[0:NOPE, b, :], ps[0:NOPE, 1, :]).then_inc(sem("heads_copied"), 1)

                def attend(i, b, ahead):
                    qbase = HEADS * sum(nqt[:l]) + (2 * i + b) * n_q

                    def exps(q):
                        k0 = 0 if q < SEQ // P else SEQ
                        act.wait_ge(sem("probs_max"), qbase + q + 1)
                        if q >= 2:
                            act.wait_ge(sem("probs_turned"), qbase + q - 1)
                        act.activation(Pb[:, q % 2, k0:T], ps[:, 3 + q % 2, k0:T], ACT.Exp, scale=SCALE,
                                       bias=small[:, 2 + q % 2:3 + q % 2],
                                       accum_out=small[:, 4 + q % 2:5 + q % 2]).then_inc(sem("probs_exp"), 1)

                    exps(0)
                    for q in range(n_q):
                        if q + 1 < n_q:
                            exps(q + 1)
                        if ahead and q == 0:
                            copy_head(*ahead)
                        k0 = 0 if q < SEQ // P else SEQ
                        act.wait_ge(sem("probs_turned"), qbase + q + 1)
                        act.copy(PT[:, q % 2, k0:T], ps[:, 5 + q % 2, k0:T]).then_inc(sem("probs_copied"), 1)

                copy_head(0, 0)
                head_rounds(act, attend)
                handover("act", act, act.copy(dummy[:, 1:2], epst[:, 0:1]))

                for o in range(RT):
                    act.wait_ge(sem("rin_ready"), RT * l + o + 1)
                    act.wait_ge(sem("rin_padded"), l + 1)
                    if o >= 2:
                        act.wait_ge(sem("rin_mixed"), RT * l + o - 1)
                    act.copy(PP[:, o % 2, :, 1:SEQ + 1], ps[:, o % 8, :].rearrange("p (s n) -> p s n", s=2))\
                       .then_inc(sem("rin_copied"), 1)
                handover("act", act, act.copy(dummy[:, 1:2], epst[:, 0:1]))

                for j in range(RJ):
                    act.wait_ge(sem("key_sums"), RJ * l + j + 1)
                    rsqrt(B[1][:, j, :], ps[:, j, :], 1, 1).then_inc(sem("key_rstd"), 1)
                act.copy(DA[64:128, 1, :], WA[64:128, 0, :])
                act.activation(DA[0:64, 0, :], WA[0:64, 0, :], ACT.Tanh).then_inc(sem("decay_input"), 1)
                act.activation(GX[:, 0, :], GX[:, 0, :], ACT.Sigmoid)
                for u in range(2 * RJ):
                    j, d = u // 2, u % 2
                    for half, (out_, v) in enumerate(((LW[d][:, j, :], "w0"), (TS[:, u % 2, :], "a0"))):
                        act.wait_ge(sem("lora_up"), 16 * l + 2 * u + half + 1)
                        if half and u >= 2:
                            act.wait_ge(sem("rates_used"), 8 * l + u - 1)
                        col = VEC[v] + d * RJ + j
                        act.activation(out_, ps[:, 4 + (2 * u + half) % 4, :], ACT.Sigmoid, bias=vecs[:, l, col:col + 1])\
                           .then_inc(sem("lora_gates"), 1)
                act.preload_act_table_set("natural_log_exp_and_others")
                handover("act", act, act.copy(dummy[:, 1:2], epst[:, 0:1]))

                flat = lambda name, d: SB[name][d].rearrange("p j n -> p (j n)")
                turned = lambda d: ps[:, 4 * d + 3, :]

                def log_decays(at):
                    for d in range(2):
                        act.copy(SB["lw"][d], LW[d][:, :, bass.ds(at[d], CH)]).then_inc(sem(f"decays{d}"), 1)

                def decays(step):
                    for d in range(2):
                        act.wait_ge(sem(f"cumulated{d}"), step + 1)
                        act.activation(flat("E1", d), flat("L", d), ACT.Exp, scale=-DECAY).then_inc(sem(f"exps{d}"), 1)

                def decays_before(step):
                    for d in range(2):
                        act.wait_ge(sem(f"before{d}"), step + 1)
                        act.activation(flat("E3", d), flat("E3", d), ACT.Exp, scale=-DECAY).then_inc(sem(f"exps{d}"), 1)

                def growths(step):
                    for d in range(2):
                        wait_apart(act, f"step{d}", step + 1)
                        act.activation(flat("E2", d), flat("L", d), ACT.Exp, scale=DECAY).then_inc(sem(f"exps{d}"), 1)

                def scan_step(s, c, step, at, ahead):
                    for n, name in enumerate(("Bt", "Kt", "Vt")):
                        for d in range(2):
                            act.wait_ge(sem(f"grams{d}"), 3 * step + n + 1)
                            act.copy(flat(name, d), turned(d)).then_inc(sem(f"turned{d}"), 1)
                    for n in range(len(LEVELS)):
                        for d in range(2):
                            act.wait_ge(sem(f"joined{d}"), step * len(LEVELS) + n + 1)
                            act.copy(flat("P", d), turned(d)).then_inc(sem(f"joined_copied{d}"), 1)
                        if ahead and n == 0:
                            log_decays(ahead)
                        if ahead and n == 2:
                            decays(step + 1)
                        if ahead and n == 3:
                            decays_before(step + 1)
                    for d in range(2):
                        act.wait_ge(sem(f"rhs{d}"), step + 1)
                        act.copy(flat("RHS", d), turned(d)).then_inc(sem(f"rhs_copied{d}"), 1)
                    for d in range(2):
                        act.wait_ge(sem(f"u{d}"), step + 1)
                        act.copy(flat("U", d), turned(d)).then_inc(sem(f"u_copied{d}"), 1)
                    if ahead:
                        growths(step + 1)

                first = 2 * l * NCH
                log_decays(first_columns())
                decays(first)
                decays_before(first)
                growths(first)
                scan_steps(act, l, scan_step)
                handover("act", act, act.copy(dummy[:, 1:2], epst[:, 0:1]))

                for j in range(RJ):
                    act.wait_ge(sem("head_vars"), RJ * l + j + 1)
                    rsqrt(B[0][:, j, :], ps[:, 4 * (j % 2) + 3, :], RN, 2).then_inc(sem("head_rstd"), 1)
                handover("act", act, act.copy(dummy[:, 1:2], epst[:, 0:1]))

                act.preload_act_table_set("sigmoid_and_others")
                for o in range(24 * l, 24 * l + 24):
                    act.wait_ge(sem("merge_gate"), o + 1)
                    if o - 24 * l >= 2:
                        act.wait_ge(sem("merged"), o - 1)
                    act.activation(SG[:, o % 2, 0:w], ps[:, 2 * (o % 4), 0:w], ACT.Sigmoid).then_inc(sem("merge_sigmoid"), 1)
                act.preload_act_table_set("natural_log_exp_and_others")
                handover("act", act, act.copy(dummy[:, 1:2], epst[:, 0:1]))
                handover("act", act, act.copy(dummy[:, 1:2], epst[:, 0:1]))
                norm(w, l, 1)

                nt = w // P
                act.wait_ge(sem("router_ready"), l + 1)
                act.activation(rt[0][:, 0:nt * NE], ps[:, 7, 0:nt * NE], ACT.Sigmoid).then_inc(sem("router_scores"), 1)
                for t in range(nt):
                    at = sum(nqt[:l]) + t
                    act.wait_ge(sem("tokens_turned"), at + 1)
                    for half in range(2):
                        act.copy(MT_[:, t, 512 * half:512 * half + 512], ps[:, 2 * (t % 2) + half, :])\
                           .then_inc(sem("tokens_copied"), 1)
                act.preload_act_table_set("silu_and_others")
                for j in range(FK):
                    act.wait_ge(sem("gate_ready"), FK * l + j + 1)
                    act.activation(HS[:, j, 0:w], ps[:, 2 * (j % 2), 0:w], ACT.Silu).then_inc(sem("gate_silu"), 1)

                def copy_rows(b, count):
                    act.wait_ge(sem(f"rows_turned{b}"), count)
                    act.copy(XGT[:, 0:4, :], ps[:, 0, :].rearrange("p (k n) -> p k n", n=P)).then_inc(sem("rows_copied"), 1)

                act.wait_ge(sem("route_ready"), l + 1)
                pairs = pair_count(act, l)
                copy_rows(0, pairs_before + l + 2)
                with act.Fori(0, pairs) as i:
                    it = pairs_before + i
                    for b in range(2):
                        jt = 2 * it + b
                        act.wait_ge(sem("tile_gate"), jt + 1)
                        act.activation(SIL[:, 0, :], ps[:, 2, :], ACT.Silu).then_inc(sem("tile_silu"), 1)
                        copy_rows(1 - b, it + 2 + b + (l if b else 0))
                        act.wait_ge(sem("hidden_turned"), jt + 1)
                        act.copy(HIDT[:, 0, :], ps[:, 4, :]).then_inc(sem("hidden_copied"), 1)
                        act.wait_ge(sem("tile_half"), jt + 1)
                        act.wait_ge(sem("result_free"), jt + 1)
                        act.copy(YG[:, b, 0:512], ps[:, 5, :]).then_inc(sem("result_copied"), 1)
                act.preload_act_table_set("natural_log_exp_and_others")
                handover("act", act, act.copy(dummy[:, 1:2], epst[:, 0:1]))
                pairs_before = pairs_before + pairs
            norm(SEQ)

        @block.vector
        def _(dve):
            link = Chain(dve, "dve_order")
            tt, stt, ts = dve.tensor_tensor, dve.scalar_tensor_tensor, dve.tensor_scalar

            def over():
                handover("dve", dve, dve.memset(dummy[:, 0:1], 0.0))

            norms = 0

            def odd_squares(w):
                for k in range(1, KD, 2):
                    tt(H[:, k, 0:w], X[:, k, 0:w], X[:, k, 0:w], ALU.mult).then_inc(sem("squares1"), 1)

            def norm(w, l, n):
                nonlocal norms
                norms += 1
                odd_squares(w)
                dve.wait_ge(sem("rstd"), norms)
                for k in range(KD):
                    tt(H[:, k, 0:w], X[:, k, 0:w], RS[:, 0, 0:w], ALU.mult).then_inc(sem("normed"), 1)
                over()

            dve.wait_ge(sem("params"), 16 * 7)
            pairs_before = 0
            for l in range(DEPTH):
                w = width[l]

                def vec_(name, j=0, n=1):
                    return vecs[:, l, VEC[name] + j:VEC[name] + j + n]

                link(dve.memset(CP, 0.0))
                dve.wait_ge(sem("csil"), 1)
                dve.tensor_copy(CP[:, :, 0:2], csil[:]).then_inc(sem("csil"), 1)
                with dve.Fori(0, N_ADA // NSLOT) as i:
                    at = N_ADA * l + i * NSLOT

                    def row(s):
                        dve.wait_ge(sem("ada_rows"), at + s + 1)
                        dve.tensor_copy(ROW[:, s, :], ps[:, s, :]).then_inc(sem("ada_copied"), 1)

                    def cols(s):
                        dve.wait_ge(sem("ada_cols"), at + s + 1)
                        c = (i * NSLOT + s) * 4
                        tt(mod[:, bass.ds(c, 4), :], ps[:, 3 + s, 0:8].rearrange("p (c q) -> p c q", q=2),
                           vecs[:, l, bass.ds(VEC["bada"] + c, 4)].unsqueeze(2).broadcast_to([P, 4, 2]), ALU.add)\
                            .then_inc(sem("ada_mod"), 1)
                    row(0)
                    row(1)
                    cols(0)
                    row(2)
                    cols(1)
                    cols(2)
                dve.wait_ge(sem("ada_mod"), N_ADA * (l + 1) + 1)
                for n, name in enumerate(("n1", "n2")):
                    for s in range(2):
                        stt(gsc[:, n, :, s], mod[:, 24 * n + 8:24 * n + 16, s], 1.0, vec_(name, 0, KD), ALU.add, ALU.mult)
                over()
                norm(T, l, 0)
                over()

                base = sum(four[:l])
                for u in range(four[l]):
                    dve.wait_ge(sem("fourier_first"), base + u + 1)
                    if u >= 2:
                        dve.wait_ge(sem("fourier_ready"), base + u - 1)
                    dve.tensor_copy(FA[:, u % 2, :], ps[:, u % 2, :]).then_inc(sem("fourier_mid"), 1)
                over()

                rr = slice(NOPE, QK)
                cos, sin = (cons[rr, CON[x]:CON[x] + SEQ] for x in ("cos", "sin"))
                dve.wait_ge(sem("key_turned"), l + 1)
                link(tt(RP[rr, 0, 0:SEQ], ps[rr, 2, 0:SEQ], sin, ALU.mult))
                link(tt(KR[rr, 0, 0:SEQ], KR[rr, 0, 0:SEQ], cos, ALU.mult))
                link(tt(KR[rr, 0, 0:SEQ], KR[rr, 0, 0:SEQ], RP[rr, 0, 0:SEQ], ALU.add))
                for b in range(2):
                    dve.tensor_copy(Kh[rr, b, :], KR[rr, 0, :])
                dve.wait_ge(sem("lora_rstd"), 2 * l + 1)
                for k in range(3):
                    stt(CQ[:, k, 0:w], CQ[:, k, 0:w], vec_("qg", k), RQ[:, 0, 0:w], ALU.mult, ALU.mult)
                dve.wait_ge(sem("lora_rstd"), 2 * l + 2)
                for k in range(2):
                    ins = stt(CKV[:, k, :], CKV[:, k, :], vec_("kvg", k), RQ[:, 1, :], ALU.mult, ALU.mult)
                ins.then_inc(sem("lora_normed"), 1)
                over()

                n_q = nqt[l]
                def prepare(i, b):
                    h = l * HEADS + 2 * i + b
                    dve.tensor_copy(Vh[:, b, :].rearrange("p (c n) -> p c n", n=VD),
                                    VT[:, :, bass.ds((2 * i + b) * VD, VD)])
                    dve.wait_ge(sem("query_turned"), h + 1)
                    link(tt(RP[rr, 0, 0:SEQ], ps[rr, 2, 0:SEQ], sin, ALU.mult))
                    link(tt(Qh[rr, b, 0:SEQ], Qh[rr, b, 0:SEQ], cos, ALU.mult))
                    tt(Qh[rr, b, 0:SEQ], Qh[rr, b, 0:SEQ], RP[rr, 0, 0:SEQ], ALU.add).then_inc(sem("query_done"), 1)

                def attend(i, b, ahead):
                    h = l * HEADS + 2 * i + b
                    qbase = HEADS * sum(nqt[:l]) + (2 * i + b) * n_q

                    def largest(q):
                        k0 = 0 if q < SEQ // P else SEQ
                        dve.wait_ge(sem("scores_ready"), qbase + q + 1)
                        link(dve.tensor_reduce(small[:, q % 2:q % 2 + 1], ps[:, 3 + q % 2, k0:T], AX_X, ALU.max))
                        ts(small[:, 2 + q % 2:3 + q % 2], small[:, q % 2:q % 2 + 1], -SCALE, None, ALU.mult)\
                            .then_inc(sem("probs_max"), 1)

                    largest(0)
                    for q in range(n_q):
                        if q + 1 < n_q:
                            largest(q + 1)
                        k0 = 0 if q < SEQ // P else SEQ
                        dve.wait_ge(sem("probs_exp"), qbase + q + 1)
                        link(dve.reciprocal(small[:, 6 + q % 2:7 + q % 2], small[:, 4 + q % 2:5 + q % 2]))
                        ts(Pb[:, q % 2, k0:T], Pb[:, q % 2, k0:T], small[:, 6 + q % 2:7 + q % 2], None, ALU.mult)\
                            .then_inc(sem("probs_ready"), 1)
                        if ahead and q == 1:
                            prepare(*ahead)
                    dve.wait_ge(sem("attention_ready"), h + 1)
                    half = slice(b * VD, b * VD + VD)
                    dve.tensor_copy(work[half, bass.ds(2048 + i * T, w)], ps[half, 7, 0:w])\
                       .then_inc(sem("heads_out"), 1)

                prepare(0, 0)
                head_rounds(dve, attend, lambda i: link.loop(i, 2 * (2 + 2 * n_q)), lambda: link.end(HEADS // 2 - 1))
                over()

                for o in range(RT):
                    dst = [R, K1, V][o // 4][:, o % 4, :] if o < 12 else (WA, GX)[o - 12][:, 0, :]
                    p = PP[:, o % 2, :, 1:SEQ + 1]
                    t = TS[:, 0, :].rearrange("p (s n) -> p s n", s=2)
                    dve.wait_ge(sem("rin_copied"), RT * l + o + 1)
                    link(tt(t, PP[:, o % 2, :, 0:SEQ], PP[:, o % 2, :, 2:SEQ + 2], ALU.add))
                    link(stt(t, t, 0.5, p, ALU.mult, ALU.subtract))
                    stt(dst.rearrange("p (s n) -> p s n", s=2), t, vec_("mu", o), p, ALU.mult, ALU.add)\
                        .then_inc(sem("rin_mixed"), 1)
                    dve.wait_ge(sem("rin_mixed"), RT * l + o + 1)
                over()

                dve.memset(DA[0:64, 1, :], 0.0)
                dve.memset(DA[64:128, 0, :], 0.0).then_inc(sem("decay_input"), 1)
                for j in range(RJ):
                    link(ts(KK[:, j, :], K1[:, j, :], vec_("kk", j), None, ALU.mult))
                    tt(B[0][:, j, :], KK[:, j, :], KK[:, j, :], ALU.mult).then_inc(sem("key_squares"), 1)
                for j in range(RJ):
                    dve.wait_ge(sem("key_rstd"), RJ * l + j + 1)
                    link(tt(KK[:, j, :], KK[:, j, :], B[1][:, j, :], ALU.mult))
                for u in range(2 * RJ):
                    j, d = u // 2, u % 2
                    rate = TS[:, u % 2, :]
                    dve.wait_ge(sem("lora_gates"), 16 * l + 2 * u + 2)
                    link(tt(B[d][:, j, :], KK[:, j, :], rate, ALU.mult))
                    link(ts(rate, rate, -1.0, vec_("ka", j), ALU.add, ALU.mult))
                    stt(KDs[d][:, j, :], rate, 1.0, K1[:, j, :], ALU.add, ALU.mult).then_inc(sem("rates_used"), 1)
                over()

                flat = lambda name, d: SB[name][d].rearrange("p j n -> p (j n)")
                bank = lambda d, n: ps[:, 4 * d + n, :].rearrange("p (j n) -> p j n", n=P)
                half = lambda d, n, x: ps[:, 4 * d + n, 256 * x:256 * x + 256].rearrange("p (j n) -> p j n", n=CH)
                b_ = lambda name, d: SB[name][d]

                def cumulate(step):
                    for d in range(2):
                        dve.wait_ge(sem(f"decays{d}"), step + 1)
                        if d == 0:
                            dve.tensor_tensor_scan(flat("L", 0), con_("reset", RJ * CH), flat("lw", 0), 0.0,
                                                   ALU.mult, ALU.add).then_inc(sem("cumulated0"), 1)
                        else:
                            link(dve.tensor_tensor_scan(flat("E1", 1), con_("reset", RJ * CH), flat("lw", 1), 0.0,
                                                        ALU.mult, ALU.add))
                            link(tt(b_("E3", 1), b_("lw", 1), b_("E1", 1), ALU.subtract))
                            tt(b_("L", 1), b_("E3", 1), b_("E1", 1)[:, :, CH - 1:CH].broadcast_to([P, RJ, CH]), ALU.add)\
                                .then_inc(sem("cumulated1"), 1)

                def decayed_keys(step, at):
                    for d in range(2):
                        wait_apart(dve, f"exps{d}", 3 * step + 2)
                        link(tt(b_("E3", d), KK[:, :, bass.ds(at[d], CH)], b_("E3", d), ALU.mult))

                def operands(step, at, d):
                    cols = bass.ds(at[d], CH)
                    wait_apart(dve, f"exps{d}", 3 * step + 3)
                    for h in range(2):
                        hh = slice(64 * h, 64 * h + 64)
                        tt(blocks(b_("bKk", d))[hh, :, h, :], KDs[d][hh, :, cols], b_("E2", d)[hh], ALU.mult)
                        tt(blocks(b_("bE2", d))[hh, :, h, :], B[d][hh, :, cols], b_("E2", d)[hh], ALU.mult)
                    end = CH - 1 if d == 0 else 0
                    dve.tensor_copy(total[:, d, :].unsqueeze(2), b_("E1", d)[:, :, end:end + 1])
                    tt(blocks(b_("bE3", d)), both_heads(b_("E3", d)), blocks_mask("same"), ALU.mult)\
                        .then_inc(sem(f"scaled{d}"), 1)

                def scan_step(s, c, step, at, ahead):
                    stream = s == 1 or l < DEPTH - 1
                    if not isinstance(c, int):
                        link.loop(c, 2 * (2 + len(LEVELS) - 1 + 1 + stream) + 2 + 2)
                    for d in range(2):
                        dve.wait_ge(sem(f"grams{d}"), 3 * step + 1)
                        tt(b_("MT", d), half(d, 0, 0), over_pairs(con_(f"minus{d}")), ALU.mult).then_inc(sem(f"coupling{d}"), 1)
                        link(tt(b_("X", d), bank(d, 2), over_pairs(con_(f"pair{d}", P)), ALU.mult))
                        dve.wait_ge(sem(f"coupling{d}"), step + 1)
                        link(tt(blocks(b_("XT", d)), both_heads(b_("MT", d)), blocks_mask("lev1"), ALU.mult))
                        tt(b_("X", d), b_("X", d), over_pairs(ident), ALU.add)
                        tt(b_("XT", d), b_("XT", d), over_pairs(ident), ALU.add).then_inc(sem(f"inverse{d}"), 1)
                    for d in range(2):
                        dve.wait_ge(sem(f"grams{d}"), 3 * step + 2)
                        tt(blocks(b_("Gak", d)), both_heads(half(d, 1, 0)), blocks_mask(f"before{d}"), ALU.mult)
                        tt(b_("Grb", d), half(d, 0, 1), over_pairs(con_(f"incl{d}")), ALU.mult)
                        tt(b_("Grk", d), half(d, 1, 1), over_pairs(con_(f"incl{d}")), ALU.mult).then_inc(sem(f"masked{d}"), 1)
                    for n in range(len(LEVELS)):
                        for d in range(2):
                            dve.wait_ge(sem(f"grown{d}"), step * len(LEVELS) + n + 1)
                            if n < len(LEVELS) - 1:
                                link(tt(b_("X", d), b_("X", d), bank(d, 2), ALU.add))
                            tt(b_("XT", d), b_("XT", d), bank(d, 1), ALU.add).then_inc(sem(f"inverse{d}"), 1)
                        if ahead and n == 1:
                            cumulate(step + 1)
                        if ahead and n == 3:
                            decayed_keys(step + 1, ahead)
                    for d in range(2):
                        cols = bass.ds(at[d], CH)
                        wait_apart(dve, f"step{d}", step + 2)
                        if stream:
                            link(tt(Y[:, :, cols], Y[:, :, cols], half(d, 0, 0), ALU.add))
                        link(tt(b_("S", d), b_("S", d), bank(d, 2), ALU.add))
                        tt(b_("S", d), b_("S", d), total[:, d, :].unsqueeze(2).broadcast_to([P, RJ, P]), ALU.mult)\
                            .then_inc(sem(f"state{d}"), 1)
                        dve.wait_ge(sem(f"state{d}"), step + l + 2)
                        if ahead:
                            operands(step + 1, ahead, d)
                    if not isinstance(c, int):
                        link.end(NCH - 1)

                first = 2 * l * NCH
                cumulate(first)
                decayed_keys(first, first_columns())
                for d in range(2):
                    operands(first, first_columns(), d)
                scan_steps(dve, l, scan_step)
                over()

                def bonus(j):
                    link(tt(B[0][:, j, :], KDs[0][:, j, :], KDs[1][:, j, :], ALU.add))
                    stt(TS[:, 0, :], R[:, j, :], vec_("rk", j), B[0][:, j, :], ALU.mult, ALU.mult)\
                        .then_inc(sem("bonus_input"), 1)

                bonus(0)
                for j in range(RJ):
                    bank = 4 * (j % 2)
                    dve.wait_ge(sem("head_sums"), RJ * l + j + 1)
                    y = KK[:, j, :]
                    link(stt(y, ps[:, bank + 1, :], -1.0 / RN, Y[:, j, :], ALU.mult, ALU.add))
                    tt(TS[:, 1, :], y, y, ALU.mult).then_inc(sem("centred_squares"), 1)
                    if j + 1 < RJ:
                        bonus(j + 1)
                    link(tt(B[1][:, j, :], ps[:, bank, :], V[:, j, :], ALU.mult))
                    dve.wait_ge(sem("head_rstd"), RJ * l + j + 1)
                    link(tt(y, y, B[0][:, j, :], ALU.mult))
                    link(ts(y, y, vec_("gng", j), vec_("gnb", j), ALU.mult, ALU.add))
                    link(tt(y, y, B[1][:, j, :], ALU.add))
                    link(tt(Y[:, j, :], y, ps[:, bank + 2, :], ALU.mult))
                over()

                o = 24 * l
                for g in range(2):
                    for b in range(3):
                        for j in range(4):
                            dve.wait_ge(sem("merge_sigmoid"), o + 1)
                            dve.wait_ge(sem("merge_proj"), o + 1)
                            m = M[:, 4 * g + j, 0:w]
                            gate, proj = SG[:, o % 2, 0:w], ps[:, 2 * (o % 4) + 1, 0:w]
                            if b == 0:
                                tt(m, gate, proj, ALU.mult).then_inc(sem("merged"), 1)
                            else:
                                link(tt(TM[:, 0, 0:w], gate, proj, ALU.mult))
                                tt(m, m, TM[:, 0, 0:w], ALU.add).then_inc(sem("merged"), 1)
                                dve.wait_ge(sem("merged"), o + 1)
                            o += 1
                over()
                for j in range(KD):
                    dve.wait_ge(sem("out_ready"), KD * l + j + 1)
                    for s in range(w // SEQ):
                        x = X[:, j, s * SEQ:s * SEQ + SEQ]
                        stt(x, ps[:, j, s * SEQ:s * SEQ + SEQ], mod[:, 16 + j, s:s + 1], x, ALU.mult, ALU.add)
                over()
                norm(w, l, 1)

                nt = w // P
                v3 = lambda x, n, q: x[:, 0:n * q].rearrange("p (n q) -> p n q", q=q)
                wide = lambda x, n, q: x[:, 0:n].unsqueeze(2).broadcast_to([P, n, q])
                prio = cons[:, CON["prio"]:CON["prio"] + NE]
                ng = nt * NG
                dve.wait_ge(sem("router_scores"), l + 1)
                sel = v3(rt[1], nt, NE)
                link(tt(sel, v3(rt[0], nt, NE), rbs[:, :].unsqueeze(1).broadcast_to([P, nt, NE]), ALU.add))
                x4, pr = v3(rt[1], ng, EPG), v3(rt[2], ng, 6)
                tt(pr[:, :, 0:3], x4[:, :, 0:3], x4[:, :, 1:4], ALU.add)
                tt(pr[:, :, 3:5], x4[:, :, 0:2], x4[:, :, 2:4], ALU.add)
                link(tt(pr[:, :, 5:6], x4[:, :, 0:1], x4[:, :, 3:4], ALU.add))
                link(dve.tensor_reduce(rt[3][:, 0:ng], pr, AX_X, ALU.max))

                def first_largest(out_, x, n, q, pri):
                    link(dve.tensor_reduce(rt[4][:, 0:n], v3(x, n, q), AX_X, ALU.max))
                    link(tt(v3(rt[5], n, q), v3(x, n, q), wide(rt[4], n, q), ALU.is_equal))
                    link(tt(v3(rt[5], n, q), v3(rt[5], n, q), pri.unsqueeze(1).broadcast_to([P, n, q]), ALU.mult))
                    link(dve.tensor_reduce(rt[4][:, 0:n], v3(rt[5], n, q), AX_X, ALU.max))
                    link(tt(v3(out_, n, q), v3(rt[5], n, q), wide(rt[4], n, q), ALU.is_equal))

                first_largest(rt[6], rt[3], nt, NG, prio[:, 0:NG])
                link(ts(rt[7][:, 0:ng], rt[6][:, 0:ng], 1e30, -1e30, ALU.mult, ALU.add))
                link(tt(x4, x4, wide(rt[6], ng, EPG), ALU.mult))
                link(tt(x4, x4, wide(rt[7], ng, EPG), ALU.add))
                first_largest(rt[6], rt[1], nt, NE, prio)
                link(stt(rt[1][:, 0:nt * NE], rt[6][:, 0:nt * NE], -1e35, rt[1][:, 0:nt * NE], ALU.mult, ALU.add))
                first_largest(rt[7], rt[1], nt, NE, prio)
                n16 = nt * NE
                link(tt(rt[2][:, 0:n16], rt[6][:, 0:n16], rt[7][:, 0:n16], ALU.add))
                tt(rt[8][:, 0:n16], rt[2][:, 0:n16], rt[0][:, 0:n16], ALU.mult).then_inc(sem("chosen"), 1)
                dve.wait_ge(sem("chosen"), l + 1)
                link(dve.tensor_reduce(rt[4][:, 0:nt], v3(rt[8], nt, NE), AX_X, ALU.add))
                link(dve.reciprocal(rt[3][:, 0:nt], rt[4][:, 0:nt]))
                link(tt(v3(rt[9], nt, NE), v3(rt[8], nt, NE), wide(rt[3], nt, NE), ALU.mult))
                choice = small16[4:6]
                for c in range(2):
                    link(tt(rt[5][:, 0:n16], rt[6 + c][:, 0:n16], rt[9][:, 0:n16], ALU.mult))
                    link(dve.tensor_reduce(choice[c][:, 0:nt], v3(rt[5], nt, NE), AX_X, ALU.add))

                for j in range(FK):
                    dve.wait_ge(sem("gate_silu"), FK * l + j + 1)
                    dve.wait_ge(sem("up_ready"), FK * l + j + 1)
                    tt(HS[:, j, 0:w], HS[:, j, 0:w], ps[:, 2 * (j % 2) + 1, 0:w], ALU.mult).then_inc(sem("hidden_ready"), 1)

                dve.wait_ge(sem("ranked"), l + 1)
                count, tiles, upto, base = small16[0:4]
                link(dve.tensor_copy(count, ps[:, 7, 128:128 + NE]))
                link(ts(tiles, count, 0.0, None, ALU.is_gt))
                for q in range(1, T // P):
                    link(stt(tiles, count, float(q * P), tiles, ALU.is_gt, ALU.add))
                link(dve.tensor_tensor_scan(upto, ones[:, 0:NE], tiles, 0.0, ALU.mult, ALU.add))
                link(tt(base, upto, tiles, ALU.subtract))
                link(ts(base, base, float(P), None, ALU.mult))
                link(tt(v3(rt[3], nt, NE), ps[:, 7, 0:n16].rearrange("p (n q) -> p n q", q=NE),
                        base.unsqueeze(1).broadcast_to([P, nt, NE]), ALU.add))
                for c in range(2):
                    link(tt(rt[5][:, 0:n16], rt[6 + c][:, 0:n16], rt[3][:, 0:n16], ALU.mult))
                    link(dve.tensor_reduce(small16[6 + c][:, 0:nt], v3(rt[5], nt, NE), AX_X, ALU.add))
                    dve.tensor_copy(pos[:, c * nt:c * nt + nt], small16[6 + c][:, 0:nt]).then_inc(sem("placed"), 1)
                tab = TAB.rearrange("p (n e) -> p n e", e=NE)
                link(tt(tab, upto.unsqueeze(1).broadcast_to([P, NTAB, NE]),
                        cons[:, CON["iota"]:CON["iota"] + NTAB].unsqueeze(2).broadcast_to([P, NTAB, NE]), ALU.is_le))
                link(dve.tensor_reduce(rt[4][:, 0:NTAB], tab, AX_X, ALU.add))
                link(ts(rt[4][:, 0:NTAB], rt[4][:, 0:NTAB], float(NE - 1), None, ALU.min))
                link(dve.tensor_copy(tile_expert[:, :], rt[4][:, 0:NTAB]))
                link(tt(rt[5][:, 0:NTAB // 2], cons[:, CON["iota"]:CON["iota"] + NTAB].rearrange("p (n b) -> p n b", b=2)[:, :, 0],
                        upto[:, NE - 1:NE].broadcast_to([P, NTAB // 2]), ALU.is_lt))
                link(dve.tensor_reduce(rt[5][:, 64:65], rt[5][:, 0:NTAB // 2], AX_X, ALU.add))
                dve.tensor_copy(tile_pairs[:, l:l + 1], rt[5][:, 64:65]).then_inc(sem("route_ready"), 1)
                dve.wait_ge(sem("route_ready"), l + 1)

                for j in range(KD):
                    dve.wait_ge(sem("down_ready"), KD * l + j + 1)
                    for s in range(nt // 2):
                        x = X[:, j, s * SEQ:s * SEQ + SEQ]
                        ins = stt(x, ps[:, 4 + j % 3, s * SEQ:s * SEQ + SEQ], mod[:, 40 + j, s:s + 1], x, ALU.mult, ALU.add)
                    ins.then_inc(sem("down_added"), 1)
                dve.wait_ge(sem("down_added"), KD * (l + 1))

                def copy_rows(b, count):
                    dve.wait_ge(sem(f"rows_turned{b}"), count)
                    dve.tensor_copy(XGT[:, 4:8, :], ps[:, 1, :].rearrange("p (k n) -> p k n", n=P))\
                       .then_inc(sem("rows_copied"), 1)

                pairs = pair_count(dve, l)
                copy_rows(0, pairs_before + l + 2)
                with dve.Fori(0, pairs) as i:
                    it = pairs_before + i
                    for b in range(2):
                        jt = 2 * it + b
                        dve.wait_ge(sem("tile_silu"), jt + 1)
                        dve.wait_ge(sem(f"tile_up{b}"), it + 2)
                        tt(HID[:, 0, :], SIL[:, 0, :], ps[:, 3, :], ALU.mult).then_inc(sem("tile_hidden"), 1)
                        copy_rows(1 - b, it + 2 + b + (l if b else 0))
                        dve.wait_ge(sem(f"tile_down{b}"), it + 2)
                        dve.wait_ge(sem("result_free"), jt + 1)
                        dve.tensor_copy(YG[:, b, 512:1024], ps[:, 6, :]).then_inc(sem("result_copied"), 1)

                for t in range(nt):
                    at = sum(nqt[:l]) + t
                    dve.wait_ge(sem(f"choices_loaded{t % 2}"), 32 * (at // 2 + 1))
                    y1, y2 = YT[:, 2 * (t % 2), :], YT[:, 2 * (t % 2) + 1, :]
                    link(ts(y1, y1, choice[0][:, t:t + 1], None, ALU.mult))
                    stt(y1, y2, choice[1][:, t:t + 1], y1, ALU.mult, ALU.add).then_inc(sem("choices_summed"), 1)
                    dve.wait_ge(sem("choices_turned"), at + 1)
                    for k in range(KD):
                        x = X[:, k, t * P:t * P + P]
                        stt(x, ps[:, 2 * (t % 4) + k // 4, (k % 4) * P:(k % 4) * P + P], mod[:, 40 + k, t // 2:t // 2 + 1],
                            x, ALU.mult, ALU.add)
                over()
                pairs_before = pairs_before + pairs
            odd_squares(SEQ)
            dve.wait_ge(sem("rstd"), 2 * DEPTH + 1)
            for k in range(KD):
                ins = stt(H[:, k, 0:SEQ], X[:, k, 0:SEQ], fngs[:, k:k + 1], RS[:, 0, 0:SEQ], ALU.mult, ALU.mult)
            ins.then_inc(sem("result"), 1)
            over()

        @block.gpsimd
        def _(pool):
            tt = pool.tensor_tensor
            over = lambda: handover("pool", pool, pool.memset(dummy[:, 2:3], 0.0))
            for n, eps in enumerate((EPS, 1e-12, GN_EPS)):
                pool.memset(epst[:, n:n + 1], eps).then_inc(sem("constants_set"), 1)
            pool.memset(zeros, 0.0).then_inc(sem("constants_set"), 1)
            for n, (name, count) in enumerate((
                    ("ada_mod", 1), ("heads_out", 1), ("step0", 1), ("step1", 1), ("tile_up0", 1), ("tile_up1", 1),
                    ("rows_turned0", 1), ("rows_turned1", 1), ("tile_down0", 1), ("tile_down1", 1), ("result_copied", 2),
                    ("result_free", 2))):
                pool.memset(starts[:, n:n + 1], 0.0).then_inc(sem(name), count)
            pool.wait_ge(sem("params"), 16 * 7)
            pairs_before = 0
            for l in range(DEPTH):
                for stage in ("ada", "norm1", "ina", "fourier", "lora", "attn"):
                    over()
                for col in (0, SEQ + 1):
                    ins = pool.memset(PP[:, :, :, col:col + 1], 0.0)
                ins.then_inc(sem("rin_padded"), 1)
                over()
                pool.memset(Y[:, :, :], 0.0)
                for d in range(2):
                    for name in ("bE2", "bKk", "bV", "S"):
                        ins = pool.memset(SB[name][d], 0.0)
                    ins.then_inc(sem(f"state{d}"), 1)
                over()

                b_ = lambda name, d: SB[name][d]

                def decays_before(step):
                    for d in range(2):
                        pool.wait_ge(sem(f"cumulated{d}"), step + 1)
                        tt(b_("E3", d), b_("L", d), b_("lw", d), ALU.subtract).then_inc(sem(f"before{d}"), 1)

                def operands(step, at):
                    for d in range(2):
                        wait_apart(pool, f"step{d}", step + 1)
                        tt(blocks(b_("bV", d)), both_heads(V[:, :, bass.ds(at[d], CH)]), blocks_mask("heads"), ALU.mult)
                        wait_apart(pool, f"exps{d}", 3 * step + 1)
                        tt(b_("Rq", d), R[:, :, bass.ds(at[d], CH)], b_("E1", d), ALU.mult).then_inc(sem(f"scaled{d}"), 1)

                def scan_step(s, c, step, at, ahead):
                    for n, b in enumerate(LEVELS):
                        for d in range(2):
                            if n == 0:
                                pool.wait_ge(sem(f"coupling{d}"), step + 1)
                            else:
                                pool.wait_ge(sem(f"joined{d}"), step * len(LEVELS) + n)
                            tt(blocks(b_("BT", d)), both_heads(b_("MT", d)), blocks_mask(f"lev{b}"), ALU.mult)\
                                .then_inc(sem(f"blocks{d}"), 1)
                        if ahead and n == 3:
                            decays_before(step + 1)
                    if ahead:
                        operands(step + 1, ahead)

                first = 2 * l * NCH
                decays_before(first)
                for d in range(2):
                    pool.wait_ge(sem(f"state{d}"), first + l + 1)
                operands(first, first_columns())
                scan_steps(pool, l, scan_step)
                over()
                pool.memset(dummy[:, 3:4], 0.0).then_inc(sem("scan_over"), 1)
                over()
                pool.memset(dummy[:, 3:4], 0.0).then_inc(sem("post_over"), 1)
                for stage in ("merge", "out", "norm2"):
                    over()

                nt = nqt[l]
                pool.wait_ge(sem("rows_zeroed"), 16 * D // ZEROS)
                pool.wait_ge(sem("tokens_copied"), 2 * sum(nqt[:l + 1]))
                for c in range(2):
                    pool.wait_ge(sem("placed"), 2 * l + c + 1)
                    for t in range(nt):
                        pool.indirect_dma_start(xg, bass.IndirectOffsetOnAxis(pos[:, c * nt + t:c * nt + t + 1], 0),
                                                MT_[:, t, :], None).then_inc(sem("rows_placed"), 16)
                pool.wait_ge(sem("route_ready"), l + 1)
                pairs = pair_count(pool, l)
                with pool.Fori(0, pairs) as i:
                    it = pairs_before + i
                    for b in range(2):
                        pool.wait_ge(sem("result_copied"), 4 * it + 2 * b + 4)
                        pool.dma_start(xg[bass.ds((2 * i + b) * P, P), :], YG[:, b, :]).then_inc(sem("result_stored"), 16)
                        pool.wait_ge(sem("result_free"), 2 * it + b + 2)
                        wait_apart(pool, "result_stored", 32 * it + 16 * (b + 1))
                        pool.memset(starts[:, 15:16], 0.0).then_inc(sem("result_free"), 1)
                pool.wait_ge(sem("rows_placed"), 16 * sum(2 * n for n in nqt[:l + 1]))
                for t in range(nt):
                    at = sum(nqt[:l]) + t
                    if t >= 2:
                        pool.wait_ge(sem("choices_turned"), at - 1)
                    for c in range(2):
                        pool.indirect_dma_start(YT[:, 2 * (t % 2) + c, :], None, xg,
                                                bass.IndirectOffsetOnAxis(pos[:, c * nt + t:c * nt + t + 1], 0))\
                            .then_inc(sem(f"choices_loaded{t % 2}"), 16)
                over()
                pairs_before = pairs_before + pairs
            over()


def constants():
    con = np.zeros((P, NCON), np.float64)

    def put(name, a):
        con[0:a.shape[0], CON[name]:CON[name] + a.shape[1]] = a

    part = np.arange(P)
    put("ident", np.eye(P))
    put("ones", np.ones((P, P)))
    put("groups", part[:, None] % 32 == np.arange(2)[None])
    put("heads", (part[:, None] // RN == part[None] // RN) * 1.0)
    rot = np.zeros((QK, QK))
    half = ROPE // 4
    for axis in range(2):
        for n in range(half):
            first = NOPE + axis * 2 * half + n
            rot[first + half, first] = -1.0
            rot[first, first + half] = 1.0
    put("rot", rot)
    a, b = np.arange(P)[:, None] % CH, np.arange(CH)[None]
    put("minus0", -1.0 * (a < b))
    put("minus1", -1.0 * (a > b))
    put("incl0", a <= b)
    put("incl1", a >= b)
    a, b = part[:, None], part[None]
    same = a // CH == b // CH

    def level(n):
        return (a // (2 * n) == b // (2 * n)) & (a // n != b // n)
    put("before0", -1.0 * (same & (a < b)))
    put("before1", -1.0 * (same & (a > b)))
    put("pair0", (a > b) & level(1))
    put("pair1", (a < b) & level(1))
    put("same", -1.0 * same)
    put("lev1", level(1))
    for n in LEVELS:
        put(f"lev{n}", level(n))
    put("reset", np.tile((np.arange(RJ * CH) % CH != 0) * 1.0, (P, 1)))
    put("before", part[:, None] < part[None])
    put("iota", np.tile(np.arange(NTAB), (P, 1)))
    put("prio", np.tile(np.arange(NE, 0, -1.0), (P, 1)))
    t = np.arange(SEQ)
    inv = (10000.0 ** (-np.arange(half, dtype=np.float32) / np.float32(half))).astype(np.float32)
    ang = np.stack([t // GRID_W, t % GRID_W], -1).astype(np.float32)[..., None] * inv
    ang = np.repeat(ang[:, :, None, :], 2, 2).reshape(SEQ, ROPE).T.astype(np.float64)
    con[NOPE:QK, CON["cos"]:CON["cos"] + SEQ] = np.cos(ang)
    con[NOPE:QK, CON["sin"]:CON["sin"] + SEQ] = np.sin(ang)
    ch = 2 * np.pi * np.outer(np.arange(FGD), np.arange(FGD)) / FGD
    tk = 2 * np.pi * np.outer(t, t) / SEQ
    ct, st = (f(tk) * SEQ ** -0.5 for f in (np.cos, np.sin))
    dft = np.concatenate([f(ch) * FGD ** -0.5 for f in (np.cos, np.sin)] +
                         [x[n * P:n * P + P] for x in (ct, -st) for n in range(2)], 1)
    return con.astype(np.float32), dft.astype(np.float32)


def kernel(**inputs):
    from concourse import bacc
    from concourse.bass_utils import run_bass_kernel_spmd

    a = {k: np.asarray(v) for k, v in inputs.items()}
    L = DEPTH

    def cols(x):
        x = x.reshape(*x.shape[:-1], -1, P)
        return np.moveaxis(x, -1, 0)

    tok = np.concatenate([a["x"][0], a["ctx"][0]], 0)
    xT = cols(tok).transpose(0, 2, 1).reshape(P, KD * T)
    cT = cols(np.stack([a["c"][0], a["c_ctx"]])).transpose(0, 2, 1).reshape(P, KD * 2)
    parts = [a["norm1_g"], a["norm2_g"], a["b_ada"], a["q_norm_g"], a["kv_norm_g"], a["rwkv_mu"],
             a["rwkv_w0"].reshape(L, -1), a["rwkv_a0"].reshape(L, -1), a["rwkv_k_k"], a["rwkv_k_a"],
             a["rwkv_r_k"].reshape(L, -1), a["rwkv_gn_g"], a["rwkv_gn_b"]]
    vec = np.concatenate([cols(x) for x in parts], 2).reshape(P, L * NVEC)
    con, dft = constants()
    uq = a["w_uq"].reshape(L, 3, P, HEADS, QK).transpose(0, 3, 2, 1, 4).reshape(L, HEADS, P, 3 * QK)
    uk = a["w_ukv"].reshape(L, 2, P, HEADS, NOPE + VD)[..., :NOPE].transpose(0, 3, 2, 1, 4).reshape(L, HEADS, P, 2 * NOPE)
    up = np.concatenate([a["rwkv_w_up"], a["rwkv_a_up"]], 2).transpose(0, 2, 1, 3).reshape(L, P, 2 * RD)
    arrays = dict(
        xT=xT, cT=cT, vec=vec, fng=cols(a["final_norm_g"]), rb=np.tile(a["router_b"][None], (P, 1)),
        rw=a["router_w"].reshape(KD, P, NE).transpose(1, 0, 2).reshape(P, KD * NE),
        w_ada=a["w_ada"], w_in=a["w_in"], headw=np.concatenate([uq, uk], 3), w_ukv=a["w_ukv"],
        lora=np.concatenate([up, a["rwkv_g_up"]], 2), w_a=a["w_proj_a"], w_b=a["w_proj_b"], w_c=a["w_proj_c"],
        w_out=a["w_out"], eg=a["exp_w_gate"], eu=a["exp_w_up"], ed=a["exp_w_down"], sg=a["sh_w_gate"],
        su=a["sh_w_up"], sd=a["sh_w_down"], con=con, dft=dft)
    arrays = {f"in_{k}": np.ascontiguousarray(v) for k, v in arrays.items()}
    nc = bacc.Bacc("TRN2", target_bir_lowering=False, num_devices=1)
    args = {k[3:]: nc.dram_tensor(k, v.shape, mybir.dt.from_np(v.dtype), kind="ExternalInput").ap()
            for k, v in arrays.items()}
    out = nc.dram_tensor("out", (P, KD, SEQ), F32, kind="ExternalOutput").ap()
    build(nc, **args, out=out)
    r = run_bass_kernel_spmd(nc, [arrays], core_ids=[0])
    y = np.asarray(r.results[0]["out"]).reshape(P, KD, SEQ)
    return y.transpose(2, 1, 0).reshape(1, SEQ, D)
```
